# Optimizing a Trainium2 kernel written in Bass

```python
import jax, jax.numpy as jnp
from jax import lax
import numpy as np

D_MODEL = 1024
BATCH = 1
SEQ = 1024
DEPTH = 2

N_POOL_LAYERS = DEPTH // 2
N_ATTN_LAYERS = DEPTH - N_POOL_LAYERS

POOL_WINDOWS = (2, 4, 8, 16)
N_POOL_GROUPS = len(POOL_WINDOWS)
POOL_GROUP_WIDTH = D_MODEL // N_POOL_GROUPS

HEAD_DIM = 64
N_HEADS = D_MODEL // HEAD_DIM
Q_BLOCK = 128
ATTN_SCALE = HEAD_DIM ** -0.5
NEG_BIG = -1e30

N_GROUPS = 4
EXPERTS_PER_GROUP = 4
N_EXPERTS = N_GROUPS * EXPERTS_PER_GROUP
TOP_K = 2
D_EXPERT = D_MODEL // 4

EPS = 1e-6

kernel_name = "yoco_pool_fox_hmoe_trunk"

def rmsnorm(x, g):
    xf = x.astype(jnp.float32)
    inv = lax.rsqrt(jnp.mean(xf * xf, axis=-1, keepdims=True) + EPS)
    return (xf * inv * g.astype(jnp.float32)).astype(x.dtype)

def pool_mixer(xn, w_pool, scale):
    B, S, D = xn.shape
    xg = xn.astype(jnp.float32).reshape(B, S, N_POOL_GROUPS, POOL_GROUP_WIDTH)
    cs = jnp.cumsum(xg, axis=1)
    pos1 = jnp.arange(1, S + 1)
    outs = []
    for g, w in enumerate(POOL_WINDOWS):
        c = cs[:, :, g]
        lag = jnp.pad(c, ((0, 0), (w, 0), (0, 0)))[:, :S]
        cnt = jnp.minimum(pos1, w).astype(jnp.float32)[None, :, None]
        outs.append((c - lag) / cnt)
    pooled = jnp.stack(outs, axis=2)
    diff = (pooled - xg).astype(xn.dtype)
    y = jnp.einsum('bsgc,gcd->bsgd', diff, w_pool).reshape(B, S, D)
    return y * scale

def shared_kv(h, kv_norm, w_k, w_v, w_f, b_f):
    B, S, _ = h.shape
    hn = rmsnorm(h, kv_norm)
    k = (hn @ w_k).reshape(B, S, N_HEADS, HEAD_DIM).transpose(0, 2, 1, 3)
    v = (hn @ w_v).reshape(B, S, N_HEADS, HEAD_DIM).transpose(0, 2, 1, 3)
    log_f = jax.nn.log_sigmoid((hn @ w_f).astype(jnp.float32) + b_f.astype(jnp.float32))
    F = jnp.cumsum(log_f, axis=1).transpose(0, 2, 1)
    return k, v, F

def forgetting_attention(xn, w_q, w_o, k, v, F):
    B, S, _ = xn.shape
    n_blk = S // Q_BLOCK
    q = (xn @ w_q).reshape(B, S, N_HEADS, HEAD_DIM).transpose(0, 2, 1, 3)
    q_blocks = q.reshape(B, N_HEADS, n_blk, Q_BLOCK, HEAD_DIM).transpose(2, 0, 1, 3, 4)
    F_blocks = F.reshape(B, N_HEADS, n_blk, Q_BLOCK).transpose(2, 0, 1, 3)
    k_pos = jnp.arange(S)

    def one_block(args):
        i, qb, Fb = args
        s = jnp.einsum('bhqd,bhkd->bhqk', qb, k).astype(jnp.float32) * ATTN_SCALE
        s = s + Fb[..., None] - F[:, :, None, :]
        q_pos = i * Q_BLOCK + jnp.arange(Q_BLOCK)
        mask = k_pos[None, :] <= q_pos[:, None]
        s = jnp.where(mask, s, NEG_BIG)
        p = jax.nn.softmax(s, axis=-1).astype(v.dtype)
        return jnp.einsum('bhqk,bhkd->bhqd', p, v)

    o = lax.map(one_block, (jnp.arange(n_blk), q_blocks, F_blocks))
    o = o.transpose(1, 0, 3, 2, 4).reshape(B, S, N_HEADS * HEAD_DIM)
    return o @ w_o

def hierarchical_moe(xn, wg, bg, we, be, w_gate, w_up, w_down):
    B, S, D = xn.shape
    N = B * S
    t = xn.reshape(N, D)
    g_logits = (t @ wg).astype(jnp.float32) + bg.astype(jnp.float32)
    g_prob = jax.nn.softmax(g_logits, axis=-1)
    g_idx = jnp.argmax(g_logits, axis=-1)
    g_w = jnp.take_along_axis(g_prob, g_idx[:, None], axis=1)
    e_logits = ((t @ we).astype(jnp.float32) + be.astype(jnp.float32)).reshape(N, N_GROUPS, EXPERTS_PER_GROUP)
    e_sel = jnp.take_along_axis(e_logits, g_idx[:, None, None], axis=1)[:, 0]
    top_v, top_i = lax.top_k(e_sel, TOP_K)
    top_w = jax.nn.softmax(top_v, axis=-1) * g_w
    expert_id = g_idx[:, None] * EXPERTS_PER_GROUP + top_i
    gates = jnp.sum(jax.nn.one_hot(expert_id, N_EXPERTS, dtype=jnp.float32) * top_w[..., None], axis=1)
    hg = jnp.einsum('nd,edf->nef', t, w_gate)
    hu = jnp.einsum('nd,edf->nef', t, w_up)
    h = jax.nn.silu(hg) * hu * gates[:, :, None].astype(hu.dtype)
    y = h.reshape(N, N_EXPERTS * D_EXPERT) @ w_down.reshape(N_EXPERTS * D_EXPERT, D)
    return y.reshape(B, S, D)

def setup_inputs(seed: int = 0) -> dict:
    key = jax.random.key(seed)
    ks = jax.random.split(key, 21)
    f32 = jnp.float32
    D = D_MODEL
    HD_ALL = N_HEADS * HEAD_DIM
    GW = POOL_GROUP_WIDTH

    def nrm(k, shape, fan_in):
        return jax.random.normal(k, shape, f32) * fan_in ** -0.5

    def gain(k, shape):
        return 1.0 + 0.02 * jax.random.normal(k, shape, f32)

    return {
        "x": jax.random.normal(ks[0], (BATCH, SEQ, D), f32),
        "mix_norm": gain(ks[1], (DEPTH, D)),
        "ffn_norm": gain(ks[2], (DEPTH, D)),
        "pool_w": nrm(ks[3], (N_POOL_LAYERS, N_POOL_GROUPS, GW, GW), GW),
        "pool_scale": 0.5 + 0.05 * jax.random.normal(ks[4], (N_POOL_LAYERS, D), f32),
        "kv_norm": gain(ks[5], (D,)),
        "w_k": nrm(ks[6], (D, HD_ALL), D),
        "w_v": nrm(ks[7], (D, HD_ALL), D),
        "w_f": nrm(ks[8], (D, N_HEADS), D),
        "b_f": 2.0 + 0.5 * jax.random.normal(ks[9], (N_HEADS,), f32),
        "w_q": nrm(ks[10], (N_ATTN_LAYERS, D, HD_ALL), D),
        "w_o": nrm(ks[11], (N_ATTN_LAYERS, HD_ALL, D), HD_ALL),
        "router_g": nrm(ks[12], (DEPTH, D, N_GROUPS), D),
        "router_g_b": 0.01 * jax.random.normal(ks[13], (DEPTH, N_GROUPS), f32),
        "router_e": nrm(ks[14], (DEPTH, D, N_EXPERTS), D),
        "router_e_b": 0.01 * jax.random.normal(ks[15], (DEPTH, N_EXPERTS), f32),
        "w_gate": nrm(ks[16], (DEPTH, N_EXPERTS, D, D_EXPERT), D),
        "w_up": nrm(ks[17], (DEPTH, N_EXPERTS, D, D_EXPERT), D),
        "w_down": nrm(ks[18], (DEPTH, N_EXPERTS, D_EXPERT, D), D_EXPERT),
        "final_norm": gain(ks[19], (D,)),
    }

def reference(x, mix_norm, ffn_norm, pool_w, pool_scale, kv_norm, w_k, w_v, w_f, b_f,
              w_q, w_o, router_g, router_g_b, router_e, router_e_b,
              w_gate, w_up, w_down, final_norm):
    h = x
    k = v = F = None
    for layer in range(DEPTH):
        if layer == N_POOL_LAYERS:
            k, v, F = shared_kv(h, kv_norm, w_k, w_v, w_f, b_f)
        hn = rmsnorm(h, mix_norm[layer])
        if layer < N_POOL_LAYERS:
            h = h + pool_mixer(hn, pool_w[layer], pool_scale[layer])
        else:
            j = layer - N_POOL_LAYERS
            h = h + forgetting_attention(hn, w_q[j], w_o[j], k, v, F)
        hn = rmsnorm(h, ffn_norm[layer])
        h = h + hierarchical_moe(hn, router_g[layer], router_g_b[layer], router_e[layer],
                                 router_e_b[layer], w_gate[layer], w_up[layer], w_down[layer])
    return rmsnorm(h, final_norm)


_drawn_inputs = setup_inputs


def setup_inputs(seed=0):
    import zlib

    import numpy as np

    out = dict(_drawn_inputs(seed))
    spreads = {}
    factors = {'kv_norm': 3.462, 'router_g_b': 4.47, 'router_e_b': 3.584, 'final_norm': 2.836}
    for name, (base, spread) in spreads.items():
        noise = np.random.default_rng([zlib.crc32(name.encode()), seed]).standard_normal(out[name].shape)
        drawn = base * np.exp(spread * noise) if base else spread * noise
        out[name] = __import__('jax').numpy.asarray(drawn.astype(out[name].dtype))
    for name, factor in factors.items():
        out[name] = (out[name] * factor).astype(out[name].dtype)
    return out
```

```python
import concourse.bass as bass
from concourse import mybir

F32 = mybir.dt.float32
F32R = mybir.dt.float32r
BF16 = mybir.dt.bfloat16
I32 = mybir.dt.int32
U32 = mybir.dt.uint32
ALU = mybir.AluOpType
ACT = mybir.ActivationFunctionType
AX = mybir.AxisListType

P = 128
S = 1024
D = 1024
T = S // P
K = D // P
HEADS, HD = 16, 64
WINDOWS = (2, 4, 8, 16)
GW = D // len(WINDOWS)
G, E = 4, 4
NE = G * E
FE = 256
KF = FE // P
TOPK = 2
BLOCKS = (TOPK * S + NE * (P - 1)) // P
NB = 32
LEAST = TOPK * S // P
EPS = 1e-6
NEG = -1e30
CH = 2048
ORDER = (7, 0, 6, 1, 5, 2, 4, 3)
AUG = 4
HK = HD + AUG


def trunk(nc, x, mix_norm, ffn_norm, pool_w, pool_scale, kv_norm, w_k, w_v, w_f, b_f, w_q, w_o,
          router_g, router_g_b, router_e, router_e_b, w_gate, w_up, w_down, final_norm, out):
    start = (nc.sbuf_base + 31) // 32 * 32
    REG = 32768
    R = [start, start + REG, start + 2 * REG]
    RAW0 = start + 3 * REG
    SPL0 = RAW0 + 6 * CH * 4
    SMALL0 = SPL0 + 6 * CH * 4
    small_at = [SMALL0]

    def at(name, shape, dtype, offset):
        return nc.alloc_sbuf_tensor_at(name, shape, dtype, offset=offset)

    def size(shape, dtype):
        n = 2 if dtype == BF16 else 4
        for s in shape[1:]:
            n *= s
        return (n + 31) // 32 * 32

    def small(name, shape, dtype=F32):
        t = at(name, shape, dtype, small_at[0])
        small_at[0] += size(shape, dtype)
        return t

    def pack(name_shape_dtypes, offset, limit):
        made = []
        for name, shape, dtype in name_shape_dtypes:
            made.append(at(name, shape, dtype, offset))
            offset += size(shape, dtype)
        assert offset <= limit, (name_shape_dtypes[0][0], offset - limit)
        return made

    raw = at("raw", [P, 6, CH], F32, RAW0)
    w_hi = at("w_hi", [P, 3, CH], F32R, SPL0)
    w_lo = at("w_lo", [P, 3, CH], F32R, SPL0 + 3 * CH * 4)

    ident = small("ident", [P, P])
    ones = small("ones", [P, P])
    before = small("before", [P, P])
    upto = small("upto", [P, P])
    iota_p = small("iota_p", [P, P])
    ident_bf = small("ident_bf", [P, P], BF16)
    future_bf = small("future_bf", [P, P], BF16)
    stage = small("stage", [P, 4, 512], F32R)
    sumsq = small("sumsq", [P, T])
    inv = small("inv", [P, T])
    halfneg = small("halfneg", [P, T])
    gain_kv = small("gain_kv", [P, K])
    gain_q = small("gain_q", [P, K])
    wf_raw = small("wf_raw", [P, K, HEADS])
    wf_hi = small("wf_hi", [P, K, HEADS], F32R)
    wf_lo = small("wf_lo", [P, K, HEADS], F32R)
    bf_bc = small("bf_bc", [P, HEADS])
    neg_max = small("neg_max", [P, 4])
    row_sum = small("row_sum", [P, 4])
    row_inv = small("row_inv", [P, 2])
    idx_now = small("idx_now", [P, 2], I32)
    idle = small("idle", [P, 1])
    limit = nc.sbuf_usable_end
    assert small_at[0] <= limit, small_at[0] - limit

    h0 = at("h0", [P, T, D], F32, R[0])
    h1 = at("h1", [P, T, D], F32, R[2])
    pool_x = at("pool_x", [P, T, D], F32, R[1])
    (band, band0, band_prev, dT_hi, dT_lo, gain_bc0, scale_bc, idx_row) = pack([
        ("band", [P, 4, P], F32), ("band0", [P, 4, P], F32), ("band_prev", [P, 4, P], F32),
        ("dT_hi", [P, K, P], F32R), ("dT_lo", [P, K, P], F32R),
        ("gain_bc0", [P, D], F32), ("scale_bc", [P, D], F32), ("idx_row", [P, P], F32)],
        R[2], R[2] + REG)
    moe_mem = []
    for L in range(2):
        A, B = (R[1], R[2]) if L == 0 else (R[1], R[0])
        m = {}

        def put(specs, offset, lim):
            for (name, shape, dtype), t in zip(specs, pack([(f"{n}_{L}", s, d) for n, s, d in specs], offset, lim)):
                m[name] = t
        put([("xn", [P, 2, D], F32), ("xg", [P, 2, D], F32), ("xT_hi", [P, 2, D], F32R),
             ("xT_lo", [P, 2, D], F32R)], A, A + REG)
        put([("yg", [P, 4, D], F32), ("slot_of", [P, 2 * T, P], F32), ("junk", [P, D], F32)], A, A + REG)
        put([("y", [P, 2, D], F32), ("gain", [P, D], F32), ("rT", [P, D], F32), ("act", [P, FE], F32),
             ("silu", [P, FE], F32), ("aT_hi", [P, FE], F32R), ("aT_lo", [P, FE], F32R),
             ("wr", [P, K, G + NE], F32), ("br", [P, G + NE], F32), ("lg", [P, T, G + NE], F32),
             ("gm", [P, T], F32), ("t4", [P, T, G], F32), ("gi", [P, T], F32), ("og", [P, T, G], F32),
             ("gw", [P, T], F32), ("t16", [P, T, NE], F32), ("es", [P, T, E], F32),
             ("m1", [P, T], F32), ("m2", [P, T], F32), ("o1", [P, T, E], F32), ("o2", [P, T, E], F32),
             ("e2", [P, T], F32), ("wt", [P, 2, T], F32),
             ("s1", [P, T, NE], F32), ("s2", [P, T, NE], F32), ("sel", [P, T, NE], F32),
             ("cum", [P, T + 1, NE], F32), ("cmp", [P, NB * NE], F32), ("nb", [P, NE], F32),
             ("end", [P, NE], F32), ("base", [P, NE], F32), ("zero", [P, NE], F32), ("pf", [P, T, NE], F32),
             ("pos", [P, 2, T], F32), ("pos_i", [P, 2, T], I32), ("part_i", [P, 2, 2 * T], I32),
             ("part", [P, 2, 2 * T], F32), ("blk_of", [P, 2 * T, NB], F32),
             ("tok_i", [P, NB], I32), ("tab", [P, 3, NB], F32), ("tab_i", [P, 3, NB], I32), ("bit", [P, NB], F32)], B, B + REG)
        moe_mem.append(m)
    io4 = small("io4", [P, 4])
    thr = small("thr", [P, T])
    tokid = small("tokid", [P, T])
    assert small_at[0] <= limit, small_at[0] - limit
    hT_hi = at("hT_hi", [P, K, S], F32R, R[1])
    hT_lo = at("hT_lo", [P, K, S], F32R, R[2])
    (q1, q2, k1, k2) = pack([(n, [P, 2, S], F32R) for n in ("q1", "q2", "k1", "k2")], R[1], R[2])
    val = at("val", [P, T, D], F32, R[0])
    o_tok = at("o_tok", [P, T, D], F32, R[2])
    probs = at("probs", [P, 2, S], F32, RAW0 + 2 * CH * 4)
    probsT = at("probsT", [P, 2, S], F32, RAW0 + 3 * CH * 4)
    oT_hi = at("oT_hi", [P, K, S], F32R, R[1])
    oT_lo = at("oT_lo", [P, K, S], F32R, R[0])
    xhat = at("xhat", [P, 2, D], F32, RAW0 + 2 * CH * 4)
    zf = at("zf", [P, 3, T * HEADS], F32, RAW0 + 3 * CH * 4)
    fin_gain = at("fin_gain", [P, D], F32, R[1])
    fin_out = at("fin_out", [P, 4, D], F32, R[1] + 4096)
    fin_junk = at("fin_junk", [P, D], F32, R[1] + 5 * 4096)

    ps = nc.alloc_psum_tensor("ps", [P, 8, 512], F32)

    def banks(a, n=1):
        return ps[:, a:a + n, :].rearrange("p b n -> p (b n)")

    xn_d = nc.dram_tensor("xn_d", [S, D], F32)
    y_d = nc.dram_tensor("y_d", [BLOCKS * P, D], F32)
    h_d = nc.dram_tensor("h_d", [S, D], F32)
    kh_d = nc.dram_tensor("kh_d", [HEADS, HD, S], F32)
    ql_d = nc.dram_tensor("ql_d", [HEADS, HD, S], F32)
    k2_d = nc.dram_tensor("k2_d", [HEADS, HK, S], F32)
    q2_d = nc.dram_tensor("q2_d", [HEADS, HK, S], F32)

    def sem(name):
        return nc.alloc_semaphore(name=name)

    consts = sem("consts")
    x_in = [sem(f"x_in{t}") for t in range(T)]
    gains_in = sem("gains_in")
    loaded = [[sem(f"loaded{s}_{q}") for q in range(2)] for s in range(3)]
    hi_done = [sem(f"hi_done{s}") for s in range(3)]
    lo_done = [sem(f"lo_done{s}") for s in range(3)]
    used = [sem(f"used{s}") for s in range(3)]
    y_cleared = sem("y_cleared")
    slot_free = sem("slot_free")
    pool_w_scaled = sem("pool_w_scaled")
    sq_done = sem("sq_done")
    inv_done = sem("inv_done")
    dve_step = sem("dve_step")
    pool_step = sem("pool_step")
    act_step = sem("act_step")
    barrier = sem("barrier")
    poolx_done = sem("poolx_done")
    dT_ps = sem("dT_ps")
    dT_hi_done = sem("dT_hi_done")
    dT_lo_done = sem("dT_lo_done")
    py_ps = sem("py_ps")
    h_done = sem("h_done")
    xn_done = sem("xn_done")
    xn_out = [sem("xn_out0"), sem("xn_out1")]
    rT_ps = sem("rT_ps")
    rT_done = sem("rT_done")
    lg_ps = sem("lg_ps")
    soft_in = sem("soft_in")
    soft_out = sem("soft_out")
    sel_done = sem("sel_done")
    rank_ps = sem("rank_ps")
    slots_done = sem("slots_done")
    tok_ps = sem("tok_ps")
    tok_done = sem("tok_done")
    eid_done = sem("eid_done")
    idx_done = sem("idx_done")
    idle_done = sem("idle_done")
    gathered = [[sem(f"gathered{L}_{q}") for q in range(2)] for L in range(2)]
    xT_ps = sem("xT_ps")
    xT_hi_done = sem("xT_hi_done")
    xT_lo_done = sem("xT_lo_done")
    silu_done = sem("silu_done")
    act_done = sem("act_done")
    aT_ps = sem("aT_ps")
    aT_hi_done = sem("aT_hi_done")
    aT_lo_done = sem("aT_lo_done")
    y_act = sem("y_act")
    y_out = [sem("y_out0"), sem("y_out1")]
    y_back = [sem("y_back0"), sem("y_back1")]
    y_added = sem("y_added")
    xhat_done = sem("xhat_done")
    h_spilled = sem("h_spilled")
    h_back = [sem(f"h_back{t}") for t in range(T)]
    hT_ps = sem("hT_ps")
    hT_hi_done = sem("hT_hi_done")
    hT_lo_done = sem("hT_lo_done")
    wf_done = sem("wf_done")
    z_ps = sem("z_ps")
    zf_dve = sem("zf_dve")
    zf_act = sem("zf_act")
    f_ps = sem("f_ps")
    f_hi_done = sem("f_hi_done")
    f_lo_done = sem("f_lo_done")
    f_out = sem("f_out")
    ones_out = sem("ones_out")
    v_ps = sem("v_ps")
    v_done = sem("v_done")
    kq_ps = sem("kq_ps")
    kq_hi_done = sem("kq_hi_done")
    kq_lo_done = sem("kq_lo_done")
    kq_out = [sem("kq_out0"), sem("kq_out1")]
    head_in = [sem("head_in0"), sem("head_in1")]
    qk_ps = sem("qk_ps")
    max_done = sem("max_done")
    exp_done = sem("exp_done")
    pT_ps = sem("pT_ps")
    pT_dve = sem("pT_dve")
    pT_act = sem("pT_act")
    pv_ps = sem("pv_ps")
    rinv_done = sem("rinv_done")
    o_done = sem("o_done")
    oT_ps = sem("oT_ps")
    oT_hi_done = sem("oT_hi_done")
    oT_lo_done = sem("oT_lo_done")
    op_ps = sem("op_ps")
    op_done = sem("op_done")
    fin_done = sem("fin_done")
    out_done = [sem(f"out_done{q}") for q in range(4)]

    M_MOE0 = (1, 0, 0)
    PROJ = []
    nxt = [M_MOE0[0] + BLOCKS, BLOCKS, BLOCKS]
    for i in range(16):
        s = (i + 1) % 3
        PROJ.append((s, nxt[s]))
        nxt[s] += 1
    M_MOE1 = tuple(nxt)
    M_MOE = (M_MOE0, M_MOE1)

    def raw_slot(s, par):
        return s + 3 * par

    def gu_src(L, e, s):
        return [w[L][e].rearrange("(p k) f -> p k f", k=K)[:, 4 * s:4 * s + 4, :] for w in (w_gate, w_up)]

    def load(sp, s, m, par, parts, needed=None):
        sp_wait(sp, lo_done[s], m, -1)
        if needed is not None:
            sp.sem_inc(slot_free, 1)
        for j, src in enumerate(parts):
            dst = raw[:, raw_slot(s, par), j * CH // 2:(j + 1) * CH // 2]
            if len(src.shape) == 3:
                dst = dst.rearrange("p (k n) -> p k n", k=src.shape[1])
            if needed is None:
                sp.dma_start(dst, src).then_inc(loaded[s][par], 16)
            else:
                sp.dma_start(dst, src, cond=needed).then_inc(loaded[s][par], 16)

    def sp_wait(eng, sm, value, plus):
        if not isinstance(value, int) or value + plus > 0:
            eng.wait_ge(sm, value + plus)

    def loaded_value(m, par):
        return 16 * (m - par) + 32

    def hi(act, s, m, par, gain=None):
        act.wait_ge(loaded[s][par], loaded_value(m, par))
        sp_wait(act, used[s], m, 0)
        src = raw[:, raw_slot(s, par), :]
        if gain is None:
            return act.activation(w_hi[:, s, :], src, ACT.Copy).then_inc(hi_done[s], 1)
        n = CH // K
        for k in range(K):
            ins = act.activation(w_hi[:, s, k * n:(k + 1) * n], src[:, k * n:(k + 1) * n], ACT.Copy,
                                 scale=gain[:, k:k + 1])
        ins.then_inc(hi_done[s], 1)

    def lo(dve, s, m, par, gain=None):
        dve.wait_ge(hi_done[s], m + 1)
        src = raw[:, raw_slot(s, par), :]
        if gain is None:
            return dve.tensor_tensor(w_lo[:, s, :], src, w_hi[:, s, :].bitcast(F32), ALU.subtract)\
                      .then_inc(lo_done[s], 1)
        n = CH // K
        for k in range(K):
            ins = dve.scalar_tensor_tensor(out=w_lo[:, s, k * n:(k + 1) * n], in0=src[:, k * n:(k + 1) * n],
                                           scalar=gain[:, k:k + 1],
                                           in1=w_hi[:, s, k * n:(k + 1) * n].bitcast(F32),
                                           op0=ALU.mult, op1=ALU.subtract)
        ins.then_inc(lo_done[s], 1)

    def three(pe, o, a_hi, a_lo, b_hi, b_lo, first, last):
        pe.matmul(o, a_hi, b_hi, start=first, stop=False)
        pe.matmul(o, a_hi, b_lo, start=False, stop=False)
        return pe.matmul(o, a_lo, b_hi, start=False, stop=last)

    n_barrier = {}

    def meet(eng, key):
        n_barrier[key] = n_barrier.get(key, 0) + 1
        eng.drain().then_inc(barrier, 1)
        eng.wait_ge(barrier, 4 * n_barrier[key])

    chain = {"dve": 0, "pool": 0, "act": 0}
    steps = {"dve": dve_step, "pool": pool_step, "act": act_step}

    def link(eng, who, ins):
        chain[who] += 1
        ins.then_inc(steps[who], 1)
        eng.wait_ge(steps[who], chain[who])

    def blocks(eng, L, body, skip, finish, skip_last):
        eng.wait_ge(eid_done, L + 1)
        live = eng.value_load(moe_mem[L]["tab_i"][0:1, 2, 0:1], min_val=LEAST, max_val=BLOCKS)
        for b in range(3):
            body(b, b % 2, b == 0, False)
        with eng.Fori(0, (BLOCKS - 5) // 2) as i:
            with eng.If(2 * i + 2 < live):
                body(2 * i + 3, 1, False, False)
                body(2 * i + 4, 0, False, False)
            with eng.Else():
                skip(2 * i + 3)
        with eng.If(live > BLOCKS - 3):
            body(BLOCKS - 2, 1, False, False)
            body(BLOCKS - 1, 0, False, True)
            finish()
        with eng.Else():
            skip_last()

    def count(eng, *counts):
        eng.drain()
        for sems, n in counts:
            for sm in sems:
                eng.sem_inc(sm, n)

    def fresh_mask(eng, L):
        eng.wait_ge(eid_done, L + 1)
        row = moe_mem[L]["tab_i"]
        low = eng.value_load(row[0:1, 2, 1:2], min_val=0, max_val=2 ** 16 - 1)
        high = eng.value_load(row[0:1, 2, 2:3], min_val=0, max_val=2 ** 15 - 1)
        return low + high * 2 ** 16

    def is_fresh(mask, b):
        return (mask >> b) & 1

    def bc(ap, shape):
        return ap.to_broadcast(shape)

    block = nc.Block()
    block.__enter__()

    def sp_moe(sp, L):
        m = moe_mem[L]
        base = M_MOE[L]
        for t in range(T):
            sp.wait_ge(xn_done, T * L + t + 1)
            sp.dma_start(xn_d[t * P:(t + 1) * P, :], m["xn"][:, t % 2, :]).then_inc(xn_out[t % 2], 16)
        sp.wait_ge(eid_done, L + 1)

        def table(row, b):
            return sp.value_load(m["tab_i"][0:1, row, bass.ds(b, 1)], min_val=0, max_val=NE - 1)

        def load_block(b, par):
            e, fresh = table(0, b), table(1, b)
            for s in range(2):
                ws = [w[L][bass.ds(e, 1)].rearrange("e (p k) f -> p (e k) f", k=K)[:, 4 * s:4 * s + 4, :]
                      for w in (w_gate, w_up)]
                load(sp, s, base[s] + b, (base[s] + par) % 2, ws, fresh)
            wd = w_down[L][bass.ds(e, 1)].rearrange("e (p k) n -> p (e k) n", k=KF)
            load(sp, 2, base[2] + b, (base[2] + par) % 2, [wd[:, 0, :], wd[:, 1, :]], fresh)

        def store_y(b, par):
            sp.wait_ge(y_act, L * BLOCKS + b + 1)
            sp.dma_start(y_d[bass.ds(b * P, P), :], m["y"][:, par, :]).then_inc(y_out[par], 16)

        def body(b, par, first, last):
            if not isinstance(b, int) or b + 2 < BLOCKS:
                load_block(b + 2, par)
            if not first:
                store_y(b - 1, 1 - par)

        def skip(b):
            for by_parity in loaded:
                for q in range(2):
                    sp.sem_inc(by_parity[q], 32)
            for q in range(2):
                sp.sem_inc(y_out[q], 16)

        def skip_last():
            sp.sem_inc(y_out[0], 32)
            sp.sem_inc(y_out[1], 16)

        load_block(0, 0)
        load_block(1, 1)
        sp.wait_ge(y_cleared, 16)
        blocks(sp, L, body, skip, lambda: store_y(BLOCKS - 1, 0), skip_last)

    def proj_load(sp, i):
        w = (w_v, w_k, w_q[0], w_o[0])[i // 4]
        s, m = PROJ[i]
        c = i % 4
        src = w.rearrange("(p k) n -> p k n", k=K)[:, :, c * 256:(c + 1) * 256]
        load(sp, s, m, m % 2, [src[:, 0:4, :], src[:, 4:8, :]])

    @block.sync
    def _(sp):
        for t in range(T):
            sp.dma_start(h0[:, t, :], x[0, t * P:(t + 1) * P, :]).then_inc(x_in[t], 16)
            if t == 0:
                sp.dma_start(gain_bc0[:, :], mix_norm[0:1, :].partition_broadcast(P)).then_inc(gains_in, 16)
            if t == 2:
                pw = pool_w[0].rearrange("g (c p) d -> p g c d", p=P)
                for j in range(2):
                    dst = raw[:, 0, j * CH // 2:(j + 1) * CH // 2].rearrange("p (g c d) -> p g c d", g=2, c=2)
                    sp.dma_start(dst, pw[:, 2 * j:2 * j + 2, :, :]).then_inc(loaded[0][0], 16)
        sp.dma_start(gain_kv[:, :], kv_norm.rearrange("(p k) -> p k", k=K)).then_inc(gains_in, 16)
        sp.dma_start(gain_q[:, :], mix_norm[1].rearrange("(p k) -> p k", k=K)).then_inc(gains_in, 16)
        sp.dma_start(wf_raw[:, :, :], w_f.rearrange("(p k) n -> p k n", k=K)).then_inc(gains_in, 16)
        sp.dma_start(bf_bc[:, :], b_f.unsqueeze(0).partition_broadcast(P)).then_inc(gains_in, 16)
        sp.wait_ge(consts, 1)
        sp.dma_start(y_d[LEAST * P:, :].rearrange("(p b) (c n) -> p (b c) n", p=P, n=P),
                     bc(ones[:, :].unsqueeze(1), [P, (BLOCKS - LEAST) * D // P, P])).then_inc(y_cleared, 16)
        for L in range(2):
            m = moe_mem[L]
            sp.wait_ge(barrier, 4 * (1 if L == 0 else 4))
            for dst, src in ((m["gain"][:, :], ffn_norm[L:L + 1, :].partition_broadcast(P)),
                             (m["wr"][:, :, 0:G], router_g[L].rearrange("(p k) n -> p k n", k=K)),
                             (m["wr"][:, :, G:G + NE], router_e[L].rearrange("(p k) n -> p k n", k=K)),
                             (m["br"][:, 0:G], router_g_b[L:L + 1, :].partition_broadcast(P)),
                             (m["br"][:, G:G + NE], router_e_b[L:L + 1, :].partition_broadcast(P))):
                sp.dma_start(dst, src).then_inc(gains_in, 16)
            sp_moe(sp, L)
            if L == 1:
                break
            for i in range(3):
                proj_load(sp, i)
            sp.wait_ge(y_added, T)
            for t in range(T):
                sp.dma_start(h_d[t * P:(t + 1) * P, :], h0[:, t, :]).then_inc(h_spilled, 16)
            proj_load(sp, 3)
            for d, row in ((q2_d, HD), (q2_d, HD + 1), (k2_d, HD + 2), (k2_d, HD + 3)):
                sp.dma_start(d[:, row, :].rearrange("h (c n) -> h c n", n=P),
                             ones[0:HEADS, :].unsqueeze(1).to_broadcast([HEADS, S // P, P]))\
                  .then_inc(ones_out, 16)
            for half in range(2):
                cols = slice(512 * half, 512 * half + 512)
                sp.wait_ge(f_lo_done, half + 1)
                for row, j, d in ((66, 0, q2_d), (67, 1, q2_d), (64, 2, k2_d), (65, 3, k2_d)):
                    sp.dma_start(d[:, row, cols], stage[0:HEADS, j, :].bitcast(F32)).then_inc(f_out, 16)
            for i in range(4, 7):
                proj_load(sp, i)
            for c in range(8):
                proj_load(sp, 7 + c)
                for u in range(4):
                    n = 4 * c + u
                    i, par = n // 2 % 8, n % 2
                    half = n % 2
                    cols = slice(512 * half, 512 * half + 512)
                    sp.wait_ge(kq_lo_done, n + 1)
                    full, aug = (kh_d, k2_d) if n < 16 else (ql_d, q2_d)
                    jf, ja = (0, 1) if n < 16 else (1, 0)
                    sp.dma_start(full[2 * i:2 * i + 2, :, cols].rearrange("h d n -> (h d) n"),
                                 stage[:, 2 * par + jf, :].bitcast(F32)).then_inc(kq_out[par], 16)
                    for z in range(2):
                        sp.dma_start(aug[2 * i + z, 0:HD, cols],
                                     stage[HD * z:HD * z + HD, 2 * par + ja, :].bitcast(F32)).then_inc(kq_out[par], 16)
            proj_load(sp, 15)
            for q in range(2):
                sp.wait_ge(kq_out[q], 48 * 16)
            sp.wait_ge(f_out, 128)
            sp.wait_ge(ones_out, 64)
            sp.wait_ge(h_spilled, 16 * T)
            sp.wait_ge(barrier, 4 * 2)

            def load_head(hd, par):
                for dst, src in ((q1[0:HD, par, :], q2_d[bass.ds(hd, 1), 0:HD, :]),
                                 (q1[HD:P, par, :], ql_d[bass.ds(hd, 1), :, :]),
                                 (k1[0:HD, par, :], kh_d[bass.ds(hd, 1), :, :]),
                                 (k1[HD:P, par, :], kh_d[bass.ds(hd, 1), :, :]),
                                 (q2[0:HK, par, :], q2_d[bass.ds(hd, 1), :, :]),
                                 (k2[0:HK, par, :], k2_d[bass.ds(hd, 1), :, :])):
                    sp.dma_start(dst.bitcast(F32), src.rearrange("h d n -> (h d) n")).then_inc(head_in[par], 16)
            load_head(0, 0)
            load_head(1, 1)
            with sp.Fori(0, HEADS // 2 - 1) as p:
                hd = 2 * p
                sp.wait_ge(qk_ps, hd * T + T)
                load_head(hd + 2, 0)
                sp.wait_ge(qk_ps, hd * T + 2 * T)
                load_head(hd + 3, 1)
            for t in range(T):
                sp.wait_ge(oT_ps, t + 1)
                sp.dma_start(h1[:, t, :], h_d[t * P:(t + 1) * P, :]).then_inc(h_back[t], 16)
        sp.wait_ge(barrier, 4 * 5)
        sp.dma_start(fin_gain[:, :], final_norm.unsqueeze(0).partition_broadcast(P)).then_inc(gains_in, 16)
        for t in range(T):
            sp.wait_ge(fin_done, t + 1)
            sp.dma_start(out[0, t * P:(t + 1) * P, :], fin_out[:, t % 4, :]).then_inc(out_done[t % 4], 16)
        for q in range(4):
            sp.wait_ge(out_done[q], 16 * T // 4)
        for s in range(3):
            chunks = M_MOE1[s] + BLOCKS
            for q in range(2):
                sp.wait_ge(loaded[s][q], 32 * ((chunks + 1 - q) // 2))

    n_inv = [0]

    def rsqrt_tile(pool, t):
        n_inv[0] += 1
        pool.wait_ge(sq_done, n_inv[0])
        link(pool, "pool", pool.tensor_scalar(sumsq[:, t:t + 1], sumsq[:, t:t + 1], 1.0 / D, EPS, ALU.mult, ALU.add))
        pool.tensor_tensor(inv[:, t:t + 1], sumsq[:, t:t + 1], halfneg[:, t:t + 1], ALU.pow).then_inc(inv_done, 1)

    def pool_moe(pool, L):
        m = moe_mem[L]
        for t in range(T):
            rsqrt_tile(pool, t)
        pool.wait_ge(tok_done, L + 1)
        for q in range(2):
            pool.wait_ge(xn_out[q], 64 * (L + 1))

        def gather(b, par):
            if not isinstance(b, int) or b >= 2:
                pool.wait_ge(xT_ps, L * BLOCKS + b - 1)
            sp_wait(pool, idle_done, L * BLOCKS + b, 0)
            pool.tensor_copy(idx_now[:, par:par + 1], m["tok_i"][:, bass.ds(b, 1)]).then_inc(idx_done, 1)
            pool.wait_ge(idx_done, L * BLOCKS + b + 1)
            pool.tensor_tensor(idle[:, :], halfneg[:, 0:1], halfneg[:, 0:1], ALU.add).then_inc(idle_done, 1)
            pool.indirect_dma_start(
                out=m["xg"][:, par, :], out_offset=None, in_=xn_d[:, :],
                in_offset=bass.IndirectOffsetOnAxis(ap=idx_now[:, par:par + 1].bitcast(U32), axis=0),
            ).then_inc(gathered[L][par], 16)

        def body(b, par, first, last):
            if not last:
                gather(b + 1, 1 - par)

        gather(0, 0)
        blocks(pool, L, body, lambda b: count(pool, ((idx_done, idle_done), 2)), lambda: None,
               lambda: count(pool, ((idx_done, idle_done), 1)))
        pool.wait_ge(y_out[0], 16 * 16 * (L + 1))
        pool.wait_ge(y_out[1], 16 * 15 * (L + 1))
        for t in range(T):
            if t >= 2:
                pool.wait_ge(y_added, T * L + t - 1)
            for j in range(2):
                pool.indirect_dma_start(
                    out=m["yg"][:, 2 * (t % 2) + j, :], out_offset=None, in_=y_d[:, :],
                    in_offset=bass.IndirectOffsetOnAxis(ap=m["pos_i"][:, j, t:t + 1].bitcast(U32), axis=0),
                ).then_inc(y_back[t % 2], 16)

    @block.gpsimd
    def _(pool):
        pool.memset(halfneg[:, :], -0.5)
        pool.memset(ones[:, :], 1.0)
        pool.memset(ident[:, :], 0.0)
        pool.memset(before[:, :], 1.0)
        pool.memset(upto[:, :], 1.0)
        pool.memset(future_bf[:, :], 0.0)
        for g, w in enumerate(WINDOWS):
            pool.memset(band[:, g, :], 1.0)
            pool.memset(band_prev[:, g, :], 1.0 / w)
        pool.iota(iota_p[:, :], [[1, P]], base=0, channel_multiplier=0, allow_small_or_imprecise_dtypes=True)
        pool.iota(idx_row[:, :], [[1, P]], base=1, channel_multiplier=0, allow_small_or_imprecise_dtypes=True)
        pool.iota(io4[:, :], [[1, 4]], base=-8, channel_multiplier=0, allow_small_or_imprecise_dtypes=True)
        pool.iota(thr[:, :], [[P, T]], base=0, channel_multiplier=0, allow_small_or_imprecise_dtypes=True)
        link(pool, "pool", pool.iota(tokid[:, :], [[P, T]], base=0, channel_multiplier=1,
                                     allow_small_or_imprecise_dtypes=True))
        row = [[1, P]]
        pool.affine_select(out=ident[:, :], in_=ident[:, :], compare_op=ALU.not_equal, fill=1.0, base=0,
                           pattern=[[-1, P]], channel_multiplier=1)
        pool.affine_select(out=before[:, :], in_=before[:, :], compare_op=ALU.is_gt, fill=0.0, base=0,
                           pattern=row, channel_multiplier=-1)
        pool.affine_select(out=upto[:, :], in_=upto[:, :], compare_op=ALU.is_ge, fill=0.0, base=0,
                           pattern=row, channel_multiplier=-1)
        pool.affine_select(out=future_bf[:, :], in_=future_bf[:, :], compare_op=ALU.is_ge, fill=NEG, base=0,
                           pattern=[[-1, P]], channel_multiplier=1)
        for g, w in enumerate(WINDOWS):
            pool.affine_select(out=band_prev[:, g, :], in_=band_prev[:, g, :], compare_op=ALU.is_ge, fill=0.0,
                               base=w - 1 - P, pattern=[[-1, P]], channel_multiplier=1)
            link(pool, "pool", pool.affine_select(out=band[:, g, :], in_=band[:, g, :], compare_op=ALU.is_ge,
                                                  fill=0.0, base=0, pattern=row, channel_multiplier=-1))
            last = pool.affine_select(out=band[:, g, :], in_=band[:, g, :], compare_op=ALU.is_ge, fill=0.0,
                                      base=w - 1, pattern=[[-1, P]], channel_multiplier=1)
        last.then_inc(consts, 1)
        for t in range(T):
            rsqrt_tile(pool, t)
        meet(pool, "pool")
        pool_moe(pool, 0)
        for t in range(T):
            rsqrt_tile(pool, t)
        meet(pool, "pool")
        meet(pool, "pool")
        meet(pool, "pool")
        pool_moe(pool, 1)
        meet(pool, "pool")
        for t in range(T):
            rsqrt_tile(pool, t)

    def act_moe(act, L):
        m = moe_mem[L]
        base = M_MOE[L]
        N = L * BLOCKS
        h = (h0, h1)[L]
        for t in range(T):
            if t:
                act.wait_ge(sq_done, T * (1 + 2 * L) + t)
            act.activation(m["junk"][:, :], h[:, t, :], ACT.Square, accum_out=sumsq[:, t:t + 1]).then_inc(sq_done, 1)
            if t >= 1:
                router_T(act, m, L, t - 1)
        router_T(act, m, L, T - 1)
        for j in range(2):
            act.wait_ge(soft_in, 2 * L + j + 1)
            if j == 0:
                act.activation(m["t4"][:, :, :], m["t4"][:, :, :], ACT.Exp).then_inc(soft_out, 1)
            else:
                act.activation(m["e2"][:, :], m["e2"][:, :], ACT.Exp).then_inc(soft_out, 1)

        def xT_hi_(b, par):
            act.wait_ge(xT_ps, N + b + 1)
            if not isinstance(b, int) or b >= 2:
                act.wait_ge(used[1], base[1] + b - 1)
            act.activation(m["xT_hi"][:, par, :], banks(2, 2), ACT.Copy).then_inc(xT_hi_done, 1)

        def aT_hi_(b):
            act.wait_ge(aT_ps, N + b + 1)
            sp_wait(act, used[2], base[2] + b, 0)
            act.activation(m["aT_hi"][:, :], ps[:, 4, 0:FE], ACT.Copy).then_inc(aT_hi_done, 1)

        def y_copy(b, par):
            act.wait_ge(used[2], base[2] + b + 1)
            if not isinstance(b, int) or b >= 2:
                act.wait_ge(y_out[par], y_count(L, b, par))
            act.activation(m["y"][:, par, :], banks(5, 2), ACT.Copy).then_inc(y_act, 1)

        mask = fresh_mask(act, L)

        def body(b, par, first, last):
            def middle():
                act.wait_ge(used[1], base[1] + b + 1)
                if not first:
                    act.wait_ge(act_done, N + b)
                act.activation(m["silu"][:, :], ps[:, par, 0:FE], ACT.Silu).then_inc(silu_done, 1)

            if not first:
                aT_hi_(b - 1)
            if last:
                middle()
            else:
                xT_hi_(b + 1, 1 - par)
                with act.If(is_fresh(mask, b + 1)):
                    hi(act, 0, base[0] + b + 1, (base[0] + 1 - par) % 2)
                    middle()
                    hi(act, 1, base[1] + b + 1, (base[1] + 1 - par) % 2)
                with act.Else():
                    count(act, (hi_done[0:1], 1))
                    middle()
                    count(act, (hi_done[1:2], 1))
            with act.If(is_fresh(mask, b)):
                hi(act, 2, base[2] + b, (base[2] + par) % 2)
            with act.Else():
                count(act, (hi_done[2:3], 1))
            if not first:
                y_copy(b - 1, 1 - par)

        def finish():
            aT_hi_(BLOCKS - 1)
            y_copy(BLOCKS - 1, 0)

        def skip(b):
            count(act, ((aT_hi_done, xT_hi_done, *hi_done, silu_done, y_act), 2))

        def skip_last():
            count(act, ((xT_hi_done, *hi_done[0:2]), 1), ((hi_done[2], silu_done), 2), ((aT_hi_done, y_act), 3))

        hi(act, 0, base[0], base[0] % 2)
        hi(act, 1, base[1], base[1] % 2)
        xT_hi_(0, 0)
        blocks(act, L, body, skip, finish, skip_last)

    def y_count(L, b, par):
        per = (16, 15)[par] * 16 * L
        return per + 8 * (b - par)

    def router_T(act, m, L, t):
        act.wait_ge(rT_ps, T * L + t + 1)
        sp_wait(act, lg_ps, T * L + t, 0)
        act.activation(m["rT"][:, :], banks(2, 2) if t % 2 else banks(0, 2), ACT.Copy).then_inc(rT_done, 1)

    @block.scalar
    def _(act):
        act.dma_start(scale_bc[:, :], pool_scale[0:1, :].partition_broadcast(P)).then_inc(gains_in, 16)
        for t in range(T):
            act.wait_ge(x_in[t], 16)
            act.activation(pool_x[:, t, :], h0[:, t, :], ACT.Square, accum_out=sumsq[:, t:t + 1]).then_inc(sq_done, 1)
        act.wait_ge(pool_w_scaled, 1)
        act.activation(w_hi[:, 0, :], raw[:, 0, :], ACT.Copy).then_inc(hi_done[0], 1)
        for t in range(T):
            act.wait_ge(dT_ps, t + 1)
            if t >= 1:
                act.wait_ge(py_ps, t)
            act.activation(dT_hi[:, :, :].rearrange("p k n -> p (k n)"), banks(2 * (t % 2), 2), ACT.Copy)\
               .then_inc(dT_hi_done, 1)
        meet(act, "act")
        act_moe(act, 0)
        for t in range(T):
            act.wait_ge(y_added, t + 1)
            if t >= 2:
                act.wait_ge(hT_ps, t - 1)
            act.activation(xhat[:, t % 2, :], h0[:, t, :], ACT.Square, accum_out=sumsq[:, t:t + 1]).then_inc(sq_done, 1)
            act.wait_ge(inv_done, 2 * T + t + 1)
            act.wait_ge(sq_done, 2 * T + t + 1)
            act.activation(xhat[:, t % 2, :], h0[:, t, :], ACT.Copy, scale=inv[:, t:t + 1]).then_inc(xhat_done, 1)
            act.wait_ge(hT_ps, t + 1)
            act.wait_ge(y_added, T)
            act.activation(hT_hi[:, :, t * P:(t + 1) * P], banks(2 * (t % 2), 2).rearrange("p (k n) -> p k n", k=K),
                           ACT.Copy).then_inc(hT_hi_done, 1)
        act.wait_ge(gains_in, 16 * 11)
        for k in range(K):
            act.activation(wf_hi[:, k, :], wf_raw[:, k, :], ACT.Copy, scale=gain_kv[:, k:k + 1]).then_inc(wf_done, 1)
        for i in range(3):
            hi(act, *PROJ[i], PROJ[i][1] % 2, gain_kv)
        act.wait_ge(zf_dve, 1)
        act.activation(zf[:, 1, :], zf[:, 1, :], ACT.Exp, scale=-1.0).then_inc(zf_act, 1)
        act.wait_ge(zf_act, 1)
        act.activation(zf[:, 1, :], zf[:, 1, :], ACT.Ln, bias=1.0).then_inc(zf_act, 1)
        act.wait_ge(h_spilled, 16 * T)
        for c in range(4):
            for t in range(T):
                n = T * c + t
                act.wait_ge(v_ps, n + 1)
                act.activation(val[:, t, c * 256:(c + 1) * 256], ps[:, n % 4, 0:256], ACT.Copy).then_inc(v_done, 1)
            hi(act, *PROJ[c + 3], PROJ[c + 3][1] % 2, gain_kv)
            if c == 0:
                for half in range(2):
                    act.wait_ge(f_ps, 1)
                    if half:
                        act.wait_ge(f_out, 64)
                    act.activation(stage[0:HEADS, 0, :], ps[0:HEADS, 6 + half, :], ACT.Copy).then_inc(f_hi_done, 1)
        hi_next = 7
        for n in range(32):
            act.wait_ge(kq_ps, n + 1)
            if n >= 2:
                act.wait_ge(kq_out[n % 2], 48 * (n // 2))
            elif n == 0:
                act.wait_ge(f_out, 128)
            scale = 1.0 if n < 16 else HD ** -0.5
            act.activation(stage[:, 2 * (n % 2), :], ps[:, n % 4, :], ACT.Copy, scale=scale).then_inc(kq_hi_done, 1)
            if n % 4 == 3 and hi_next < 15:
                g = gain_kv if hi_next < 8 else gain_q if hi_next < 12 else None
                hi(act, *PROJ[hi_next], PROJ[hi_next][1] % 2, g)
                hi_next += 1
        meet(act, "act")

        def exp_(hd, i):
            u, q = i % 2, i % 4
            act.wait_ge(max_done, hd * T + i + 1)
            if not isinstance(hd, int) or hd * T + i >= 2:
                act.wait_ge(pT_ps, hd * T + i - 1)
            if not isinstance(hd, int) or hd * T + i >= 4:
                act.wait_ge(rinv_done, hd * T + i - 3)
            n = (ORDER[i] + 1) * P
            act.activation(probs[:, u, 0:n], banks(2 * u, 2)[:, 0:n], ACT.Exp, bias=neg_max[:, q:q + 1],
                           accum_out=row_sum[:, q:q + 1]).then_inc(exp_done, 1)

        def pT_late(hd, i):
            if ORDER[i] >= 4:
                act.wait_ge(pT_ps, hd * T + i + 1)
                sp_wait(act, pv_ps, hd * T + i, -1)
                n = (ORDER[i] - 3) * P
                act.activation(probsT[:, i % 2, 512:512 + n], ps[:, 5, 0:n], ACT.Copy).then_inc(pT_act, 1)

        def pair(hd, last):
            for j in range(2):
                for i in range(T):
                    if i < T - 1:
                        exp_(hd + j, i + 1)
                    elif not (last and j == 1):
                        exp_(hd + j + 1, 0)
                    pT_late(hd + j, i)

        act.wait_ge(lo_done[0], 36)
        act.wait_ge(lo_done[2], 35)
        exp_(0, 0)
        pair(0, False)
        with act.Fori(1, HEADS // 2 - 1) as p:
            pair(2 * p, False)
        pair(HEADS - 2, True)
        meet(act, "act")
        for t in range(T):
            act.wait_ge(oT_ps, t + 1)
            act.activation(oT_hi[:, :, t * P:(t + 1) * P], banks(2 * (t % 2), 2).rearrange("p (k n) -> p k n", k=K),
                           ACT.Copy).then_inc(oT_hi_done, 1)
        hi(act, *PROJ[15], PROJ[15][1] % 2)
        meet(act, "act")
        act_moe(act, 1)
        meet(act, "act")
        for t in range(T):
            if t:
                act.wait_ge(sq_done, 4 * T + t)
            act.activation(fin_junk[:, :], h1[:, t, :], ACT.Square, accum_out=sumsq[:, t:t + 1]).then_inc(sq_done, 1)

    def dve_moe(dve, L):
        m = moe_mem[L]
        base = M_MOE[L]
        N = L * BLOCKS
        h = (h0, h1)[L]
        dve.wait_ge(gains_in, 16 * (11 if L == 0 else 16))
        for t in range(T):
            dve.wait_ge(inv_done, T * (1 + 2 * L) + t + 1)
            if t >= 2:
                dve.wait_ge(xn_out[t % 2], 64 * L + 16 * (t // 2))
                dve.wait_ge(rT_ps, T * L + t - 1)
            dve.scalar_tensor_tensor(out=m["xn"][:, t % 2, :], in0=h[:, t, :], scalar=inv[:, t:t + 1],
                                     in1=m["gain"][:, :], op0=ALU.mult, op1=ALU.mult).then_inc(xn_done, 1)

        def do(ins):
            link(dve, "dve", ins)

        do(dve.memset(m["zero"][:, :], 0.0))
        for n in range(NB // 2):
            ins = dve.memset(m["bit"][:, n:NB:NB // 2], 2.0 ** n)
        do(ins)
        do(dve.memset(m["cum"][:, 0, :], 0.0))
        dve.wait_ge(lg_ps, T * (L + 1))
        lg, gl = m["lg"], m["lg"][:, :, 0:G]
        el = m["lg"][:, :, G:G + NE].rearrange("p t (g e) -> p t g e", g=G)
        do(dve.tensor_tensor(lg[:, :, :], ps[:, 7, 0:T * (G + NE)].rearrange("p (t n) -> p t n", t=T),
                             bc(m["br"][:, :].unsqueeze(1), [P, T, G + NE]), ALU.add))

        def first_max(values, top, index, one_hot):
            do(dve.tensor_reduce(top[:, :], values, AX.X, ALU.max))
            do(dve.tensor_tensor(one_hot, values, bc(top[:, :].unsqueeze(2), [P, T, 4]), ALU.is_ge))
            do(dve.tensor_tensor(one_hot, one_hot, bc(io4[:, :].unsqueeze(1), [P, T, 4]), ALU.mult))
            do(dve.tensor_reduce(index[:, :], one_hot, AX.X, ALU.min))
            do(dve.tensor_tensor(one_hot, bc(io4[:, :].unsqueeze(1), [P, T, 4]),
                                 bc(index[:, :].unsqueeze(2), [P, T, 4]), ALU.is_equal))

        first_max(gl, m["gm"], m["gi"], m["og"][:, :, :])
        do(dve.tensor_tensor(m["t4"][:, :, :], gl, bc(m["gm"][:, :].unsqueeze(2), [P, T, G]), ALU.subtract))
        dve.sem_inc(soft_in, 1)
        t16 = m["t16"][:, :, :].rearrange("p t (g e) -> p t g e", g=G)
        do(dve.tensor_tensor(t16, el, bc(m["og"][:, :, :].unsqueeze(3), [P, T, G, E]), ALU.mult))
        do(dve.tensor_reduce(m["es"][:, :, :], m["t16"][:, :, :].rearrange("p t (g e) -> p t e g", g=G), AX.X, ALU.add))
        first_max(m["es"][:, :, :], m["m1"], m["gi"], m["o1"][:, :, :])
        do(dve.scalar_tensor_tensor(out=m["es"][:, :, :], in0=m["o1"][:, :, :], scalar=3 * NEG, in1=m["es"][:, :, :],
                                    op0=ALU.mult, op1=ALU.add))
        first_max(m["es"][:, :, :], m["m2"], m["gi"], m["o2"][:, :, :])
        do(dve.tensor_tensor(m["e2"][:, :], m["m2"][:, :], m["m1"][:, :], ALU.subtract))
        dve.sem_inc(soft_in, 1)
        for s_, o_ in (("s1", "o1"), ("s2", "o2")):
            do(dve.tensor_tensor(m[s_][:, :, :].rearrange("p t (g e) -> p t g e", g=G),
                                 bc(m["og"][:, :, :].unsqueeze(3), [P, T, G, E]),
                                 bc(m[o_][:, :, :].unsqueeze(2), [P, T, G, E]), ALU.mult))
        do(dve.tensor_tensor(m["sel"][:, :, :], m["s1"][:, :, :], m["s2"][:, :, :], ALU.add))
        for t in range(T):
            do(dve.tensor_tensor(m["cum"][:, t + 1, :], m["cum"][:, t, :], m["sel"][:, t, :], ALU.add))
        dve.sem_inc(sel_done, 1)
        dve.wait_ge(rank_ps, L + 1)
        cmp_ = m["cmp"][:, 0:NE * T].rearrange("p (e t) -> p e t", e=NE)
        do(dve.tensor_tensor(cmp_, bc(ps[:, 6, P:P + NE].unsqueeze(2), [P, NE, T]),
                             bc(thr[:, :].unsqueeze(1), [P, NE, T]), ALU.is_gt))
        do(dve.tensor_reduce(m["nb"][:, :], cmp_, AX.X, ALU.add))
        do(dve.tensor_tensor_scan(m["end"][:, :], m["nb"][:, :], m["zero"][:, :], 0.0, ALU.add, ALU.add))
        do(dve.tensor_tensor(m["base"][:, :], m["end"][:, :], m["nb"][:, :], ALU.subtract))
        cmp2 = m["cmp"][:, :].rearrange("p (b e) -> p b e", e=NE)
        do(dve.tensor_tensor(cmp2, bc(iota_p[:, 0:NB].unsqueeze(2), [P, NB, NE]),
                             bc(m["end"][:, :].unsqueeze(1), [P, NB, NE]), ALU.is_ge))
        do(dve.tensor_reduce(m["tab"][:, 1, :], cmp2, AX.X, ALU.add))
        do(dve.tensor_scalar(m["tab"][:, 0, :], m["tab"][:, 1, :], float(NE - 1), None, ALU.min))
        do(dve.tensor_tensor(m["tab"][:, 1, 1:NB], m["tab"][:, 0, 1:NB], m["tab"][:, 0, 0:NB - 1], ALU.not_equal))
        do(dve.memset(m["tab"][:, 1, 0:1], 1.0))
        do(dve.tensor_copy(m["tab"][:, 2, :], bc(m["end"][:, NE - 1:NE], [P, NB])))
        do(dve.tensor_tensor(m["bit"][:, :], m["bit"][:, :], m["tab"][:, 1, :], ALU.mult))
        do(dve.tensor_reduce(m["tab"][:, 2, 1:3], m["bit"][:, :].rearrange("p (h n) -> p h n", h=2), AX.X, ALU.add))
        dve.tensor_copy(m["tab_i"][:, :, :], m["tab"][:, :, :]).then_inc(eid_done, 1)
        do(dve.scalar_tensor_tensor(out=m["pf"][:, :, :], in0=bc(m["base"][:, :].unsqueeze(1), [P, T, NE]),
                                    scalar=float(P), in1=ps[:, 6, 0:P].rearrange("p (t e) -> p t e", t=T),
                                    op0=ALU.mult, op1=ALU.add))
        for j, s_ in enumerate(("s1", "s2")):
            do(dve.tensor_tensor(m["t16"][:, :, :], m["pf"][:, :, :], m[s_][:, :, :], ALU.mult))
            do(dve.tensor_reduce(m["pos"][:, j, :], m["t16"][:, :, :], AX.X, ALU.add))
        do(dve.tensor_copy(m["pos_i"][:, :, :], m["pos"][:, :, :]))
        flat_i = m["pos_i"][:, :, :].rearrange("p j t -> p (j t)")
        do(dve.tensor_scalar(m["part_i"][:, 0, :], flat_i, P - 1, None, ALU.bitwise_and))
        do(dve.tensor_scalar(m["part_i"][:, 1, :], flat_i, 7, None, ALU.arith_shift_right))
        do(dve.tensor_copy(m["part"][:, :, :], m["part_i"][:, :, :]))
        do(dve.tensor_tensor(m["slot_of"][:, :, :], bc(iota_p[:, :].unsqueeze(1), [P, 2 * T, P]),
                             bc(m["part"][:, 0, :].unsqueeze(2), [P, 2 * T, P]), ALU.is_equal))
        do(dve.tensor_tensor(m["blk_of"][:, :, :], bc(iota_p[:, 0:NB].unsqueeze(1), [P, 2 * T, NB]),
                             bc(m["part"][:, 1, :].unsqueeze(2), [P, 2 * T, NB]), ALU.is_equal))
        for j in range(2):
            ins = dve.tensor_tensor(m["blk_of"][:, j * T:(j + 1) * T, :], m["blk_of"][:, j * T:(j + 1) * T, :],
                                    bc(tokid[:, :].unsqueeze(2), [P, T, NB]), ALU.mult)
            ins.then_inc(slots_done, 1)
        dve.wait_ge(tok_ps, L + 1)
        dve.tensor_copy(m["tok_i"][:, :], ps[:, 6, 256:256 + NB]).then_inc(tok_done, 1)

        def combine_weights():
            dve.wait_ge(soft_out, 2 * L + 1)
            do(dve.tensor_reduce(m["gw"][:, :], m["t4"][:, :, :], AX.X, ALU.add))
            do(dve.reciprocal(m["gw"][:, :], m["gw"][:, :]))
            dve.wait_ge(soft_out, 2 * L + 2)
            do(dve.tensor_scalar(m["m1"][:, :], m["e2"][:, :], 1.0, None, ALU.add))
            do(dve.reciprocal(m["m1"][:, :], m["m1"][:, :]))
            do(dve.tensor_tensor(m["wt"][:, 0, :], m["m1"][:, :], m["gw"][:, :], ALU.mult))
            do(dve.tensor_tensor(m["wt"][:, 1, :], m["wt"][:, 0, :], m["e2"][:, :], ALU.mult))

        def xT_lo_(b, par):
            dve.wait_ge(xT_hi_done, N + b + 1)
            dve.tensor_tensor(m["xT_lo"][:, par, :], banks(2, 2), m["xT_hi"][:, par, :].bitcast(F32), ALU.subtract)\
               .then_inc(xT_lo_done, 1)

        def aT_lo_(b):
            dve.wait_ge(aT_hi_done, N + b + 1)
            dve.tensor_tensor(m["aT_lo"][:, :], ps[:, 4, 0:FE], m["aT_hi"][:, :].bitcast(F32), ALU.subtract)\
               .then_inc(aT_lo_done, 1)

        mask = fresh_mask(dve, L)

        def body(b, par, first, last):
            def middle():
                dve.wait_ge(silu_done, N + b + 1)
                if not first:
                    dve.wait_ge(aT_ps, N + b)
                dve.tensor_tensor(m["act"][:, :], m["silu"][:, :], ps[:, par, FE:2 * FE], ALU.mult)\
                   .then_inc(act_done, 1)

            if not first:
                aT_lo_(b - 1)
            if last:
                middle()
            else:
                xT_lo_(b + 1, 1 - par)
                with dve.If(is_fresh(mask, b + 1)):
                    lo(dve, 0, base[0] + b + 1, (base[0] + 1 - par) % 2)
                    middle()
                    lo(dve, 1, base[1] + b + 1, (base[1] + 1 - par) % 2)
                with dve.Else():
                    count(dve, (lo_done[0:1], 1))
                    middle()
                    count(dve, (lo_done[1:2], 1))
            with dve.If(is_fresh(mask, b)):
                lo(dve, 2, base[2] + b, (base[2] + par) % 2)
            with dve.Else():
                count(dve, (lo_done[2:3], 1))

        def skip(b):
            count(dve, ((aT_lo_done, xT_lo_done, *lo_done, act_done), 2))

        def skip_last():
            count(dve, ((xT_lo_done, *lo_done[0:2]), 1), ((lo_done[2], act_done), 2), ((aT_lo_done,), 3))

        lo(dve, 0, base[0], base[0] % 2)
        lo(dve, 1, base[1], base[1] % 2)
        xT_lo_(0, 0)
        blocks(dve, L, body, skip, lambda: aT_lo_(BLOCKS - 1), skip_last)
        combine_weights()
        for t in range(T):
            dve.wait_ge(y_back[t % 2], 128 * L + 32 * (t // 2 + 1))
            for j in range(2):
                ins = dve.scalar_tensor_tensor(out=h[:, t, :], in0=m["yg"][:, 2 * (t % 2) + j, :],
                                               scalar=m["wt"][:, j, t:t + 1], in1=h[:, t, :],
                                               op0=ALU.mult, op1=ALU.add)
                if j == 0:
                    do(ins)
            ins.then_inc(y_added, 1)

    @block.vector
    def _(dve):
        def do(ins):
            link(dve, "dve", ins)

        dve.wait_ge(consts, 1)
        do(dve.tensor_copy(ident_bf[:, :], ident[:, :]))
        for g, w in enumerate(WINDOWS):
            do(dve.tensor_scalar(band0[:, g, :], idx_row[:, :], float(w), None, ALU.min))
            do(dve.reciprocal(band0[:, g, :], band0[:, g, :]))
            do(dve.tensor_tensor(band0[:, g, :], band0[:, g, :], band[:, g, :], ALU.mult))
            do(dve.tensor_tensor(band0[:, g, :], band0[:, g, :], ident[:, :], ALU.subtract))
            ins = dve.scalar_tensor_tensor(out=band[:, g, :], in0=band[:, g, :], scalar=1.0 / w, in1=ident[:, :],
                                           op0=ALU.mult, op1=ALU.subtract)
        ins.then_inc(consts, 1)
        dve.wait_ge(gains_in, 16 * 6)
        dve.wait_ge(loaded[0][0], 32)
        for c in range(2):
            rw = raw[:, 0, :].rearrange("p (g c d) -> p g c d", g=4, c=2)[:, :, c, :]
            ins = dve.tensor_tensor(rw, rw, scale_bc[:, :].rearrange("p (g d) -> p g d", g=4), ALU.mult)
            do(ins) if c == 0 else ins.then_inc(pool_w_scaled, 1)
        for t in range(T):
            dve.wait_ge(inv_done, t + 1)
            dve.scalar_tensor_tensor(out=pool_x[:, t, :], in0=h0[:, t, :], scalar=inv[:, t:t + 1],
                                     in1=gain_bc0[:, :], op0=ALU.mult, op1=ALU.mult).then_inc(poolx_done, 1)
        dve.wait_ge(hi_done[0], 1)
        dve.tensor_tensor(w_lo[:, 0, :], raw[:, 0, :], w_hi[:, 0, :].bitcast(F32), ALU.subtract).then_inc(lo_done[0], 1)
        for t in range(T):
            dve.wait_ge(dT_hi_done, t + 1)
            dve.tensor_tensor(dT_lo[:, :, :].rearrange("p k n -> p (k n)"), banks(2 * (t % 2), 2),
                              dT_hi[:, :, :].rearrange("p k n -> p (k n)").bitcast(F32), ALU.subtract)\
               .then_inc(dT_lo_done, 1)
            dve.wait_ge(py_ps, t + 1)
            dve.tensor_tensor(h0[:, t, :], h0[:, t, :], banks(4 + 2 * (t % 2), 2), ALU.add).then_inc(h_done, 1)
        meet(dve, "dve")
        dve_moe(dve, 0)
        for t in range(T):
            dve.wait_ge(hT_hi_done, t + 1)
            dve.tensor_tensor(hT_lo[:, :, t * P:(t + 1) * P], banks(2 * (t % 2), 2).rearrange("p (k n) -> p k n", k=K),
                              hT_hi[:, :, t * P:(t + 1) * P].bitcast(F32), ALU.subtract).then_inc(hT_lo_done, 1)
        for k in range(K):
            dve.wait_ge(wf_done, K)
            dve.scalar_tensor_tensor(out=wf_lo[:, k, :], in0=wf_raw[:, k, :], scalar=gain_kv[:, k:k + 1],
                                     in1=wf_hi[:, k, :].bitcast(F32), op0=ALU.mult, op1=ALU.subtract)\
               .then_inc(wf_done, 1)
        for i in range(3):
            lo(dve, *PROJ[i], PROJ[i][1] % 2, gain_kv)
        dve.wait_ge(z_ps, 1)
        zt = "p (t n) -> p t n"
        do(dve.tensor_tensor(zf[:, 0, :].rearrange(zt, t=T), ps[:, 4, 0:P].rearrange(zt, t=T),
                             bc(bf_bc[:, :].unsqueeze(1), [P, T, HEADS]), ALU.add))
        do(dve.tensor_scalar(zf[:, 2, :], zf[:, 0, :], 0.0, None, ALU.min))
        dve.scalar_tensor_tensor(out=zf[:, 1, :], in0=zf[:, 0, :], scalar=-1.0, in1=zf[:, 0, :],
                                 op0=ALU.mult, op1=ALU.max).then_inc(zf_dve, 1)
        dve.wait_ge(zf_act, 2)
        dve.tensor_tensor(zf[:, 0, :], zf[:, 2, :], zf[:, 1, :], ALU.subtract).then_inc(zf_dve, 1)
        lo(dve, *PROJ[3], PROJ[3][1] % 2, gain_kv)
        for half in range(2):
            dve.wait_ge(f_hi_done, half + 1)
            do(dve.tensor_tensor(stage[0:HEADS, 1, :], ps[0:HEADS, 6 + half, :],
                                 stage[0:HEADS, 0, :].bitcast(F32), ALU.subtract))
            do(dve.tensor_scalar(stage[0:HEADS, 2, :], stage[0:HEADS, 0, :].bitcast(F32), -1.0, None, ALU.mult))
            dve.tensor_scalar(stage[0:HEADS, 3, :], stage[0:HEADS, 1, :].bitcast(F32), -1.0, None, ALU.mult)\
               .then_inc(f_lo_done, 1)
        for i in range(4, 7):
            lo(dve, *PROJ[i], PROJ[i][1] % 2, gain_kv)
        lo_next = 7
        for n in range(32):
            dve.wait_ge(kq_hi_done, n + 1)
            scale = 1.0 if n < 16 else HD ** -0.5
            dve.scalar_tensor_tensor(out=stage[:, 2 * (n % 2) + 1, :], in0=ps[:, n % 4, :], scalar=scale,
                                     in1=stage[:, 2 * (n % 2), :].bitcast(F32), op0=ALU.mult, op1=ALU.subtract)\
               .then_inc(kq_lo_done, 1)
            if n % 4 == 3 and lo_next < 15:
                g = gain_kv if lo_next < 8 else gain_q if lo_next < 12 else None
                lo(dve, *PROJ[lo_next], PROJ[lo_next][1] % 2, g)
                lo_next += 1
        meet(dve, "dve")

        def max_(hd, i):
            u, q = i % 2, i % 4
            dve.wait_ge(qk_ps, hd * T + i + 1)
            if not isinstance(hd, int) or hd * T + i >= 4:
                dve.wait_ge(exp_done, hd * T + i - 3)
            dve.tensor_reduce(neg_max[:, q:q + 1], banks(2 * u, 2)[:, 0:(ORDER[i] + 1) * P], AX.X, ALU.max,
                              negate=True).then_inc(max_done, 1)

        def pT_early(hd, i):
            dve.wait_ge(pT_ps, hd * T + i + 1)
            n = min(ORDER[i] + 1, 4) * P
            dve.tensor_copy(probsT[:, i % 2, 0:n], ps[:, 4, 0:n]).then_inc(pT_dve, 1)

        def o_(hd, i):
            u, q = i % 2, i % 4
            dve.reciprocal(row_inv[:, u:u + 1], row_sum[:, q:q + 1]).then_inc(rinv_done, 1)
            dve.wait_ge(pv_ps, hd * T + i + 1)
            dve.wait_ge(rinv_done, hd * T + i + 1)
            dve.tensor_scalar(o_tok[:, ORDER[i], bass.ds(hd * HD, HD)], ps[:, 6 + u, 0:HD], row_inv[:, u:u + 1], None,
                              ALU.mult).then_inc(o_done, 1)

        def pair(hd, first, last):
            for j in range(2):
                for i in range(T):
                    if i < T - 1:
                        max_(hd + j, i + 1)
                    elif not (last and j == 1):
                        max_(hd + j + 1, 0)
                    pT_early(hd + j, i)
                    if i:
                        o_(hd + j, i - 1)
                    elif not (first and j == 0):
                        o_(hd + j - 1, T - 1)

        max_(0, 0)
        pair(0, True, False)
        with dve.Fori(1, HEADS // 2 - 1) as p:
            pair(2 * p, False, False)
        pair(HEADS - 2, False, True)
        o_(HEADS - 1, T - 1)
        meet(dve, "dve")
        for t in range(T):
            dve.wait_ge(oT_hi_done, t + 1)
            dve.tensor_tensor(oT_lo[:, :, t * P:(t + 1) * P], banks(2 * (t % 2), 2).rearrange("p (k n) -> p k n", k=K),
                              oT_hi[:, :, t * P:(t + 1) * P].bitcast(F32), ALU.subtract).then_inc(oT_lo_done, 1)
        for c in range(4):
            if c == 1:
                lo(dve, *PROJ[15], PROJ[15][1] % 2)
            for t in range(T):
                n = T * c + t
                if c == 0:
                    dve.wait_ge(h_back[t], 16)
                dve.wait_ge(op_ps, n + 1)
                hv = h1[:, t, c * 256:(c + 1) * 256]
                dve.tensor_tensor(hv, hv, ps[:, 4 + n % 4, 0:256], ALU.add).then_inc(op_done, 1)
        meet(dve, "dve")
        dve_moe(dve, 1)
        meet(dve, "dve")
        dve.wait_ge(gains_in, 16 * 17)
        for t in range(T):
            dve.wait_ge(inv_done, 4 * T + t + 1)
            if t >= 4:
                dve.wait_ge(out_done[t % 4], 16)
            dve.scalar_tensor_tensor(out=fin_out[:, t % 4, :], in0=h1[:, t, :], scalar=inv[:, t:t + 1],
                                     in1=fin_gain[:, :], op0=ALU.mult, op1=ALU.mult).then_inc(fin_done, 1)

    def transposes(pe, src, bank, n):
        dst = banks(bank, 2) if n * P > 512 else ps[:, bank, :]
        for k in range(n):
            ins = pe.transpose(dst[:, k * P:(k + 1) * P], src[:, k:n * P:n], ident[:, :])
        return ins

    def pe_moe(pe, L):
        m = moe_mem[L]
        base = M_MOE[L]
        N = L * BLOCKS
        pe.wait_ge(gains_in, 16 * (11 if L == 0 else 16))

        def logits(t):
            pe.wait_ge(rT_done, T * L + t + 1)
            o = ps[:, 7, t * (G + NE):(t + 1) * (G + NE)]
            for k in range(K):
                ins = pe.matmul(o, m["rT"][:, k * P:(k + 1) * P], m["wr"][:, k, :], start=(k == 0), stop=(k == K - 1))
            ins.then_inc(lg_ps, 1)

        for t in range(T):
            pe.wait_ge(xn_done, T * L + t + 1)
            if t >= 2:
                pe.wait_ge(rT_done, T * L + t - 1)
            transposes(pe, m["xn"][:, t % 2, :], 2 * (t % 2), K).then_inc(rT_ps, 1)
            if t >= 1:
                logits(t - 1)
        logits(T - 1)
        pe.wait_ge(sel_done, L + 1)
        sel = m["sel"][:, :, :].rearrange("p t e -> p (t e)")
        cum = m["cum"][:, 0:T, :].rearrange("p t e -> p (t e)")
        pe.matmul(ps[:, 6, 0:P], before[:, :], sel, start=True, stop=False)
        pe.matmul(ps[:, 6, 0:P], ones[:, :], cum, start=False, stop=True)
        pe.matmul(ps[:, 6, P:P + NE], ones[:, :], m["cum"][:, T, :], start=True, stop=True).then_inc(rank_ps, 1)
        pe.wait_ge(slots_done, 2 * L + 2)
        for j in range(2 * T):
            ins = pe.matmul(ps[:, 6, 256:256 + NB], m["slot_of"][:, j, :], m["blk_of"][:, j, :],
                            start=(j == 0), stop=(j == 2 * T - 1))
        ins.then_inc(tok_ps, 1)

        def xT(b, par):
            pe.wait_ge(gathered[L][par], 8 * (b - par) + 16)
            sp_wait(pe, xT_lo_done, N + b, 0)
            transposes(pe, m["xg"][:, par, :], 2, K).then_inc(xT_ps, 1)

        def gate_up(b, par, s):
            pe.wait_ge(lo_done[s], base[s] + b + 1)
            if s == 0:
                pe.wait_ge(xT_lo_done, N + b + 1)
                if not isinstance(b, int) or b >= 2:
                    pe.wait_ge(act_done, N + b - 1)
            o = ps[:, par, :].rearrange("p (j f) -> p j f", j=2)
            for k in range(4):
                kk = 4 * s + k
                wh = w_hi[:, s, :].rearrange("p (j k f) -> p j k f", j=2, k=4)[:, :, k, :]
                wl = w_lo[:, s, :].rearrange("p (j k f) -> p j k f", j=2, k=4)[:, :, k, :]
                ins = three(pe, o, m["xT_hi"][:, par, kk * P:(kk + 1) * P], m["xT_lo"][:, par, kk * P:(kk + 1) * P],
                            wh, wl, kk == 0, kk == K - 1)
            ins.then_inc(used[s], 1)

        def aT(b):
            pe.wait_ge(act_done, N + b + 1)
            sp_wait(pe, aT_lo_done, N + b, 0)
            transposes(pe, m["act"][:, :], 4, KF).then_inc(aT_ps, 1)

        def down(b):
            pe.wait_ge(lo_done[2], base[2] + b + 1)
            pe.wait_ge(aT_lo_done, N + b + 1)
            if not isinstance(b, int) or b >= 1:
                pe.wait_ge(y_act, N + b)
            for k in range(KF):
                for half in range(2):
                    c = slice(1024 * k + 512 * half, 1024 * k + 512 * half + 512)
                    ins = three(pe, ps[:, 5 + half, :], m["aT_hi"][:, k * P:(k + 1) * P],
                                m["aT_lo"][:, k * P:(k + 1) * P], w_hi[:, 2, c], w_lo[:, 2, c], k == 0, k == KF - 1)
            ins.then_inc(used[2], 1)

        def body(b, par, first, last):
            gate_up(b, par, 0)
            if not first:
                aT(b - 1)
            if not last:
                xT(b + 1, 1 - par)
            gate_up(b, par, 1)
            if not first:
                down(b - 1)

        def finish():
            aT(BLOCKS - 1)
            down(BLOCKS - 1)

        def skip(b):
            count(pe, ((xT_ps, aT_ps, *used), 2))

        def skip_last():
            count(pe, ((xT_ps,), 1), (used[0:2], 2), ((aT_ps, used[2]), 3))

        xT(0, 0)
        blocks(pe, L, body, skip, finish, skip_last)

    @block.tensor
    def _(pe):
        pe.wait_ge(consts, 2)

        def pooled(t):
            pe.wait_ge(poolx_done, t + 1)
            if t >= 2:
                pe.wait_ge(dT_lo_done, t - 1)
            for c in range(K):
                g = c // 2
                o = banks(2 * (t % 2), 2)[:, c * P:(c + 1) * P]
                ins = pe.matmul(o, pool_x[:, t, c * P:(c + 1) * P], (band if t else band0)[:, g, :],
                                start=True, stop=(t == 0))
                if t:
                    ins = pe.matmul(o, pool_x[:, t - 1, c * P:(c + 1) * P], band_prev[:, g, :],
                                    start=False, stop=True)
            ins.then_inc(dT_ps, 1)

        pooled(0)
        for t in range(T):
            if t + 1 < T:
                pooled(t + 1)
            pe.wait_ge(dT_lo_done, t + 1)
            if t == 0:
                pe.wait_ge(lo_done[0], 1)
            if t >= 2:
                pe.wait_ge(h_done, t - 1)
            for g in range(4):
                o = banks(4 + 2 * (t % 2), 2)[:, g * GW:(g + 1) * GW]
                for c in range(2):
                    w = slice((2 * g + c) * GW, (2 * g + c + 1) * GW)
                    ins = three(pe, o, dT_hi[:, 2 * g + c, :], dT_lo[:, 2 * g + c, :], w_hi[:, 0, w], w_lo[:, 0, w],
                                c == 0, c == 1)
            ins.then_inc(py_ps, 1)
            if t == T - 1:
                pe.drain().then_inc(used[0], 1)
        meet(pe, "pe")
        pe_moe(pe, 0)
        for t in range(T):
            pe.wait_ge(xhat_done, t + 1)
            if t >= 2:
                pe.wait_ge(hT_lo_done, t - 1)
            transposes(pe, xhat[:, t % 2, :], 2 * (t % 2), K).then_inc(hT_ps, 1)
        pe.wait_ge(hT_lo_done, T)
        pe.wait_ge(wf_done, 2 * K)
        for t in range(T):
            for k in range(K):
                ins = three(pe, ps[:, 4, t * HEADS:(t + 1) * HEADS], hT_hi[:, k, t * P:(t + 1) * P],
                            hT_lo[:, k, t * P:(t + 1) * P], wf_hi[:, k, :], wf_lo[:, k, :], k == 0, k == K - 1)
        ins.then_inc(z_ps, 1)
        def v_tiles(c):
            s, mm = PROJ[c]
            pe.wait_ge(lo_done[s], mm + 1)
            for t in range(T):
                n = T * c + t
                if n >= 4:
                    pe.wait_ge(v_done, n - 3)
                for k in range(K):
                    w = slice(k * 256, (k + 1) * 256)
                    ins = three(pe, ps[:, n % 4, 0:256], hT_hi[:, k, t * P:(t + 1) * P], hT_lo[:, k, t * P:(t + 1) * P],
                                w_hi[:, s, w], w_lo[:, s, w], k == 0, k == K - 1)
                ins.then_inc(v_ps, 1)
            pe.drain().then_inc(used[s], 1)

        v_tiles(0)
        pe.wait_ge(zf_dve, 2)
        for half in range(2):
            o = ps[0:HEADS, 6 + half, :]
            for j in range(4 * half + 4):
                lf = zf[:, 0, j * HEADS:(j + 1) * HEADS]
                first = max(0, j - 4 * half)
                if j >= 4 * half:
                    pe.matmul(o[:, first * P:(first + 1) * P], lf, upto[:, :], start=(j == 0), stop=False,
                              skip_group_check=True)
                    for c in range(first + 1, 4):
                        pe.matmul(o[:, c * P:(c + 1) * P], lf, ones[:, :], start=False, stop=False,
                                  skip_group_check=True)
                else:
                    for c in range(4):
                        pe.matmul(o[:, c * P:(c + 1) * P], lf, ones[:, :], start=(j == 0 and c == 0), stop=False,
                                  skip_group_check=True)
        pe.drain().then_inc(f_ps, 1)
        for c in range(1, 4):
            v_tiles(c)
        for c in range(8):
            s, mm = PROJ[4 + c]
            pe.wait_ge(lo_done[s], mm + 1)
            for r in range(2):
                for half in range(2):
                    n = 4 * c + 2 * r + half
                    if n >= 4:
                        pe.wait_ge(kq_lo_done, n - 3)
                    elif n == 0:
                        pe.wait_ge(v_done, 4 * T)
                    for k in range(K):
                        w = slice(k * 256 + r * P, k * 256 + (r + 1) * P)
                        tok = slice(512 * half, 512 * half + 512)
                        ins = three(pe, ps[:, n % 4, :], w_hi[:, s, w], w_lo[:, s, w], hT_hi[:, k, tok],
                                    hT_lo[:, k, tok], k == 0, k == K - 1)
                    ins.then_inc(kq_ps, 1)
            pe.drain().then_inc(used[s], 1)
        meet(pe, "pe")

        def scores(hd, hpar, u, i):
            if i == 0:
                pe.wait_ge(head_in[hpar], 48 * (hd - hpar) + 96)
            if not isinstance(hd, int) or hd * T + i >= 2:
                pe.wait_ge(exp_done, hd * T + i - 1)
            q = ORDER[i]
            tt = slice(q * P, (q + 1) * P)
            n = (q + 1) * P
            for c in range(0, n, 512):
                w = min(512, n - c)
                o = banks(2 * u, 2)[:, c:c + w]
                last = c + w == n
                pe.matmul(o, q1[:, hpar, tt], k1[:, hpar, c:c + w], start=True, stop=False)
                pe.matmul(o, q2[0:HK, hpar, tt], k2[0:HK, hpar, c:c + w], start=False, stop=not last)
            pe.matmul(banks(2 * u, 2)[:, q * P:n], ident_bf[:, :], future_bf[:, :], start=False, stop=True)\
              .then_inc(qk_ps, 1)

        def turn(hd, i):
            pe.wait_ge(exp_done, hd * T + i + 1)
            if not isinstance(hd, int) or hd * T + i >= 1:
                pe.wait_ge(pT_dve, hd * T + i)
            if ORDER[i] >= 4:
                sp_wait(pe, pT_act, hd * (T // 2), i // 2)
            for j in range(ORDER[i] + 1):
                ins = pe.transpose(banks(4, 2)[:, j * P:(j + 1) * P], probs[:, i % 2, j * P:(j + 1) * P], ident[:, :])
            ins.then_inc(pT_ps, 1)

        def weigh(hd, i):
            pe.wait_ge(pT_dve, hd * T + i + 1)
            if ORDER[i] >= 4:
                pe.wait_ge(pT_act, hd * (T // 2) + i // 2 + 1)
            if not isinstance(hd, int) or hd * T + i >= 2:
                pe.wait_ge(o_done, hd * T + i - 1)
            for j in range(ORDER[i] + 1):
                ins = pe.matmul(ps[:, 6 + i % 2, 0:HD], probsT[:, i % 2, j * P:(j + 1) * P],
                                val[:, j, bass.ds(hd * HD, HD)], start=(j == 0), stop=(j == ORDER[i]))
            ins.then_inc(pv_ps, 1)

        def pair(hd, first, last):
            for j in range(2):
                for i in range(T):
                    if i < T - 1:
                        scores(hd + j, j, (i + 1) % 2, i + 1)
                    elif not (last and j == 1):
                        scores(hd + j + 1, 1 - j, 0, 0)
                    turn(hd + j, i)
                    if i:
                        weigh(hd + j, i - 1)
                    elif not (first and j == 0):
                        weigh(hd + j - 1, T - 1)

        scores(0, 0, 0, 0)
        pair(0, True, False)
        with pe.Fori(1, HEADS // 2 - 1) as p:
            pair(2 * p, False, False)
        pair(HEADS - 2, False, True)
        weigh(HEADS - 1, T - 1)
        meet(pe, "pe")
        for t in range(T):
            if t >= 2:
                pe.wait_ge(oT_lo_done, t - 1)
            transposes(pe, o_tok[:, t, :], 2 * (t % 2), K).then_inc(oT_ps, 1)
        for c in range(4):
            s, mm = PROJ[12 + c]
            pe.wait_ge(lo_done[s], mm + 1)
            for t in range(T):
                n = T * c + t
                if c == 0:
                    pe.wait_ge(oT_lo_done, t + 1)
                if n >= 4:
                    pe.wait_ge(op_done, n - 3)
                for k in range(K):
                    w = slice(k * 256, (k + 1) * 256)
                    ins = three(pe, ps[:, 4 + n % 4, 0:256], oT_hi[:, k, t * P:(t + 1) * P],
                                oT_lo[:, k, t * P:(t + 1) * P], w_hi[:, s, w], w_lo[:, s, w], k == 0, k == K - 1)
                ins.then_inc(op_ps, 1)
            pe.drain().then_inc(used[s], 1)
        meet(pe, "pe")
        pe_moe(pe, 1)
        meet(pe, "pe")

    block.__exit__(None, None, None)


_INS = ['x', 'mix_norm', 'ffn_norm', 'pool_w', 'pool_scale', 'kv_norm', 'w_k', 'w_v', 'w_f', 'b_f', 'w_q', 'w_o',
        'router_g', 'router_g_b', 'router_e', 'router_e_b', 'w_gate', 'w_up', 'w_down', 'final_norm']


def kernel(**inputs):
    import numpy as np
    import concourse.bacc as bacc
    from concourse.bass_utils import run_bass_kernel_spmd

    nc = bacc.Bacc("TRN2", target_bir_lowering=False, num_devices=1)
    arrays, aps = {}, []
    for name in _INS:
        a = np.ascontiguousarray(inputs[name])
        arrays[f"in_{name}"] = a
        aps.append(nc.dram_tensor(f"in_{name}", a.shape, mybir.dt.from_np(a.dtype), kind="ExternalInput").ap())
    aps.append(nc.dram_tensor("out_0", (1, S, D), F32, kind="ExternalOutput").ap())
    trunk(nc, *aps)
    r = run_bass_kernel_spmd(nc, [arrays], core_ids=[0])
    return np.asarray(r.results[0]["out_0"])
```

```python
import concourse.bass as bass
from concourse import mybir

F32 = mybir.dt.float32
F32R = mybir.dt.float32r
BF16 = mybir.dt.bfloat16
I32 = mybir.dt.int32
U32 = mybir.dt.uint32
ALU = mybir.AluOpType
ACT = mybir.ActivationFunctionType
AX = mybir.AxisListType

P = 128
S = 1024
D = 1024
T = S // P
K = D // P
HEADS, HD = 16, 64
WINDOWS = (2, 4, 8, 16)
GW = D // len(WINDOWS)
G, E = 4, 4
NE = G * E
FE = 256
KF = FE // P
TOPK = 2
BLOCKS = (TOPK * S + NE * (P - 1)) // P
NB = 32
LEAST = TOPK * S // P
EPS = 1e-6
NEG = -1e30
CH = 2048
ORDER = (7, 3, 6, 2, 5, 1, 4, 0)
AUG = 4
HK = HD + AUG


def trunk(nc, x, mix_norm, ffn_norm, pool_w, pool_scale, kv_norm, w_k, w_v, w_f, b_f, w_q, w_o,
          router_g, router_g_b, router_e, router_e_b, w_gate, w_up, w_down, final_norm, out):
    start = (nc.sbuf_base + 31) // 32 * 32
    REG = 32768
    R = [start, start + REG, start + 2 * REG]
    RAW0 = start + 3 * REG
    SPL0 = RAW0 + 6 * CH * 4
    SMALL0 = SPL0 + 6 * CH * 4
    small_at = [SMALL0]

    def at(name, shape, dtype, offset):
        return nc.alloc_sbuf_tensor_at(name, shape, dtype, offset=offset)

    def size(shape, dtype):
        n = 2 if dtype == BF16 else 4
        for s in shape[1:]:
            n *= s
        return (n + 31) // 32 * 32

    def small(name, shape, dtype=F32):
        t = at(name, shape, dtype, small_at[0])
        small_at[0] += size(shape, dtype)
        return t

    def pack(name_shape_dtypes, offset, limit):
        made = []
        for name, shape, dtype in name_shape_dtypes:
            made.append(at(name, shape, dtype, offset))
            offset += size(shape, dtype)
        assert offset <= limit, (name_shape_dtypes[0][0], offset - limit)
        return made

    raw = at("raw", [P, 6, CH], F32, RAW0)
    w_hi = at("w_hi", [P, 3, CH], F32R, SPL0)
    w_lo = at("w_lo", [P, 3, CH], F32R, SPL0 + 3 * CH * 4)

    ident = small("ident", [P, P])
    ones = small("ones", [P, P])
    before = small("before", [P, P])
    upto = small("upto", [P, P])
    iota_p = small("iota_p", [P, P])
    ident_bf = small("ident_bf", [P, P], BF16)
    future_bf = small("future_bf", [P, P], BF16)
    stage = small("stage", [P, 4, 512], F32R)
    sumsq = small("sumsq", [P, T])
    inv = small("inv", [P, T])
    halfneg = small("halfneg", [P, T])
    gain_kv = small("gain_kv", [P, K])
    gain_q = small("gain_q", [P, K])
    wf_raw = small("wf_raw", [P, K, HEADS])
    wf_hi = small("wf_hi", [P, K, HEADS], F32R)
    wf_lo = small("wf_lo", [P, K, HEADS], F32R)
    bf_col = small("bf_col", [P, 1])
    neg_max = small("neg_max", [P, 4])
    row_sum = small("row_sum", [P, 4])
    row_inv = small("row_inv", [P, 2])
    idx_now = small("idx_now", [P, 2], I32)
    idle = small("idle", [P, 1])
    limit = nc.sbuf_usable_end
    assert small_at[0] <= limit, small_at[0] - limit

    h0 = at("h0", [P, T, D], F32, R[0])
    h1 = at("h1", [P, T, D], F32, R[2])
    pool_x = at("pool_x", [P, T, D], F32, R[1])
    (band, band0, band_prev, dT_hi, dT_lo) = pack([
        ("band", [P, 4, P], F32), ("band0", [P, 4, P], F32), ("band_prev", [P, 4, P], F32),
        ("dT_hi", [P, K, P], F32R), ("dT_lo", [P, K, P], F32R)], SPL0 + CH * 4, SPL0 + 3 * CH * 4)
    (gain_bc0, scale_bc, idx_row) = pack([
        ("gain_bc0", [P, D], F32), ("scale_bc", [P, D], F32), ("idx_row", [P, P], F32)],
        SPL0 + 4 * CH * 4, SPL0 + 6 * CH * 4)
    wt = small("wt", [P, 2, T])
    pos_i = small("pos_i", [P, 2, T], I32)
    yg = [at(f"yg{n}", [P, 2, D], F32, SPL0 + slot * CH * 4) for n, slot in enumerate((0, 2, 3, 5))]
    moe_mem = []
    for L in range(2):
        A, B = (R[1], R[2]) if L == 0 else (R[1], R[0])
        RT = [RAW0 + slot * CH * 4 for slot in ((5, 0, 4), (5, 0, 1))[L]]
        m = {}

        def put(specs, offset, lim):
            for (name, shape, dtype), t in zip(specs, pack([(f"{n}_{L}", s, d) for n, s, d in specs], offset, lim)):
                m[name] = t
        put([("xn", [P, 2, D], F32)], RT[0], RT[0] + CH * 4)
        put([("rT", [P, D], F32), ("junk", [P, D], F32)], RT[1], RT[1] + CH * 4)
        put([("gain", [P, D], F32), ("wr", [P, K, G + NE], F32), ("br", [P, G + NE], F32)], RT[2], RT[2] + CH * 4)
        put([("lgT", [P, S], F32)], B, B + REG)
        put([("xg", [P, 2, D], F32), ("xT_hi", [P, 2, D], F32R),
             ("xT_lo", [P, 2, D], F32R)], A, A + REG)
        put([("slot_of", [P, 2 * T, P], BF16)], A, A + REG)
        put([("y", [P, 2, D], F32), ("act", [P, FE], F32),
             ("silu", [P, FE], F32), ("aT_hi", [P, FE], F32R), ("aT_lo", [P, FE], F32R),
             ("lg", [P, T, G + NE], F32),
             ("gm", [P, T], F32), ("t4", [P, T, G], F32), ("gi", [P, T], F32), ("og", [P, T, G], F32),
             ("gw", [P, T], F32), ("t16", [P, T, NE], F32), ("es", [P, T, E], F32),
             ("m1", [P, T], F32), ("m2", [P, T], F32), ("o1", [P, T, E], F32), ("o2", [P, T, E], F32),
             ("e2", [P, T], F32),
             ("s1", [P, T, NE], F32), ("s2", [P, T, NE], F32), ("sel", [P, T, NE], F32),
             ("cum", [P, T + 1, NE], F32), ("cmp", [P, NB * NE], F32), ("nb", [P, NE], F32),
             ("end", [P, NE], F32), ("base", [P, NE], F32), ("zero", [P, NE], F32), ("pf", [P, T, NE], F32),
             ("pos", [P, 2, T], F32), ("part_i", [P, 2, 2 * T], I32),
             ("part", [P, 2, 2 * T], F32), ("blk_of", [P, 2 * T, NB], F32), ("tok_of", [P, 2 * T, 2, NB], BF16),
             ("tok_i", [P, NB], I32), ("tok", [P, NB], F32), ("tab", [P, 3, NB], F32), ("tab_i", [P, 3, NB], I32), ("bit", [P, NB], F32)], B, B + REG)
        moe_mem.append(m)
    io4 = small("io4", [P, 4])
    thr = small("thr", [P, T])
    tok_part = small("tok_part", [P, T, 2])
    assert small_at[0] <= limit, small_at[0] - limit
    hT_hi = at("hT_hi", [P, K, S], F32R, R[1])
    hT_lo = at("hT_lo", [P, K, S], F32R, R[2])
    heads_mem = [pack([(f"{n}_{q}", [P, S], F32R) for n in ("q1", "q2", "k1", "k2")], at_, at_ + 2 * CH * 4)
                 for q, at_ in enumerate((RAW0 + 4 * CH * 4, R[1]))]
    val = at("val", [P, T, D], F32, R[0])
    o_tok = at("o_tok", [P, T, D], F32, R[2])
    probs = at("probs", [P, 2, S], F32, RAW0 + 2 * CH * 4)
    probsT = at("probsT", [P, 2, S], F32, RAW0 + 3 * CH * 4)
    oT_hi = at("oT_hi", [P, K, S], F32R, R[1])
    oT_lo = at("oT_lo", [P, K, S], F32R, R[0])
    xhat = at("xhat", [P, 2, D], F32, RAW0 + 2 * CH * 4)
    square = at("square", [P, D], F32, RAW0 + 3 * CH * 4)
    zf = at("zf", [P, 2, S], F32, RAW0 + 3 * CH * 4)
    fin_gain = at("fin_gain", [P, D], F32, R[1])
    fin_out = at("fin_out", [P, 4, D], F32, R[1] + 4096)
    fin_junk = at("fin_junk", [P, D], F32, R[1] + 5 * 4096)

    ps = nc.alloc_psum_tensor("ps", [P, 8, 512], F32)

    def banks(a, n=1):
        return ps[:, a:a + n, :].rearrange("p b n -> p (b n)")

    xn_d = nc.dram_tensor("xn_d", [S, D], F32)
    y_d = nc.dram_tensor("y_d", [BLOCKS * P, D], F32)
    h_d = nc.dram_tensor("h_d", [S, D], F32)
    kh_d = nc.dram_tensor("kh_d", [HEADS, HD, S], F32)
    ql_d = nc.dram_tensor("ql_d", [HEADS, HD, S], F32)
    k2_d = nc.dram_tensor("k2_d", [HEADS, HK, S], F32)
    q2_d = nc.dram_tensor("q2_d", [HEADS, HK, S], F32)

    def sem(name):
        return nc.alloc_semaphore(name=name)

    consts = sem("consts")
    x_in = [sem(f"x_in{t}") for t in range(T)]
    mix_in = sem("mix_in")
    scale_in = sem("scale_in")
    gains_in = sem("gains_in")
    loaded = [[sem(f"loaded{s}_{q}") for q in range(2)] for s in range(3)]
    hi_done = [sem(f"hi_done{s}") for s in range(3)]
    lo_done = [sem(f"lo_done{s}") for s in range(3)]
    used = [sem(f"used{s}") for s in range(3)]
    y_cleared = sem("y_cleared")
    slot_free = sem("slot_free")
    pool_w_scaled = sem("pool_w_scaled")
    sq_done = sem("sq_done")
    inv_done = sem("inv_done")
    dve_step = sem("dve_step")
    pool_step = sem("pool_step")
    act_step = sem("act_step")
    barrier = sem("barrier")
    router_in = [sem(f"router_in{L}") for L in range(2)]
    ahead = [sem(f"ahead{L}") for L in range(2)]
    poolx_done = sem("poolx_done")
    dT_ps = sem("dT_ps")
    dT_hi_done = sem("dT_hi_done")
    dT_lo_done = sem("dT_lo_done")
    py_ps = sem("py_ps")
    h_done = sem("h_done")
    xn_done = sem("xn_done")
    xn_out = [sem("xn_out0"), sem("xn_out1")]
    rT_ps = sem("rT_ps")
    rT_done = sem("rT_done")
    lgT_ps = sem("lgT_ps")
    lgT_done = sem("lgT_done")
    lg_ps = sem("lg_ps")
    soft_in = sem("soft_in")
    soft_out = sem("soft_out")
    sel_done = sem("sel_done")
    rank_ps = sem("rank_ps")
    slots_done = sem("slots_done")
    tok_ps = sem("tok_ps")
    tok_done = sem("tok_done")
    eid_done = sem("eid_done")
    idx_done = sem("idx_done")
    idle_done = sem("idle_done")
    gathered = [[sem(f"gathered{L}_{q}") for q in range(2)] for L in range(2)]
    xT_ps = sem("xT_ps")
    xT_hi_done = sem("xT_hi_done")
    xT_lo_done = sem("xT_lo_done")
    silu_done = sem("silu_done")
    act_done = sem("act_done")
    aT_ps = sem("aT_ps")
    aT_hi_done = sem("aT_hi_done")
    aT_lo_done = sem("aT_lo_done")
    y_act = sem("y_act")
    y_out = [sem("y_out0"), sem("y_out1")]
    y_back = [sem(f"y_back{q}") for q in range(4)]
    y_added = sem("y_added")
    xhat_done = sem("xhat_done")
    h_spilled = [sem(f"h_spilled{t}") for t in range(T)]
    h_back = [sem(f"h_back{t}") for t in range(T)]
    hT_ps = sem("hT_ps")
    hT_hi_done = sem("hT_hi_done")
    hT_lo_done = sem("hT_lo_done")
    wf_done = sem("wf_done")
    z_ps = sem("z_ps")
    zf_dve = sem("zf_dve")
    zf_act = sem("zf_act")
    f_hi_done = sem("f_hi_done")
    f_lo_done = sem("f_lo_done")
    f_out = sem("f_out")
    ones_out = sem("ones_out")
    v_ps = sem("v_ps")
    v_done = sem("v_done")
    kq_ps = sem("kq_ps")
    kq_hi_done = sem("kq_hi_done")
    kq_lo_done = sem("kq_lo_done")
    kq_out = [sem("kq_out0"), sem("kq_out1")]
    head_in = [sem("head_in0"), sem("head_in1")]
    qk_ps = sem("qk_ps")
    max_done = sem("max_done")
    exp_done = sem("exp_done")
    pT_ps = sem("pT_ps")
    pT_dve = sem("pT_dve")
    pT_act = sem("pT_act")
    pv_ps = sem("pv_ps")
    rinv_done = sem("rinv_done")
    o_done = sem("o_done")
    oT_ps = sem("oT_ps")
    oT_hi_done = sem("oT_hi_done")
    oT_lo_done = sem("oT_lo_done")
    op_ps = sem("op_ps")
    op_done = sem("op_done")
    fin_done = sem("fin_done")
    out_done = [sem(f"out_done{q}") for q in range(4)]

    M_MOE0 = (1, 0, 0)
    PROJ = []
    nxt = [M_MOE0[0] + BLOCKS, BLOCKS, BLOCKS]
    for i in range(16):
        s = (i + 1) % 3
        PROJ.append((s, nxt[s]))
        nxt[s] += 1
    M_MOE1 = tuple(nxt)
    M_MOE = (M_MOE0, M_MOE1)

    def raw_slot(s, par):
        return s + 3 * par

    def gu_src(L, e, s):
        return [w[L][e].rearrange("(p k) f -> p k f", k=K)[:, 4 * s:4 * s + 4, :] for w in (w_gate, w_up)]

    def load(sp, s, m, par, parts, needed=None, done=None):
        done = done or loaded[s][par]
        sp_wait(sp, lo_done[s], m, -1)
        if needed is not None:
            sp.sem_inc(slot_free, 1)
        for j, src in enumerate(parts):
            dst = raw[:, raw_slot(s, par), j * CH // 2:(j + 1) * CH // 2]
            if len(src.shape) == 3:
                dst = dst.rearrange("p (k n) -> p k n", k=src.shape[1])
            if needed is None:
                sp.dma_start(dst, src).then_inc(done, 16)
            else:
                sp.dma_start(dst, src, cond=needed).then_inc(done, 16)

    def sp_wait(eng, sm, value, plus):
        if not isinstance(value, int) or value + plus > 0:
            eng.wait_ge(sm, value + plus)

    def loaded_value(m, par):
        return 16 * (m - par) + 32

    def hi(act, s, m, par, gain=None):
        act.wait_ge(loaded[s][par], loaded_value(m, par))
        sp_wait(act, used[s], m, 0)
        src = raw[:, raw_slot(s, par), :]
        if gain is None:
            return act.activation(w_hi[:, s, :], src, ACT.Copy).then_inc(hi_done[s], 1)
        n = CH // K
        for k in range(K):
            ins = act.activation(w_hi[:, s, k * n:(k + 1) * n], src[:, k * n:(k + 1) * n], ACT.Copy,
                                 scale=gain[:, k:k + 1])
        ins.then_inc(hi_done[s], 1)

    def lo(dve, s, m, par, gain=None):
        dve.wait_ge(hi_done[s], m + 1)
        src = raw[:, raw_slot(s, par), :]
        if gain is None:
            return dve.tensor_tensor(w_lo[:, s, :], src, w_hi[:, s, :].bitcast(F32), ALU.subtract)\
                      .then_inc(lo_done[s], 1)
        n = CH // K
        for k in range(K):
            ins = dve.scalar_tensor_tensor(out=w_lo[:, s, k * n:(k + 1) * n], in0=src[:, k * n:(k + 1) * n],
                                           scalar=gain[:, k:k + 1],
                                           in1=w_hi[:, s, k * n:(k + 1) * n].bitcast(F32),
                                           op0=ALU.mult, op1=ALU.subtract)
        ins.then_inc(lo_done[s], 1)

    def three(pe, o, a_hi, a_lo, b_hi, b_lo, first, last):
        pe.matmul(o, a_hi, b_hi, start=first, stop=False)
        pe.matmul(o, a_hi, b_lo, start=False, stop=False)
        return pe.matmul(o, a_lo, b_hi, start=False, stop=last)

    n_barrier = {}

    def meet(eng, key):
        n_barrier[key] = n_barrier.get(key, 0) + 1
        eng.drain().then_inc(barrier, 1)
        eng.wait_ge(barrier, 4 * n_barrier[key])

    chain = {"dve": 0, "pool": 0, "act": 0}
    steps = {"dve": dve_step, "pool": pool_step, "act": act_step}

    def link(eng, who, ins):
        chain[who] += 1
        ins.then_inc(steps[who], 1)
        eng.wait_ge(steps[who], chain[who])

    def blocks(eng, L, body, skip, finish, skip_last):
        eng.wait_ge(eid_done, L + 1)
        live = eng.value_load(moe_mem[L]["tab_i"][0:1, 2, 0:1], min_val=LEAST, max_val=BLOCKS)
        for b in range(3):
            body(b, b % 2, b == 0, False)
        with eng.Fori(0, (BLOCKS - 5) // 2) as i:
            with eng.If(2 * i + 2 < live):
                body(2 * i + 3, 1, False, False)
                body(2 * i + 4, 0, False, False)
            with eng.Else():
                skip(2 * i + 3)
        with eng.If(live > BLOCKS - 3):
            body(BLOCKS - 2, 1, False, False)
            body(BLOCKS - 1, 0, False, True)
            finish()
        with eng.Else():
            skip_last()

    def count(eng, *counts):
        eng.drain()
        for sems, n in counts:
            for sm in sems:
                eng.sem_inc(sm, n)

    def fresh_mask(eng, L):
        eng.wait_ge(eid_done, L + 1)
        row = moe_mem[L]["tab_i"]
        low = eng.value_load(row[0:1, 2, 1:2], min_val=0, max_val=2 ** 16 - 1)
        high = eng.value_load(row[0:1, 2, 2:3], min_val=0, max_val=2 ** 15 - 1)
        return low + high * 2 ** 16

    def is_fresh(mask, b):
        return (mask >> b) & 1

    def bc(ap, shape):
        return ap.to_broadcast(shape)

    block = nc.Block()
    block.__enter__()

    def load_head(sp, hd, par):
        q1, q2, k1, k2 = heads_mem[par]
        for dst, src in ((q1[0:HD, :], q2_d[bass.ds(hd, 1), 0:HD, :]),
                         (q1[HD:P, :], ql_d[bass.ds(hd, 1), :, :]),
                         (k1[0:HD, :], kh_d[bass.ds(hd, 1), :, :]),
                         (k1[HD:P, :], kh_d[bass.ds(hd, 1), :, :]),
                         (q2[0:HK, :], q2_d[bass.ds(hd, 1), :, :]),
                         (k2[0:HK, :], k2_d[bass.ds(hd, 1), :, :])):
            sp.dma_start(dst.bitcast(F32), src.rearrange("h d n -> (h d) n")).then_inc(head_in[par], 16)

    def load_expert(sp, L, e, b, par, needed=None, done=None):
        base = M_MOE[L]
        for s in range(2):
            ws = [w[L][bass.ds(e, 1)].rearrange("e (p k) f -> p (e k) f", k=K)[:, 4 * s:4 * s + 4, :]
                  for w in (w_gate, w_up)]
            load(sp, s, base[s] + b, (base[s] + par) % 2, ws, needed, done)
        wd = w_down[L][bass.ds(e, 1)].rearrange("e (p k) n -> p (e k) n", k=KF)
        load(sp, 2, base[2] + b, (base[2] + par) % 2, [wd[:, 0, :], wd[:, 1, :]], needed, done)

    def sp_moe(sp, L):
        m = moe_mem[L]
        base = M_MOE[L]
        for t in range(T):
            sp.wait_ge(xn_done, T * L + t + 1)
            sp.dma_start(xn_d[t * P:(t + 1) * P, :], m["xn"][:, t % 2, :]).then_inc(xn_out[t % 2], 16)
        sp.wait_ge(ahead[L], 96)
        for q in range(2):
            sp.wait_ge(xn_out[q], 64 * (L + 1))
        sp.wait_ge(eid_done, L + 1)

        def table(row, b):
            return sp.value_load(m["tab_i"][0:1, row, bass.ds(b, 1)], min_val=0, max_val=NE - 1)

        def load_block(b, par):
            load_expert(sp, L, table(0, b), b, par, table(1, b))

        def store_y(b, par):
            sp.wait_ge(y_act, L * BLOCKS + b + 1)
            sp.dma_start(y_d[bass.ds(b * P, P), :], m["y"][:, par, :]).then_inc(y_out[par], 16)

        def body(b, par, first, last):
            if not isinstance(b, int) or b + 2 < BLOCKS:
                load_block(b + 2, par)
            if not first:
                store_y(b - 1, 1 - par)

        def skip(b):
            for by_parity in loaded:
                for q in range(2):
                    sp.sem_inc(by_parity[q], 32)
            for q in range(2):
                sp.sem_inc(y_out[q], 16)

        def skip_last():
            sp.sem_inc(y_out[0], 32)
            sp.sem_inc(y_out[1], 16)

        load_block(0, 0)
        load_block(1, 1)
        sp.wait_ge(y_cleared, 16)
        blocks(sp, L, body, skip, lambda: store_y(BLOCKS - 1, 0), skip_last)

    def proj_load(sp, i):
        w = (w_v, w_k, w_q[0], w_o[0])[i // 4]
        s, m = PROJ[i]
        c = i % 4
        src = w.rearrange("(p k) n -> p k n", k=K)[:, :, c * 256:(c + 1) * 256]
        load(sp, s, m, m % 2, [src[:, 0:4, :], src[:, 4:8, :]])

    @block.sync
    def _(sp):
        for t in range(T):
            sp.dma_start(h0[:, t, :], x[0, t * P:(t + 1) * P, :]).then_inc(x_in[t], 16)
            if t == 0:
                sp.dma_start(gain_bc0[:, :], mix_norm[0:1, :].partition_broadcast(P)).then_inc(mix_in, 16)
            if t == 2:
                pw = pool_w[0].rearrange("g (c p) d -> p g c d", p=P)
                for j in range(2):
                    dst = raw[:, 0, j * CH // 2:(j + 1) * CH // 2].rearrange("p (g c d) -> p g c d", g=2, c=2)
                    sp.dma_start(dst, pw[:, 2 * j:2 * j + 2, :, :]).then_inc(loaded[0][0], 16)
        sp.dma_start(gain_kv[:, :], kv_norm.rearrange("(p k) -> p k", k=K)).then_inc(gains_in, 16)
        sp.dma_start(gain_q[:, :], mix_norm[1].rearrange("(p k) -> p k", k=K)).then_inc(gains_in, 16)
        sp.dma_start(wf_raw[:, :, :], w_f.rearrange("(p k) n -> p k n", k=K)).then_inc(gains_in, 16)
        sp.dma_start(bf_col[0:HEADS, :], b_f.unsqueeze(1)).then_inc(gains_in, 16)
        for L in range(2):
            m = moe_mem[L]
            if L == 1:
                sp.wait_ge(lo_done[PROJ[15][0]], PROJ[15][1] + 1)
            for dst, src in ((m["gain"][:, :], ffn_norm[L:L + 1, :].partition_broadcast(P)),
                             (m["wr"][:, :, 0:G], router_g[L].rearrange("(p k) n -> p k n", k=K)),
                             (m["wr"][:, :, G:G + NE], router_e[L].rearrange("(p k) n -> p k n", k=K)),
                             (m["br"][:, 0:G], router_g_b[L:L + 1, :].partition_broadcast(P)),
                             (m["br"][:, G:G + NE], router_e_b[L:L + 1, :].partition_broadcast(P))):
                sp.dma_start(dst, src).then_inc(router_in[L], 16)
            load_expert(sp, L, 0, 0, 0, done=ahead[L])
            if L == 0:
                sp.wait_ge(consts, 1)
                sp.dma_start(y_d[LEAST * P:, :].rearrange("(p b) (c n) -> p (b c) n", p=P, n=P),
                             bc(ones[:, :].unsqueeze(1), [P, (BLOCKS - LEAST) * D // P, P])).then_inc(y_cleared, 16)
            sp_moe(sp, L)
            if L == 1:
                break
            proj_load(sp, 0)
            for t in range(T):
                sp.wait_ge(y_added, t + 1)
                sp.dma_start(h_d[t * P:(t + 1) * P, :], h0[:, t, :]).then_inc(h_spilled[t], 16)
                if t in (3, 5, 7):
                    proj_load(sp, (t - 1) // 2)
            for d, row in ((q2_d, HD), (q2_d, HD + 1), (k2_d, HD + 2), (k2_d, HD + 3)):
                sp.dma_start(d[:, row, :].rearrange("h (c n) -> h c n", n=P),
                             ones[0:HEADS, :].unsqueeze(1).to_broadcast([HEADS, S // P, P]))\
                  .then_inc(ones_out, 16)
            sp.wait_ge(hT_ps, T)
            proj_load(sp, 4)
            for half in range(2):
                cols = slice(512 * half, 512 * half + 512)
                sp.wait_ge(f_lo_done, half + 1)
                for row, j, d in ((66, 0, q2_d), (67, 1, q2_d), (64, 2, k2_d), (65, 3, k2_d)):
                    sp.dma_start(d[:, row, cols], stage[0:HEADS, j, :].bitcast(F32)).then_inc(f_out, 16)
            for i in range(5, 7):
                proj_load(sp, i)
            for c in range(8):
                proj_load(sp, 7 + c)
                for u in range(4):
                    n = 4 * c + u
                    i, par = n // 2 % 8, n % 2
                    half = n % 2
                    cols = slice(512 * half, 512 * half + 512)
                    sp.wait_ge(kq_lo_done, n + 1)
                    full, aug = (kh_d, k2_d) if n < 16 else (ql_d, q2_d)
                    jf, ja = (0, 1) if n < 16 else (1, 0)
                    sp.dma_start(full[2 * i:2 * i + 2, :, cols].rearrange("h d n -> (h d) n"),
                                 stage[:, 2 * par + jf, :].bitcast(F32)).then_inc(kq_out[par], 16)
                    for z in range(2):
                        sp.dma_start(aug[2 * i + z, 0:HD, cols],
                                     stage[HD * z:HD * z + HD, 2 * par + ja, :].bitcast(F32)).then_inc(kq_out[par], 16)
                if c == 6:
                    for q in range(2):
                        sp.wait_ge(kq_out[q], 48 * 14)
                    sp.wait_ge(f_out, 128)
                    sp.wait_ge(ones_out, 64)
                    sp.wait_ge(lo_done[PROJ[13][0]], PROJ[13][1] + 1)
                    load_head(sp, 0, 0)
            proj_load(sp, 15)
            for q in range(2):
                sp.wait_ge(kq_out[q], 48 * 16)
            sp.wait_ge(barrier, 4 * 1)

            load_head(sp, 1, 1)
            with sp.Fori(0, HEADS // 2 - 1) as p:
                hd = 2 * p
                sp.wait_ge(qk_ps, hd * T + T)
                load_head(sp, hd + 2, 0)
                sp.wait_ge(qk_ps, hd * T + 2 * T)
                load_head(sp, hd + 3, 1)
            for t in range(T):
                sp.wait_ge(oT_ps, t + 1)
                sp.dma_start(h1[:, t, :], h_d[t * P:(t + 1) * P, :]).then_inc(h_back[t], 16)
        sp.wait_ge(used[1], M_MOE1[1] + BLOCKS)
        sp.dma_start(fin_gain[:, :], final_norm.unsqueeze(0).partition_broadcast(P)).then_inc(gains_in, 16)
        for t in range(T):
            sp.wait_ge(fin_done, t + 1)
            sp.dma_start(out[0, t * P:(t + 1) * P, :], fin_out[:, t % 4, :]).then_inc(out_done[t % 4], 16)
        for q in range(4):
            sp.wait_ge(out_done[q], 16 * T // 4)
        for s in range(3):
            chunks = M_MOE1[s] + BLOCKS
            for q in range(2):
                sp.wait_ge(loaded[s][q], 32 * ((chunks + 1 - q) // 2))

    n_inv = [0]

    def rsqrt_tile(pool, t):
        n_inv[0] += 1
        pool.wait_ge(sq_done, n_inv[0])
        link(pool, "pool", pool.tensor_scalar(sumsq[:, t:t + 1], sumsq[:, t:t + 1], 1.0 / D, EPS, ALU.mult, ALU.add))
        pool.tensor_tensor(inv[:, t:t + 1], sumsq[:, t:t + 1], halfneg[:, t:t + 1], ALU.pow).then_inc(inv_done, 1)

    def pool_moe(pool, L):
        m = moe_mem[L]
        pool.wait_ge(tok_done, L + 1)
        for q in range(2):
            pool.wait_ge(xn_out[q], 64 * (L + 1))

        def gather(b, par):
            if not isinstance(b, int) or b >= 2:
                pool.wait_ge(xT_ps, L * BLOCKS + b - 1)
            sp_wait(pool, idle_done, L * BLOCKS + b, 0)
            pool.tensor_copy(idx_now[:, par:par + 1], m["tok_i"][:, bass.ds(b, 1)]).then_inc(idx_done, 1)
            pool.wait_ge(idx_done, L * BLOCKS + b + 1)
            pool.tensor_tensor(idle[:, :], halfneg[:, 0:1], halfneg[:, 0:1], ALU.add).then_inc(idle_done, 1)
            pool.indirect_dma_start(
                out=m["xg"][:, par, :], out_offset=None, in_=xn_d[:, :],
                in_offset=bass.IndirectOffsetOnAxis(ap=idx_now[:, par:par + 1].bitcast(U32), axis=0),
            ).then_inc(gathered[L][par], 16)

        def body(b, par, first, last):
            if not last:
                gather(b + 1, 1 - par)

        gather(0, 0)
        blocks(pool, L, body, lambda b: count(pool, ((idx_done, idle_done), 2)), lambda: None,
               lambda: count(pool, ((idx_done, idle_done), 1)))
        pool.wait_ge(y_out[0], 16 * 16 * (L + 1))
        pool.wait_ge(y_out[1], 16 * 15 * (L + 1))

        def gather_y(t):
            if t >= 4:
                pool.wait_ge(y_added, T * L + t - 3)
            for j in range(2):
                pool.indirect_dma_start(
                    out=yg[t % 4][:, j, :], out_offset=None, in_=y_d[:, :],
                    in_offset=bass.IndirectOffsetOnAxis(ap=pos_i[:, j, t:t + 1].bitcast(U32), axis=0),
                ).then_inc(y_back[t % 4], 16)

        for t in range(4):
            gather_y(t)
        for t in range(T):
            if t + 4 < T:
                gather_y(t + 4)
            rsqrt_tile(pool, t)

    @block.gpsimd
    def _(pool):
        pool.memset(halfneg[:, :], -0.5)
        pool.memset(ones[:, :], 1.0)
        pool.memset(ident[:, :], 0.0)
        pool.memset(before[:, :], 1.0)
        pool.memset(upto[:, :], 1.0)
        pool.memset(future_bf[:, :], 0.0)
        for g, w in enumerate(WINDOWS):
            pool.memset(band[:, g, :], 1.0)
            pool.memset(band_prev[:, g, :], 1.0 / w)
        pool.iota(iota_p[:, :], [[1, P]], base=0, channel_multiplier=0, allow_small_or_imprecise_dtypes=True)
        pool.iota(idx_row[:, :], [[1, P]], base=1, channel_multiplier=0, allow_small_or_imprecise_dtypes=True)
        pool.iota(io4[:, :], [[1, 4]], base=-8, channel_multiplier=0, allow_small_or_imprecise_dtypes=True)
        pool.iota(thr[:, :], [[P, T]], base=0, channel_multiplier=0, allow_small_or_imprecise_dtypes=True)
        pool.iota(tok_part[:, :, 0], [[P, T]], base=0, channel_multiplier=0, allow_small_or_imprecise_dtypes=True)
        link(pool, "pool", pool.iota(tok_part[:, :, 1], [[0, T]], base=0, channel_multiplier=1,
                                     allow_small_or_imprecise_dtypes=True))
        row = [[1, P]]
        pool.affine_select(out=ident[:, :], in_=ident[:, :], compare_op=ALU.not_equal, fill=1.0, base=0,
                           pattern=[[-1, P]], channel_multiplier=1)
        pool.affine_select(out=before[:, :], in_=before[:, :], compare_op=ALU.is_gt, fill=0.0, base=0,
                           pattern=row, channel_multiplier=-1)
        pool.affine_select(out=upto[:, :], in_=upto[:, :], compare_op=ALU.is_ge, fill=0.0, base=0,
                           pattern=row, channel_multiplier=-1)
        pool.affine_select(out=future_bf[:, :], in_=future_bf[:, :], compare_op=ALU.is_ge, fill=NEG, base=0,
                           pattern=[[-1, P]], channel_multiplier=1)
        for g, w in enumerate(WINDOWS):
            pool.affine_select(out=band_prev[:, g, :], in_=band_prev[:, g, :], compare_op=ALU.is_ge, fill=0.0,
                               base=w - 1 - P, pattern=[[-1, P]], channel_multiplier=1)
            link(pool, "pool", pool.affine_select(out=band[:, g, :], in_=band[:, g, :], compare_op=ALU.is_ge,
                                                  fill=0.0, base=0, pattern=row, channel_multiplier=-1))
            last = pool.affine_select(out=band[:, g, :], in_=band[:, g, :], compare_op=ALU.is_ge, fill=0.0,
                                      base=w - 1, pattern=[[-1, P]], channel_multiplier=1)
        last.then_inc(consts, 1)
        for t in range(2 * T):
            rsqrt_tile(pool, t % T)
        pool_moe(pool, 0)
        meet(pool, "pool")
        meet(pool, "pool")
        for t in range(T):
            rsqrt_tile(pool, t)
        pool_moe(pool, 1)

    def act_moe(act, L):
        m = moe_mem[L]
        base = M_MOE[L]
        N = L * BLOCKS
        h = (h0, h1)[L]
        act.wait_ge(lgT_ps, T * (L + 1))
        act.activation(m["lgT"][0:G + NE, :], banks(6, 2)[0:G + NE, :], ACT.Copy).then_inc(lgT_done, 1)
        for j in range(2):
            act.wait_ge(soft_in, 2 * L + j + 1)
            if j == 0:
                act.activation(m["t4"][:, :, :], m["t4"][:, :, :], ACT.Exp).then_inc(soft_out, 1)
            else:
                act.activation(m["e2"][:, :], m["e2"][:, :], ACT.Exp).then_inc(soft_out, 1)

        def xT_hi_(b, par):
            act.wait_ge(xT_ps, N + b + 1)
            if not isinstance(b, int) or b >= 2:
                act.wait_ge(used[1], base[1] + b - 1)
            act.activation(m["xT_hi"][:, par, :], banks(2, 2), ACT.Copy).then_inc(xT_hi_done, 1)

        def aT_hi_(b):
            act.wait_ge(aT_ps, N + b + 1)
            sp_wait(act, used[2], base[2] + b, 0)
            act.activation(m["aT_hi"][:, :], ps[:, 4, 0:FE], ACT.Copy).then_inc(aT_hi_done, 1)

        def y_copy(b, par):
            act.wait_ge(used[2], base[2] + b + 1)
            if not isinstance(b, int) or b >= 2:
                act.wait_ge(y_out[par], y_count(L, b, par))
            act.activation(m["y"][:, par, :], banks(5, 2), ACT.Copy).then_inc(y_act, 1)

        mask = fresh_mask(act, L)

        def body(b, par, first, last):
            def middle():
                act.wait_ge(used[1], base[1] + b + 1)
                if not first:
                    act.wait_ge(act_done, N + b)
                act.activation(m["silu"][:, :], ps[:, par, 0:FE], ACT.Silu).then_inc(silu_done, 1)

            if not first:
                aT_hi_(b - 1)
            if last:
                middle()
            else:
                xT_hi_(b + 1, 1 - par)
                with act.If(is_fresh(mask, b + 1)):
                    hi(act, 0, base[0] + b + 1, (base[0] + 1 - par) % 2)
                    middle()
                    hi(act, 1, base[1] + b + 1, (base[1] + 1 - par) % 2)
                with act.Else():
                    count(act, (hi_done[0:1], 1))
                    middle()
                    count(act, (hi_done[1:2], 1))
            with act.If(is_fresh(mask, b)):
                hi(act, 2, base[2] + b, (base[2] + par) % 2)
            with act.Else():
                count(act, (hi_done[2:3], 1))
            if not first:
                y_copy(b - 1, 1 - par)

        def finish():
            aT_hi_(BLOCKS - 1)
            y_copy(BLOCKS - 1, 0)

        def skip(b):
            count(act, ((aT_hi_done, xT_hi_done, *hi_done, silu_done, y_act), 2))

        def skip_last():
            count(act, ((xT_hi_done, *hi_done[0:2]), 1), ((hi_done[2], silu_done), 2), ((aT_hi_done, y_act), 3))

        hi(act, 0, base[0], base[0] % 2)
        hi(act, 1, base[1], base[1] % 2)
        xT_hi_(0, 0)
        blocks(act, L, body, skip, finish, skip_last)

    def y_count(L, b, par):
        per = (16, 15)[par] * 16 * L
        return per + 8 * (b - par)

    def router_square(act, L, t):
        if L == 0:
            act.wait_ge(h_done, t + 1)
        else:
            act.wait_ge(op_done, 3 * T + t + 1)
        act.wait_ge(sq_done, T * (1 + 2 * L) + t)
        act.activation(moe_mem[L]["junk"][:, :], (h0, h1)[L][:, t, :], ACT.Square, accum_out=sumsq[:, t:t + 1])\
           .then_inc(sq_done, 1)

    def router_T(act, L, t):
        act.wait_ge(rT_ps, T * L + t + 1)
        sp_wait(act, lgT_ps, T * L + t, 0)
        act.activation(moe_mem[L]["rT"][:, :], banks(2, 2), ACT.Copy).then_inc(rT_done, 1)

    @block.scalar
    def _(act):
        act.dma_start(scale_bc[:, :], pool_scale[0:1, :].partition_broadcast(P)).then_inc(scale_in, 16)
        for t in range(T):
            act.wait_ge(x_in[t], 16)
            act.activation(pool_x[:, t, :], h0[:, t, :], ACT.Square, accum_out=sumsq[:, t:t + 1]).then_inc(sq_done, 1)
        act.wait_ge(pool_w_scaled, 1)
        act.activation(w_hi[:, 0, :], raw[:, 0, :], ACT.Copy).then_inc(hi_done[0], 1)
        for t in range(T):
            act.wait_ge(dT_ps, t + 1)
            if t >= 1:
                act.wait_ge(py_ps, t)
            act.activation(dT_hi[:, :, :].rearrange("p k n -> p (k n)"), banks(0, 2), ACT.Copy)\
               .then_inc(dT_hi_done, 1)
            if t >= 1:
                router_square(act, 0, t - 1)
            if t >= 2:
                router_T(act, 0, t - 2)
        router_square(act, 0, T - 1)
        router_T(act, 0, T - 2)
        router_T(act, 0, T - 1)
        act_moe(act, 0)
        hi(act, *PROJ[0], PROJ[0][1] % 2, gain_kv)
        for t in range(T + 2):
            if t < T:
                act.wait_ge(y_added, t + 1)
                if t:
                    act.wait_ge(sq_done, 2 * T + t)
                act.activation(square[:, :], h0[:, t, :], ACT.Square, accum_out=sumsq[:, t:t + 1])\
                   .then_inc(sq_done, 1)
            if 1 <= t <= T:
                if t >= 3:
                    act.wait_ge(hT_ps, t - 2)
                act.wait_ge(inv_done, 2 * T + t)
                act.activation(xhat[:, (t - 1) % 2, :], h0[:, t - 1, :], ACT.Copy, scale=inv[:, t - 1:t])\
                   .then_inc(xhat_done, 1)
            if t >= 2:
                act.wait_ge(hT_ps, t - 1)
                act.activation(hT_hi[:, :, (t - 2) * P:(t - 1) * P],
                               banks(2 * (t % 2), 2).rearrange("p (k n) -> p k n", k=K), ACT.Copy)\
                   .then_inc(hT_hi_done, 1)

        def v_copy(c, t):
            n = T * c + t
            act.wait_ge(v_ps, n + 1)
            if c == 0:
                act.wait_ge(h_spilled[t], 16)
                act.wait_ge(xhat_done, t + 1)
            act.activation(val[:, t, c * 256:(c + 1) * 256], ps[:, 4 + n % 4, 0:256], ACT.Copy).then_inc(v_done, 1)

        for t in range(4):
            v_copy(0, t)
        act.wait_ge(y_added, T)
        hi(act, *PROJ[1], PROJ[1][1] % 2, gain_kv)
        for t in range(4, T):
            v_copy(0, t)
        act.wait_ge(gains_in, 16 * 4)
        for k in range(K):
            act.activation(wf_hi[:, k, :], wf_raw[:, k, :], ACT.Copy, scale=gain_kv[:, k:k + 1]).then_inc(wf_done, 1)
        hi(act, *PROJ[2], PROJ[2][1] % 2, gain_kv)
        hi(act, *PROJ[3], PROJ[3][1] % 2, gain_kv)
        act.wait_ge(zf_dve, 1)
        act.activation(zf[0:HEADS, 1, :], zf[0:HEADS, 1, :], ACT.Exp, scale=-1.0).then_inc(zf_act, 1)
        act.wait_ge(zf_act, 1)
        act.activation(zf[0:HEADS, 1, :], zf[0:HEADS, 1, :], ACT.Ln, bias=1.0).then_inc(zf_act, 1)
        for t in range(T):
            v_copy(1, t)
        hi(act, *PROJ[4], PROJ[4][1] % 2, gain_kv)
        for half in range(2):
            act.wait_ge(zf_dve, 2)
            if half:
                act.wait_ge(f_out, 64)
                act.wait_ge(f_lo_done, 1)
            act.activation(stage[0:HEADS, 0, :], zf[0:HEADS, 0, 512 * half:512 * half + 512], ACT.Copy)\
               .then_inc(f_hi_done, 1)
        for c in range(2, 4):
            for t in range(T):
                v_copy(c, t)
            hi(act, *PROJ[c + 3], PROJ[c + 3][1] % 2, gain_kv)
        hi_next = 7
        for n in range(32):
            act.wait_ge(kq_ps, n + 1)
            if n >= 2:
                act.wait_ge(kq_out[n % 2], 48 * (n // 2))
            elif n == 0:
                act.wait_ge(f_out, 128)
            scale = 1.0 if n < 16 else HD ** -0.5
            act.activation(stage[:, 2 * (n % 2), :], ps[:, n % 4, :], ACT.Copy, scale=scale).then_inc(kq_hi_done, 1)
            if n % 4 == 3 and hi_next < 15:
                g = gain_kv if hi_next < 8 else gain_q if hi_next < 12 else None
                hi(act, *PROJ[hi_next], PROJ[hi_next][1] % 2, g)
                hi_next += 1
        meet(act, "act")

        def exp_(hd, i):
            u, q = i % 2, i % 4
            act.wait_ge(max_done, hd * T + i + 1)
            if not isinstance(hd, int) or hd * T + i >= 2:
                act.wait_ge(pT_ps, hd * T + i - 1)
            if not isinstance(hd, int) or hd * T + i >= 4:
                act.wait_ge(rinv_done, hd * T + i - 3)
            n = (ORDER[i] + 1) * P
            act.activation(probs[:, u, 0:n], banks(2 * u, 2)[:, 0:n], ACT.Exp, bias=neg_max[:, q:q + 1],
                           accum_out=row_sum[:, q:q + 1]).then_inc(exp_done, 1)

        def pT_late(hd, i):
            if ORDER[i] >= 4:
                act.wait_ge(pT_ps, hd * T + i + 1)
                sp_wait(act, pv_ps, hd * T + i, -1)
                n = (ORDER[i] - 3) * P
                act.activation(probsT[:, i % 2, 512:512 + n], ps[:, 5, 0:n], ACT.Copy).then_inc(pT_act, 1)

        def pair(hd, last):
            for j in range(2):
                for i in range(T):
                    if i < T - 1:
                        exp_(hd + j, i + 1)
                    elif not (last and j == 1):
                        exp_(hd + j + 1, 0)
                    pT_late(hd + j, i)

        act.wait_ge(lo_done[0], 36)
        act.wait_ge(lo_done[2], 35)
        exp_(0, 0)
        pair(0, False)
        with act.Fori(1, HEADS // 2 - 1) as p:
            pair(2 * p, False)
        pair(HEADS - 2, True)
        meet(act, "act")
        for t in range(T):
            act.wait_ge(oT_ps, t + 1)
            act.activation(oT_hi[:, :, t * P:(t + 1) * P], banks(2 * (t % 2), 2).rearrange("p (k n) -> p k n", k=K),
                           ACT.Copy).then_inc(oT_hi_done, 1)
        hi(act, *PROJ[15], PROJ[15][1] % 2)
        for t in range(T):
            router_square(act, 1, t)
            if t >= 1:
                router_T(act, 1, t - 1)
        router_T(act, 1, T - 1)
        act_moe(act, 1)
        for t in range(T):
            act.wait_ge(y_added, T + t + 1)
            if t:
                act.wait_ge(sq_done, 4 * T + t)
            act.activation(fin_junk[:, :], h1[:, t, :], ACT.Square, accum_out=sumsq[:, t:t + 1]).then_inc(sq_done, 1)

    def router_norm(dve, L, t):
        m = moe_mem[L]
        if t == 0:
            dve.wait_ge(router_in[L], 16 * 5)
        dve.wait_ge(inv_done, T * (1 + 2 * L) + t + 1)
        if t >= 2:
            dve.wait_ge(xn_out[t % 2], 64 * L + 16 * (t // 2))
            dve.wait_ge(rT_ps, T * L + t - 1)
        dve.scalar_tensor_tensor(out=m["xn"][:, t % 2, :], in0=(h0, h1)[L][:, t, :], scalar=inv[:, t:t + 1],
                                 in1=m["gain"][:, :], op0=ALU.mult, op1=ALU.mult).then_inc(xn_done, 1)

    def dve_moe(dve, L, follow):
        m = moe_mem[L]
        base = M_MOE[L]
        N = L * BLOCKS
        h = (h0, h1)[L]
        def do(ins):
            link(dve, "dve", ins)

        dve.wait_ge(lg_ps, L + 1)
        do(dve.memset(m["zero"][:, :], 0.0))
        for n in range(NB // 2):
            ins = dve.memset(m["bit"][:, n:NB:NB // 2], 2.0 ** n)
        do(ins)
        do(dve.memset(m["cum"][:, 0, :], 0.0))
        lg, gl = m["lg"], m["lg"][:, :, 0:G]
        el = m["lg"][:, :, G:G + NE].rearrange("p t (g e) -> p t g e", g=G)
        do(dve.tensor_tensor(lg[:, :, :], ps[:, 5, 0:T * (G + NE)].rearrange("p (t n) -> p t n", t=T),
                             bc(m["br"][:, :].unsqueeze(1), [P, T, G + NE]), ALU.add))

        def first_max(values, top, index, one_hot):
            do(dve.tensor_reduce(top[:, :], values, AX.X, ALU.max))
            do(dve.tensor_tensor(one_hot, values, bc(top[:, :].unsqueeze(2), [P, T, 4]), ALU.is_ge))
            do(dve.tensor_tensor(one_hot, one_hot, bc(io4[:, :].unsqueeze(1), [P, T, 4]), ALU.mult))
            do(dve.tensor_reduce(index[:, :], one_hot, AX.X, ALU.min))
            do(dve.tensor_tensor(one_hot, bc(io4[:, :].unsqueeze(1), [P, T, 4]),
                                 bc(index[:, :].unsqueeze(2), [P, T, 4]), ALU.is_equal))

        first_max(gl, m["gm"], m["gi"], m["og"][:, :, :])
        do(dve.tensor_tensor(m["t4"][:, :, :], gl, bc(m["gm"][:, :].unsqueeze(2), [P, T, G]), ALU.subtract))
        dve.sem_inc(soft_in, 1)
        t16 = m["t16"][:, :, :].rearrange("p t (g e) -> p t g e", g=G)
        do(dve.tensor_tensor(t16, el, bc(m["og"][:, :, :].unsqueeze(3), [P, T, G, E]), ALU.mult))
        do(dve.tensor_reduce(m["es"][:, :, :], m["t16"][:, :, :].rearrange("p t (g e) -> p t e g", g=G), AX.X, ALU.add))
        first_max(m["es"][:, :, :], m["m1"], m["gi"], m["o1"][:, :, :])
        do(dve.scalar_tensor_tensor(out=m["es"][:, :, :], in0=m["o1"][:, :, :], scalar=3 * NEG, in1=m["es"][:, :, :],
                                    op0=ALU.mult, op1=ALU.add))
        first_max(m["es"][:, :, :], m["m2"], m["gi"], m["o2"][:, :, :])
        do(dve.tensor_tensor(m["e2"][:, :], m["m2"][:, :], m["m1"][:, :], ALU.subtract))
        dve.sem_inc(soft_in, 1)
        for s_, o_ in (("s1", "o1"), ("s2", "o2")):
            do(dve.tensor_tensor(m[s_][:, :, :].rearrange("p t (g e) -> p t g e", g=G),
                                 bc(m["og"][:, :, :].unsqueeze(3), [P, T, G, E]),
                                 bc(m[o_][:, :, :].unsqueeze(2), [P, T, G, E]), ALU.mult))
        do(dve.tensor_tensor(m["sel"][:, :, :], m["s1"][:, :, :], m["s2"][:, :, :], ALU.add))
        for t in range(T):
            do(dve.tensor_tensor(m["cum"][:, t + 1, :], m["cum"][:, t, :], m["sel"][:, t, :], ALU.add))
        dve.sem_inc(sel_done, 1)
        dve.wait_ge(rank_ps, L + 1)
        cmp_ = m["cmp"][:, 0:NE * T].rearrange("p (e t) -> p e t", e=NE)
        do(dve.tensor_tensor(cmp_, bc(ps[:, 6, P:P + NE].unsqueeze(2), [P, NE, T]),
                             bc(thr[:, :].unsqueeze(1), [P, NE, T]), ALU.is_gt))
        do(dve.tensor_reduce(m["nb"][:, :], cmp_, AX.X, ALU.add))
        do(dve.tensor_tensor_scan(m["end"][:, :], m["nb"][:, :], m["zero"][:, :], 0.0, ALU.add, ALU.add))
        do(dve.tensor_tensor(m["base"][:, :], m["end"][:, :], m["nb"][:, :], ALU.subtract))
        cmp2 = m["cmp"][:, :].rearrange("p (b e) -> p b e", e=NE)
        do(dve.tensor_tensor(cmp2, bc(iota_p[:, 0:NB].unsqueeze(2), [P, NB, NE]),
                             bc(m["end"][:, :].unsqueeze(1), [P, NB, NE]), ALU.is_ge))
        do(dve.tensor_reduce(m["tab"][:, 1, :], cmp2, AX.X, ALU.add))
        do(dve.tensor_scalar(m["tab"][:, 0, :], m["tab"][:, 1, :], float(NE - 1), None, ALU.min))
        do(dve.tensor_tensor(m["tab"][:, 1, 1:NB], m["tab"][:, 0, 1:NB], m["tab"][:, 0, 0:NB - 1], ALU.not_equal))
        do(dve.memset(m["tab"][:, 1, 0:1], 1.0))
        do(dve.tensor_copy(m["tab"][:, 2, :], bc(m["end"][:, NE - 1:NE], [P, NB])))
        do(dve.tensor_tensor(m["bit"][:, :], m["bit"][:, :], m["tab"][:, 1, :], ALU.mult))
        do(dve.tensor_reduce(m["tab"][:, 2, 1:3], m["bit"][:, :].rearrange("p (h n) -> p h n", h=2), AX.X, ALU.add))
        do(dve.tensor_scalar(m["tab"][:, 1, 0:1], m["tab"][:, 0, 0:1], 0.0, None, ALU.not_equal))
        dve.tensor_copy(m["tab_i"][:, :, :], m["tab"][:, :, :]).then_inc(eid_done, 1)
        do(dve.scalar_tensor_tensor(out=m["pf"][:, :, :], in0=bc(m["base"][:, :].unsqueeze(1), [P, T, NE]),
                                    scalar=float(P), in1=ps[:, 6, 0:P].rearrange("p (t e) -> p t e", t=T),
                                    op0=ALU.mult, op1=ALU.add))
        for j, s_ in enumerate(("s1", "s2")):
            do(dve.tensor_tensor(m["t16"][:, :, :], m["pf"][:, :, :], m[s_][:, :, :], ALU.mult))
            do(dve.tensor_reduce(m["pos"][:, j, :], m["t16"][:, :, :], AX.X, ALU.add))
        do(dve.tensor_copy(pos_i[:, :, :], m["pos"][:, :, :]))
        flat_i = pos_i[:, :, :].rearrange("p j t -> p (j t)")
        do(dve.tensor_scalar(m["part_i"][:, 0, :], flat_i, P - 1, None, ALU.bitwise_and))
        do(dve.tensor_scalar(m["part_i"][:, 1, :], flat_i, 7, None, ALU.arith_shift_right))
        do(dve.tensor_copy(m["part"][:, :, :], m["part_i"][:, :, :]))
        do(dve.tensor_tensor(m["slot_of"][:, :, :], bc(iota_p[:, :].unsqueeze(1), [P, 2 * T, P]),
                             bc(m["part"][:, 0, :].unsqueeze(2), [P, 2 * T, P]), ALU.is_equal))
        do(dve.tensor_tensor(m["blk_of"][:, :, :], bc(iota_p[:, 0:NB].unsqueeze(1), [P, 2 * T, NB]),
                             bc(m["part"][:, 1, :].unsqueeze(2), [P, 2 * T, NB]), ALU.is_equal))
        for j in range(2):
            ins = dve.tensor_tensor(m["tok_of"][:, j * T:(j + 1) * T, :, :],
                                    bc(m["blk_of"][:, j * T:(j + 1) * T, :].unsqueeze(2), [P, T, 2, NB]),
                                    bc(tok_part[:, :, :].unsqueeze(3), [P, T, 2, NB]), ALU.mult)
            ins.then_inc(slots_done, 1)
        dve.wait_ge(tok_ps, L + 1)
        do(dve.tensor_copy(m["tok"][:, :], ps[:, 6, 256:256 + NB]))
        dve.tensor_tensor(m["tok_i"][:, :], m["tok"][:, :], ps[:, 6, 256 + NB:256 + 2 * NB], ALU.add)\
           .then_inc(tok_done, 1)

        def combine_weights():
            dve.wait_ge(soft_out, 2 * L + 1)
            do(dve.tensor_reduce(m["gw"][:, :], m["t4"][:, :, :], AX.X, ALU.add))
            do(dve.reciprocal(m["gw"][:, :], m["gw"][:, :]))
            dve.wait_ge(soft_out, 2 * L + 2)
            do(dve.tensor_scalar(m["m1"][:, :], m["e2"][:, :], 1.0, None, ALU.add))
            do(dve.reciprocal(m["m1"][:, :], m["m1"][:, :]))
            do(dve.tensor_tensor(wt[:, 0, :], m["m1"][:, :], m["gw"][:, :], ALU.mult))
            do(dve.tensor_tensor(wt[:, 1, :], wt[:, 0, :], m["e2"][:, :], ALU.mult))

        def xT_lo_(b, par):
            dve.wait_ge(xT_hi_done, N + b + 1)
            dve.tensor_tensor(m["xT_lo"][:, par, :], banks(2, 2), m["xT_hi"][:, par, :].bitcast(F32), ALU.subtract)\
               .then_inc(xT_lo_done, 1)

        def aT_lo_(b):
            dve.wait_ge(aT_hi_done, N + b + 1)
            dve.tensor_tensor(m["aT_lo"][:, :], ps[:, 4, 0:FE], m["aT_hi"][:, :].bitcast(F32), ALU.subtract)\
               .then_inc(aT_lo_done, 1)

        mask = fresh_mask(dve, L)

        def body(b, par, first, last):
            def middle():
                dve.wait_ge(silu_done, N + b + 1)
                if not first:
                    dve.wait_ge(aT_ps, N + b)
                dve.tensor_tensor(m["act"][:, :], m["silu"][:, :], ps[:, par, FE:2 * FE], ALU.mult)\
                   .then_inc(act_done, 1)

            if not first:
                aT_lo_(b - 1)
            if last:
                middle()
            else:
                xT_lo_(b + 1, 1 - par)
                with dve.If(is_fresh(mask, b + 1)):
                    lo(dve, 0, base[0] + b + 1, (base[0] + 1 - par) % 2)
                    middle()
                    lo(dve, 1, base[1] + b + 1, (base[1] + 1 - par) % 2)
                with dve.Else():
                    count(dve, (lo_done[0:1], 1))
                    middle()
                    count(dve, (lo_done[1:2], 1))
            with dve.If(is_fresh(mask, b)):
                lo(dve, 2, base[2] + b, (base[2] + par) % 2)
            with dve.Else():
                count(dve, (lo_done[2:3], 1))

        def skip(b):
            count(dve, ((aT_lo_done, xT_lo_done, *lo_done, act_done), 2))

        def skip_last():
            count(dve, ((xT_lo_done, *lo_done[0:2]), 1), ((lo_done[2], act_done), 2), ((aT_lo_done,), 3))

        combine_weights()
        lo(dve, 0, base[0], base[0] % 2)
        lo(dve, 1, base[1], base[1] % 2)
        xT_lo_(0, 0)
        blocks(dve, L, body, skip, lambda: aT_lo_(BLOCKS - 1), skip_last)
        if L == 0:
            lo(dve, *PROJ[0], PROJ[0][1] % 2, gain_kv)
        for t in range(T):
            dve.wait_ge(y_back[t % 4], 64 * L + 32 * (t // 4 + 1))
            for j in range(2):
                ins = dve.scalar_tensor_tensor(out=h[:, t, :], in0=yg[t % 4][:, j, :],
                                               scalar=wt[:, j, t:t + 1], in1=h[:, t, :],
                                               op0=ALU.mult, op1=ALU.add)
                if j == 0:
                    do(ins)
            ins.then_inc(y_added, 1)
            follow(t)

    @block.vector
    def _(dve):
        def do(ins):
            link(dve, "dve", ins)

        dve.wait_ge(consts, 1)
        do(dve.tensor_copy(ident_bf[:, :], ident[:, :]))
        head = WINDOWS[-1]
        for g, w in enumerate(WINDOWS):
            dve.scalar_tensor_tensor(out=band0[:, g, head:P], in0=band[:, g, head:P], scalar=1.0 / w,
                                     in1=ident[:, head:P], op0=ALU.mult, op1=ALU.subtract)
            do(dve.tensor_scalar(band0[:, g, 0:head], idx_row[:, 0:head], float(w), None, ALU.min))
            do(dve.reciprocal(band0[:, g, 0:head], band0[:, g, 0:head]))
            do(dve.tensor_tensor(band0[:, g, 0:head], band0[:, g, 0:head], band[:, g, 0:head], ALU.mult))
            do(dve.tensor_tensor(band0[:, g, 0:head], band0[:, g, 0:head], ident[:, 0:head], ALU.subtract))
            ins = dve.scalar_tensor_tensor(out=band[:, g, :], in0=band[:, g, :], scalar=1.0 / w, in1=ident[:, :],
                                           op0=ALU.mult, op1=ALU.subtract)
        ins.then_inc(consts, 1)

        def normed(t):
            dve.wait_ge(inv_done, t + 1)
            dve.scalar_tensor_tensor(out=pool_x[:, t, :], in0=h0[:, t, :], scalar=inv[:, t:t + 1],
                                     in1=gain_bc0[:, :], op0=ALU.mult, op1=ALU.mult).then_inc(poolx_done, 1)

        dve.wait_ge(mix_in, 16)
        normed(0)
        dve.wait_ge(scale_in, 16)
        dve.wait_ge(loaded[0][0], 32)
        for c in range(2):
            rw = raw[:, 0, :].rearrange("p (g c d) -> p g c d", g=4, c=2)[:, :, c, :]
            ins = dve.tensor_tensor(rw, rw, scale_bc[:, :].rearrange("p (g d) -> p g d", g=4), ALU.mult)
            do(ins) if c == 0 else ins.then_inc(pool_w_scaled, 1)
        normed(1)
        dve.wait_ge(hi_done[0], 1)
        dve.tensor_tensor(w_lo[:, 0, :], raw[:, 0, :], w_hi[:, 0, :].bitcast(F32), ALU.subtract).then_inc(lo_done[0], 1)
        for t in range(T):
            dve.wait_ge(dT_hi_done, t + 1)
            dve.tensor_tensor(dT_lo[:, :, :].rearrange("p k n -> p (k n)"), banks(0, 2),
                              dT_hi[:, :, :].rearrange("p k n -> p (k n)").bitcast(F32), ALU.subtract)\
               .then_inc(dT_lo_done, 1)
            if t >= 1:
                router_norm(dve, 0, t - 1)
            dve.wait_ge(py_ps, t + 1)
            dve.tensor_tensor(h0[:, t, :], h0[:, t, :], banks(4, 2), ALU.add).then_inc(h_done, 1)
            if t + 2 < T:
                normed(t + 2)
        router_norm(dve, 0, T - 1)
        def hT_lo_(t):
            dve.wait_ge(hT_hi_done, t + 1)
            dve.tensor_tensor(hT_lo[:, :, t * P:(t + 1) * P], banks(2 * (t % 2), 2).rearrange("p (k n) -> p k n", k=K),
                              hT_hi[:, :, t * P:(t + 1) * P].bitcast(F32), ALU.subtract).then_inc(hT_lo_done, 1)

        dve_moe(dve, 0, lambda t: hT_lo_(t - 3) if t >= 3 else None)
        for t in range(T - 3, T):
            hT_lo_(t)
        lo(dve, *PROJ[1], PROJ[1][1] % 2, gain_kv)
        for k in range(K):
            dve.wait_ge(wf_done, K)
            dve.scalar_tensor_tensor(out=wf_lo[:, k, :], in0=wf_raw[:, k, :], scalar=gain_kv[:, k:k + 1],
                                     in1=wf_hi[:, k, :].bitcast(F32), op0=ALU.mult, op1=ALU.subtract)\
               .then_inc(wf_done, 1)
        lo(dve, *PROJ[2], PROJ[2][1] % 2, gain_kv)
        lo(dve, *PROJ[3], PROJ[3][1] % 2, gain_kv)
        dve.wait_ge(z_ps, 1)
        z, lf, ln_ = banks(0, 2)[0:HEADS, :], zf[0:HEADS, 0, :], zf[0:HEADS, 1, :]
        do(dve.tensor_scalar(lf, z, bf_col[0:HEADS, :], None, ALU.add))
        do(dve.scalar_tensor_tensor(out=ln_, in0=lf, scalar=-1.0, in1=lf, op0=ALU.mult, op1=ALU.max))
        dve.sem_inc(zf_dve, 1)
        do(dve.tensor_scalar(lf, lf, 0.0, None, ALU.min))
        dve.wait_ge(zf_act, 2)
        dve.tensor_tensor_scan(lf, lf, ln_, 0.0, ALU.add, ALU.subtract).then_inc(zf_dve, 1)
        lo(dve, *PROJ[4], PROJ[4][1] % 2, gain_kv)
        for half in range(2):
            dve.wait_ge(f_hi_done, half + 1)
            if half:
                dve.wait_ge(f_out, 64)
            do(dve.tensor_tensor(stage[0:HEADS, 1, :], lf[:, 512 * half:512 * half + 512],
                                 stage[0:HEADS, 0, :].bitcast(F32), ALU.subtract))
            do(dve.tensor_scalar(stage[0:HEADS, 2, :], stage[0:HEADS, 0, :].bitcast(F32), -1.0, None, ALU.mult))
            dve.tensor_scalar(stage[0:HEADS, 3, :], stage[0:HEADS, 1, :].bitcast(F32), -1.0, None, ALU.mult)\
               .then_inc(f_lo_done, 1)
        for i in range(5, 7):
            lo(dve, *PROJ[i], PROJ[i][1] % 2, gain_kv)
        lo_next = 7
        for n in range(32):
            dve.wait_ge(kq_hi_done, n + 1)
            scale = 1.0 if n < 16 else HD ** -0.5
            dve.scalar_tensor_tensor(out=stage[:, 2 * (n % 2) + 1, :], in0=ps[:, n % 4, :], scalar=scale,
                                     in1=stage[:, 2 * (n % 2), :].bitcast(F32), op0=ALU.mult, op1=ALU.subtract)\
               .then_inc(kq_lo_done, 1)
            if n % 4 == 3 and lo_next < 15:
                g = gain_kv if lo_next < 8 else gain_q if lo_next < 12 else None
                lo(dve, *PROJ[lo_next], PROJ[lo_next][1] % 2, g)
                lo_next += 1
        meet(dve, "dve")

        def max_(hd, i):
            u, q = i % 2, i % 4
            dve.wait_ge(qk_ps, hd * T + i + 1)
            if not isinstance(hd, int) or hd * T + i >= 4:
                dve.wait_ge(exp_done, hd * T + i - 3)
            dve.tensor_reduce(neg_max[:, q:q + 1], banks(2 * u, 2)[:, 0:(ORDER[i] + 1) * P], AX.X, ALU.max,
                              negate=True).then_inc(max_done, 1)

        def pT_early(hd, i):
            dve.wait_ge(pT_ps, hd * T + i + 1)
            n = min(ORDER[i] + 1, 4) * P
            dve.tensor_copy(probsT[:, i % 2, 0:n], ps[:, 4, 0:n]).then_inc(pT_dve, 1)

        def o_(hd, i):
            u, q = i % 2, i % 4
            dve.reciprocal(row_inv[:, u:u + 1], row_sum[:, q:q + 1]).then_inc(rinv_done, 1)
            dve.wait_ge(pv_ps, hd * T + i + 1)
            dve.wait_ge(rinv_done, hd * T + i + 1)
            dve.tensor_scalar(o_tok[:, ORDER[i], bass.ds(hd * HD, HD)], ps[:, 6 + u, 0:HD], row_inv[:, u:u + 1], None,
                              ALU.mult).then_inc(o_done, 1)

        def pair(hd, first, last):
            for j in range(2):
                for i in range(T):
                    if i < T - 1:
                        max_(hd + j, i + 1)
                    elif not (last and j == 1):
                        max_(hd + j + 1, 0)
                    pT_early(hd + j, i)
                    if i:
                        o_(hd + j, i - 1)
                    elif not (first and j == 0):
                        o_(hd + j - 1, T - 1)

        max_(0, 0)
        pair(0, True, False)
        with dve.Fori(1, HEADS // 2 - 1) as p:
            pair(2 * p, False, False)
        pair(HEADS - 2, False, True)
        o_(HEADS - 1, T - 1)
        meet(dve, "dve")
        def oT_lo_(t):
            dve.wait_ge(oT_hi_done, t + 1)
            dve.tensor_tensor(oT_lo[:, :, t * P:(t + 1) * P], banks(2 * (t % 2), 2).rearrange("p (k n) -> p k n", k=K),
                              oT_hi[:, :, t * P:(t + 1) * P].bitcast(F32), ALU.subtract).then_inc(oT_lo_done, 1)

        oT_lo_(0)
        oT_lo_(1)
        for c in range(4):
            if c == 1:
                lo(dve, *PROJ[15], PROJ[15][1] % 2)
            for t in range(T):
                n = T * c + t
                if c == 0:
                    if t + 2 < T:
                        oT_lo_(t + 2)
                    dve.wait_ge(h_back[t], 16)
                if c == 3 and t >= 1:
                    router_norm(dve, 1, t - 1)
                dve.wait_ge(op_ps, n + 1)
                hv = h1[:, t, c * 256:(c + 1) * 256]
                dve.tensor_tensor(hv, hv, ps[:, 4 + n % 2, 0:256], ALU.add).then_inc(op_done, 1)
        router_norm(dve, 1, T - 1)
        def final(t):
            dve.wait_ge(inv_done, 4 * T + t + 1)
            if t == 0:
                dve.wait_ge(gains_in, 16 * 5)
            if t >= 4:
                dve.wait_ge(out_done[t % 4], 16)
            dve.scalar_tensor_tensor(out=fin_out[:, t % 4, :], in0=h1[:, t, :], scalar=inv[:, t:t + 1],
                                     in1=fin_gain[:, :], op0=ALU.mult, op1=ALU.mult).then_inc(fin_done, 1)

        dve_moe(dve, 1, lambda t: final(t - 1) if t else None)
        final(T - 1)

    def transposes(pe, src, bank, n):
        dst = banks(bank, 2) if n * P > 512 else ps[:, bank, :]
        for k in range(n):
            ins = pe.transpose(dst[:, k * P:(k + 1) * P], src[:, k:n * P:n], ident[:, :])
        return ins

    def router_turn(pe, L, t):
        pe.wait_ge(xn_done, T * L + t + 1)
        sp_wait(pe, rT_done, T * L + t, 0)
        transposes(pe, moe_mem[L]["xn"][:, t % 2, :], 2, K).then_inc(rT_ps, 1)

    def router_logits(pe, L, t):
        if t == 0:
            pe.wait_ge(router_in[L], 16 * 5)
        pe.wait_ge(rT_done, T * L + t + 1)
        for k in range(K):
            ins = pe.matmul(banks(6, 2)[0:G + NE, t * P:(t + 1) * P], moe_mem[L]["wr"][:, k, :],
                            moe_mem[L]["rT"][:, k * P:(k + 1) * P], start=(k == 0), stop=(k == K - 1))
        ins.then_inc(lgT_ps, 1)

    def pe_moe(pe, L):
        m = moe_mem[L]
        base = M_MOE[L]
        N = L * BLOCKS
        pe.wait_ge(lgT_done, L + 1)
        for t in range(T):
            ins = pe.transpose(ps[:, 5, t * (G + NE):(t + 1) * (G + NE)], m["lgT"][0:G + NE, t * P:(t + 1) * P],
                               ident[0:G + NE, 0:G + NE])
        ins.then_inc(lg_ps, 1)
        pe.wait_ge(sel_done, L + 1)
        sel = m["sel"][:, :, :].rearrange("p t e -> p (t e)")
        cum = m["cum"][:, 0:T, :].rearrange("p t e -> p (t e)")
        pe.matmul(ps[:, 6, 0:P], before[:, :], sel, start=True, stop=False)
        pe.matmul(ps[:, 6, 0:P], ones[:, :], cum, start=False, stop=True)
        pe.matmul(ps[:, 6, P:P + NE], ones[:, :], m["cum"][:, T, :], start=True, stop=True).then_inc(rank_ps, 1)
        pe.wait_ge(slots_done, 2 * L + 2)
        for j in range(2 * T):
            ins = pe.matmul(ps[:, 6, 256:256 + 2 * NB], m["slot_of"][:, j, :],
                            m["tok_of"][:, j, :, :].rearrange("p h n -> p (h n)"),
                            start=(j == 0), stop=(j == 2 * T - 1))
        ins.then_inc(tok_ps, 1)

        def xT(b, par):
            pe.wait_ge(gathered[L][par], 8 * (b - par) + 16)
            sp_wait(pe, xT_lo_done, N + b, 0)
            transposes(pe, m["xg"][:, par, :], 2, K).then_inc(xT_ps, 1)

        def gate_up(b, par, s):
            pe.wait_ge(lo_done[s], base[s] + b + 1)
            if s == 0:
                pe.wait_ge(xT_lo_done, N + b + 1)
                if not isinstance(b, int) or b >= 2:
                    pe.wait_ge(act_done, N + b - 1)
            o = ps[:, par, :].rearrange("p (j f) -> p j f", j=2)
            for k in range(4):
                kk = 4 * s + k
                wh = w_hi[:, s, :].rearrange("p (j k f) -> p j k f", j=2, k=4)[:, :, k, :]
                wl = w_lo[:, s, :].rearrange("p (j k f) -> p j k f", j=2, k=4)[:, :, k, :]
                ins = three(pe, o, m["xT_hi"][:, par, kk * P:(kk + 1) * P], m["xT_lo"][:, par, kk * P:(kk + 1) * P],
                            wh, wl, kk == 0, kk == K - 1)
            ins.then_inc(used[s], 1)

        def aT(b):
            pe.wait_ge(act_done, N + b + 1)
            sp_wait(pe, aT_lo_done, N + b, 0)
            transposes(pe, m["act"][:, :], 4, KF).then_inc(aT_ps, 1)

        def down(b):
            pe.wait_ge(lo_done[2], base[2] + b + 1)
            pe.wait_ge(aT_lo_done, N + b + 1)
            if not isinstance(b, int) or b >= 1:
                pe.wait_ge(y_act, N + b)
            for k in range(KF):
                for half in range(2):
                    c = slice(1024 * k + 512 * half, 1024 * k + 512 * half + 512)
                    ins = three(pe, ps[:, 5 + half, :], m["aT_hi"][:, k * P:(k + 1) * P],
                                m["aT_lo"][:, k * P:(k + 1) * P], w_hi[:, 2, c], w_lo[:, 2, c], k == 0, k == KF - 1)
            ins.then_inc(used[2], 1)

        def body(b, par, first, last):
            gate_up(b, par, 0)
            if not first:
                aT(b - 1)
            if not last:
                xT(b + 1, 1 - par)
            gate_up(b, par, 1)
            if not first:
                down(b - 1)

        def finish():
            aT(BLOCKS - 1)
            down(BLOCKS - 1)

        def skip(b):
            count(pe, ((xT_ps, aT_ps, *used), 2))

        def skip_last():
            count(pe, ((xT_ps,), 1), (used[0:2], 2), ((aT_ps, used[2]), 3))

        xT(0, 0)
        blocks(pe, L, body, skip, finish, skip_last)

    @block.tensor
    def _(pe):
        pe.wait_ge(consts, 2)

        def pooled(t):
            pe.wait_ge(poolx_done, t + 1)
            if t >= 1:
                pe.wait_ge(dT_lo_done, t)
            for c in range(K):
                g = c // 2
                o = banks(0, 2)[:, c * P:(c + 1) * P]
                ins = pe.matmul(o, pool_x[:, t, c * P:(c + 1) * P], (band if t else band0)[:, g, :],
                                start=True, stop=(t == 0))
                if t:
                    ins = pe.matmul(o, pool_x[:, t - 1, c * P:(c + 1) * P], band_prev[:, g, :],
                                    start=False, stop=True)
            ins.then_inc(dT_ps, 1)

        pooled(0)
        for t in range(T):
            pe.wait_ge(dT_lo_done, t + 1)
            if t == 0:
                pe.wait_ge(lo_done[0], 1)
            if t >= 1:
                pe.wait_ge(h_done, t)
            for g in range(4):
                o = banks(4, 2)[:, g * GW:(g + 1) * GW]
                for c in range(2):
                    w = slice((2 * g + c) * GW, (2 * g + c + 1) * GW)
                    ins = three(pe, o, dT_hi[:, 2 * g + c, :], dT_lo[:, 2 * g + c, :], w_hi[:, 0, w], w_lo[:, 0, w],
                                c == 0, c == 1)
            ins.then_inc(py_ps, 1)
            if t + 1 < T:
                pooled(t + 1)
            if t >= 1:
                router_turn(pe, 0, t - 1)
            if t >= 2:
                router_logits(pe, 0, t - 2)
        pe.drain().then_inc(used[0], 1)
        router_logits(pe, 0, T - 2)
        router_turn(pe, 0, T - 1)
        router_logits(pe, 0, T - 1)
        pe_moe(pe, 0)
        def v_tile(c, t):
            s, mm = PROJ[c]
            n = T * c + t
            if n >= 4:
                pe.wait_ge(v_done, n - 3)
            for k in range(K):
                w = slice(k * 256, (k + 1) * 256)
                ins = three(pe, ps[:, 4 + n % 4, 0:256], hT_hi[:, k, t * P:(t + 1) * P],
                            hT_lo[:, k, t * P:(t + 1) * P], w_hi[:, s, w], w_lo[:, s, w], k == 0, k == K - 1)
            ins.then_inc(v_ps, 1)

        for t in range(T + 3):
            if t < T:
                pe.wait_ge(xhat_done, t + 1)
                if t >= 2:
                    pe.wait_ge(hT_lo_done, t - 1)
                transposes(pe, xhat[:, t % 2, :], 2 * (t % 2), K).then_inc(hT_ps, 1)
            if t == 3:
                pe.wait_ge(lo_done[PROJ[0][0]], PROJ[0][1] + 1)
            if t >= 3:
                pe.wait_ge(hT_lo_done, t - 2)
                v_tile(0, t - 3)
        pe.drain().then_inc(used[PROJ[0][0]], 1)
        pe.wait_ge(wf_done, 2 * K)
        for half in range(2):
            tok = slice(512 * half, 512 * half + 512)
            for k in range(K):
                ins = three(pe, ps[0:HEADS, half, :], wf_hi[:, k, :], wf_lo[:, k, :], hT_hi[:, k, tok],
                            hT_lo[:, k, tok], k == 0, k == K - 1)
        ins.then_inc(z_ps, 1)
        for c in range(1, 4):
            s, mm = PROJ[c]
            pe.wait_ge(lo_done[s], mm + 1)
            for t in range(T):
                v_tile(c, t)
            pe.drain().then_inc(used[s], 1)
        for c in range(8):
            s, mm = PROJ[4 + c]
            pe.wait_ge(lo_done[s], mm + 1)
            for r in range(2):
                for half in range(2):
                    n = 4 * c + 2 * r + half
                    if n >= 4:
                        pe.wait_ge(kq_lo_done, n - 3)
                    elif n == 0:
                        pe.wait_ge(zf_dve, 1)
                    for k in range(K):
                        w = slice(k * 256 + r * P, k * 256 + (r + 1) * P)
                        tok = slice(512 * half, 512 * half + 512)
                        ins = three(pe, ps[:, n % 4, :], w_hi[:, s, w], w_lo[:, s, w], hT_hi[:, k, tok],
                                    hT_lo[:, k, tok], k == 0, k == K - 1)
                    ins.then_inc(kq_ps, 1)
            pe.drain().then_inc(used[s], 1)
        meet(pe, "pe")

        def scores(hd, hpar, u, i):
            if i == 0:
                pe.wait_ge(head_in[hpar], 48 * (hd - hpar) + 96)
            if not isinstance(hd, int) or hd * T + i >= 2:
                pe.wait_ge(exp_done, hd * T + i - 1)
            q1, q2, k1, k2 = heads_mem[hpar]
            q = ORDER[i]
            tt = slice(q * P, (q + 1) * P)
            n = (q + 1) * P
            for c in range(0, n, 512):
                w = min(512, n - c)
                o = banks(2 * u, 2)[:, c:c + w]
                last = c + w == n
                pe.matmul(o, q1[:, tt], k1[:, c:c + w], start=True, stop=False)
                pe.matmul(o, q2[0:HK, tt], k2[0:HK, c:c + w], start=False, stop=not last)
            pe.matmul(banks(2 * u, 2)[:, q * P:n], ident_bf[:, :], future_bf[:, :], start=False, stop=True)\
              .then_inc(qk_ps, 1)

        def turn(hd, i):
            pe.wait_ge(exp_done, hd * T + i + 1)
            if not isinstance(hd, int) or hd * T + i >= 1:
                pe.wait_ge(pT_dve, hd * T + i)
            if ORDER[i] >= 4:
                sp_wait(pe, pT_act, hd * (T // 2), i // 2)
            for j in range(ORDER[i] + 1):
                ins = pe.transpose(banks(4, 2)[:, j * P:(j + 1) * P], probs[:, i % 2, j * P:(j + 1) * P], ident[:, :])
            ins.then_inc(pT_ps, 1)

        def weigh(hd, i):
            pe.wait_ge(pT_dve, hd * T + i + 1)
            if ORDER[i] >= 4:
                pe.wait_ge(pT_act, hd * (T // 2) + i // 2 + 1)
            if not isinstance(hd, int) or hd * T + i >= 2:
                pe.wait_ge(o_done, hd * T + i - 1)
            for j in range(ORDER[i] + 1):
                ins = pe.matmul(ps[:, 6 + i % 2, 0:HD], probsT[:, i % 2, j * P:(j + 1) * P],
                                val[:, j, bass.ds(hd * HD, HD)], start=(j == 0), stop=(j == ORDER[i]))
            ins.then_inc(pv_ps, 1)

        def pair(hd, first, last):
            for j in range(2):
                for i in range(T):
                    if i < T - 1:
                        scores(hd + j, j, (i + 1) % 2, i + 1)
                    elif not (last and j == 1):
                        scores(hd + j + 1, 1 - j, 0, 0)
                    turn(hd + j, i)
                    if i:
                        weigh(hd + j, i - 1)
                    elif not (first and j == 0):
                        weigh(hd + j - 1, T - 1)

        scores(0, 0, 0, 0)
        pair(0, True, False)
        with pe.Fori(1, HEADS // 2 - 1) as p:
            pair(2 * p, False, False)
        pair(HEADS - 2, False, True)
        weigh(HEADS - 1, T - 1)
        meet(pe, "pe")
        def turn_values(t):
            if t >= 2:
                pe.wait_ge(oT_lo_done, t - 1)
            transposes(pe, o_tok[:, t, :], 2 * (t % 2), K).then_inc(oT_ps, 1)

        turn_values(0)
        turn_values(1)
        for c in range(4):
            s, mm = PROJ[12 + c]
            pe.wait_ge(lo_done[s], mm + 1)
            for t in range(T):
                n = T * c + t
                if c == 0:
                    pe.wait_ge(oT_lo_done, t + 1)
                if c == 0 and t + 2 < T:
                    turn_values(t + 2)
                if n >= 2:
                    pe.wait_ge(op_done, n - 1)
                for k in range(K):
                    w = slice(k * 256, (k + 1) * 256)
                    ins = three(pe, ps[:, 4 + n % 2, 0:256], oT_hi[:, k, t * P:(t + 1) * P],
                                oT_lo[:, k, t * P:(t + 1) * P], w_hi[:, s, w], w_lo[:, s, w], k == 0, k == K - 1)
                ins.then_inc(op_ps, 1)
                if c == 3 and t >= 1:
                    router_turn(pe, 1, t - 1)
                if c == 3 and t >= 2:
                    router_logits(pe, 1, t - 2)
            pe.drain().then_inc(used[s], 1)
        router_logits(pe, 1, T - 2)
        router_turn(pe, 1, T - 1)
        router_logits(pe, 1, T - 1)
        pe_moe(pe, 1)

    block.__exit__(None, None, None)


_INS = ['x', 'mix_norm', 'ffn_norm', 'pool_w', 'pool_scale', 'kv_norm', 'w_k', 'w_v', 'w_f', 'b_f', 'w_q', 'w_o',
        'router_g', 'router_g_b', 'router_e', 'router_e_b', 'w_gate', 'w_up', 'w_down', 'final_norm']


def kernel(**inputs):
    import numpy as np
    import concourse.bacc as bacc
    from concourse.bass_utils import run_bass_kernel_spmd

    nc = bacc.Bacc("TRN2", target_bir_lowering=False, num_devices=1)
    arrays, aps = {}, []
    for name in _INS:
        a = np.ascontiguousarray(inputs[name])
        arrays[f"in_{name}"] = a
        aps.append(nc.dram_tensor(f"in_{name}", a.shape, mybir.dt.from_np(a.dtype), kind="ExternalInput").ap())
    aps.append(nc.dram_tensor("out_0", (1, S, D), F32, kind="ExternalOutput").ap())
    trunk(nc, *aps)
    r = run_bass_kernel_spmd(nc, [arrays], core_ids=[0])
    return np.asarray(r.results[0]["out_0"])
```

```python
import concourse.bass as bass
from concourse import mybir

F32 = mybir.dt.float32
F32R = mybir.dt.float32r
BF16 = mybir.dt.bfloat16
I32 = mybir.dt.int32
U32 = mybir.dt.uint32
ALU = mybir.AluOpType
ACT = mybir.ActivationFunctionType
AX = mybir.AxisListType

P = 128
S = 1024
D = 1024
T = S // P
K = D // P
HEADS, HD = 16, 64
WINDOWS = (2, 4, 8, 16)
REACH = WINDOWS[-1]
GW = D // len(WINDOWS)
G, E = 4, 4
NE = G * E
FE = 256
KF = FE // P
TOPK = 2
BLOCKS = (TOPK * S + NE * (P - 1)) // P
NB = 32
LEAST = TOPK * S // P
EPS = 1e-6
NEG = -1e30
CH = 2048
ORDER = (7, 3, 6, 2, 5, 1, 4, 0)
AUG = 4
HK = HD + AUG


def trunk(nc, x, mix_norm, ffn_norm, pool_w, pool_scale, kv_norm, w_k, w_v, w_f, b_f, w_q, w_o,
          router_g, router_g_b, router_e, router_e_b, w_gate, w_up, w_down, final_norm, out):
    start = (nc.sbuf_base + 31) // 32 * 32
    REG = 32768
    R = [start, start + REG, start + 2 * REG]
    RAW0 = start + 3 * REG
    SPL0 = RAW0 + 6 * CH * 4
    SMALL0 = SPL0 + 6 * CH * 4
    small_at = [SMALL0]

    def at(name, shape, dtype, offset):
        return nc.alloc_sbuf_tensor_at(name, shape, dtype, offset=offset)

    def size(shape, dtype):
        n = 2 if dtype == BF16 else 4
        for s in shape[1:]:
            n *= s
        return (n + 31) // 32 * 32

    def small(name, shape, dtype=F32):
        t = at(name, shape, dtype, small_at[0])
        small_at[0] += size(shape, dtype)
        return t

    def pack(name_shape_dtypes, offset, limit):
        made = []
        for name, shape, dtype in name_shape_dtypes:
            made.append(at(name, shape, dtype, offset))
            offset += size(shape, dtype)
        assert offset <= limit, (name_shape_dtypes[0][0], offset - limit)
        return made

    raw = at("raw", [P, 6, CH], F32, RAW0)
    w_hi = at("w_hi", [P, 3, CH], F32R, SPL0)
    w_lo = at("w_lo", [P, 3, CH], F32R, SPL0 + 3 * CH * 4)

    ident = small("ident", [P, P])
    ones = small("ones", [P, P])
    before = small("before", [P, P])
    upto = small("upto", [P, P])
    iota_p = small("iota_p", [P, P])
    ident_bf = small("ident_bf", [P, P], BF16)
    future_bf = small("future_bf", [P, P], BF16)
    stage = small("stage", [P, 4, 512], F32R)
    sumsq = small("sumsq", [P, T])
    inv = small("inv", [P, T])
    halfneg = small("halfneg", [P, T])
    gain_kv = small("gain_kv", [P, K])
    gain_q = small("gain_q", [P, K])
    wf_raw = small("wf_raw", [P, K, HEADS])
    wf_hi = small("wf_hi", [P, K, HEADS], F32R)
    wf_lo = small("wf_lo", [P, K, HEADS], F32R)
    bf_col = small("bf_col", [P, 1])
    neg_max = small("neg_max", [P, 4])
    row_sum = small("row_sum", [P, 4])
    row_inv = small("row_inv", [P, 2])
    idx_now = small("idx_now", [P, 2], I32)
    idle = small("idle", [P, 1])
    limit = nc.sbuf_usable_end
    assert small_at[0] <= limit, small_at[0] - limit

    h0 = at("h0", [P, T, D], F32, R[0])
    h1 = at("h1", [P, T, D], F32, R[2])
    pool_x = at("pool_x", [P, T, D], F32, R[1])
    (band, band0, band_prev, dT_hi, dT_lo) = pack([
        ("band", [P, 4, P], F32), ("band0", [P, 4, P], F32), ("band_prev", [P, 4, P], F32),
        ("dT_hi", [P, K, P], F32R), ("dT_lo", [P, K, P], F32R)], SPL0 + CH * 4, SPL0 + 3 * CH * 4)
    (gain_bc0, scale_bc, idx_row) = pack([
        ("gain_bc0", [P, D], F32), ("scale_bc", [P, D], F32), ("idx_row", [P, P], F32)],
        SPL0 + 4 * CH * 4, SPL0 + 6 * CH * 4)
    wt = small("wt", [P, 2, T])
    pos_i = small("pos_i", [P, 2, T], I32)
    yg = [at(f"yg{n}", [P, 2, D], F32, SPL0 + slot * CH * 4) for n, slot in enumerate((0, 2, 3, 5))]
    moe_mem, raw_third = [], []
    for L in range(2):
        A, B = (R[1], R[2]) if L == 0 else (R[1], R[0])
        raw_third.append([at(f"raw_third{L}_{s}", [P, CH], F32, place)
                          for s, place in enumerate((A + 3 * CH * 4, B + 2 * CH * 4, B + 3 * CH * 4))])
        RT = [RAW0 + slot * CH * 4 for slot in (5, 4, 3)]
        m = {}

        def put(specs, offset, lim):
            for (name, shape, dtype), t in zip(specs, pack([(f"{n}_{L}", s, d) for n, s, d in specs], offset, lim)):
                m[name] = t
        put([("xn", [P, 2, D], F32)], RT[0], RT[0] + CH * 4)
        put([("rT", [P, D], F32), ("junk", [P, D], F32)], RT[1], RT[1] + CH * 4)
        put([("gain", [P, D], F32), ("wr", [P, K, G + NE], F32), ("br", [P, G + NE], F32)], RT[2], RT[2] + CH * 4)
        put([("lgT", [P, S], F32)], B, B + REG)
        put([("xg", [P, 2, D], F32), ("xT_hi", [P, 2, D], F32R),
             ("xT_lo", [P, 2, D], F32R)], A, A + 3 * CH * 4)
        put([("slot_of", [P, 2 * T, P], BF16)], A, A + REG)
        put([("y", [P, 2, D], F32), ("act", [P, FE], F32), ("silu", [P, FE], F32), ("aT_hi", [P, FE], F32R),
             ("aT_lo", [P, FE], F32R), ("t4", [P, T, G], F32), ("gw", [P, T], F32), ("m1", [P, T], F32),
             ("e2", [P, T], F32), ("tok_i", [P, NB], I32), ("tab_i", [P, 3, NB], I32)], B, B + 2 * CH * 4)
        put([("lg", [P, T, G + NE], F32), ("gm", [P, T], F32), ("gi", [P, T], F32), ("og", [P, T, G], F32),
             ("t16", [P, T, NE], F32), ("es", [P, T, E], F32), ("m2", [P, T], F32),
             ("o1", [P, T, E], F32), ("o2", [P, T, E], F32),
             ("s1", [P, T, NE], F32), ("s2", [P, T, NE], F32), ("sel", [P, T, NE], F32),
             ("cum", [P, T + 1, NE], F32), ("cmp", [P, NB * NE], F32), ("nb", [P, NE], F32),
             ("end", [P, NE], F32), ("base", [P, NE], F32), ("zero", [P, NE], F32), ("pf", [P, T, NE], F32),
             ("pos", [P, 2, T], F32), ("part_i", [P, 2, 2 * T], I32), ("part", [P, 2, 2 * T], F32),
             ("blk_of", [P, 2 * T, NB], F32), ("tok_of", [P, 2 * T, 2, NB], BF16), ("tok", [P, NB], F32),
             ("tab", [P, 3, NB], F32), ("bit", [P, NB], F32)], B + 2 * CH * 4, B + REG)
        moe_mem.append(m)
    io4 = small("io4", [P, 4])
    thr = small("thr", [P, T])
    tok_part = small("tok_part", [P, T, 2])
    assert small_at[0] <= limit, small_at[0] - limit
    hT_hi = at("hT_hi", [P, K, S], F32R, R[1])
    hT_lo = at("hT_lo", [P, K, S], F32R, R[2])
    heads_mem = [pack([(f"{n}_{q}", [P, S], F32R) for n in ("q1", "q2", "k1", "k2")], at_, at_ + 2 * CH * 4)
                 for q, at_ in enumerate((RAW0 + 4 * CH * 4, R[1]))]
    val = at("val", [P, T, D], F32, R[0])
    o_tok = at("o_tok", [P, T, D], F32, R[2])
    probs = at("probs", [P, 2, S], F32, RAW0 + 2 * CH * 4)
    probsT = at("probsT", [P, 2, S], F32, RAW0 + 3 * CH * 4)
    oT_hi = at("oT_hi", [P, K, S], F32R, R[1])
    oT_lo = at("oT_lo", [P, K, S], F32R, R[0])
    xhat = at("xhat", [P, 2, D], F32, RAW0 + 2 * CH * 4)
    square = at("square", [P, D], F32, RAW0 + 3 * CH * 4)
    zf = at("zf", [P, 2, S], F32, RAW0 + 3 * CH * 4)
    fin_gain = at("fin_gain", [P, D], F32, R[1])
    fin_out = at("fin_out", [P, 4, D], F32, R[1] + 4096)
    fin_junk = at("fin_junk", [P, D], F32, R[1] + 5 * 4096)

    ps = nc.alloc_psum_tensor("ps", [P, 8, 512], F32)

    def banks(a, n=1):
        return ps[:, a:a + n, :].rearrange("p b n -> p (b n)")

    xn_d = nc.dram_tensor("xn_d", [S, D], F32)
    y_d = nc.dram_tensor("y_d", [BLOCKS * P, D], F32)
    h_d = nc.dram_tensor("h_d", [S, D], F32)
    kh_d = nc.dram_tensor("kh_d", [HEADS, HD, S], F32)
    ql_d = nc.dram_tensor("ql_d", [HEADS, HD, S], F32)
    k2_d = nc.dram_tensor("k2_d", [HEADS, HK, S], F32)
    q2_d = nc.dram_tensor("q2_d", [HEADS, HK, S], F32)

    def sem(name):
        return nc.alloc_semaphore(name=name)

    consts = sem("consts")
    x_in = [sem(f"x_in{t}") for t in range(T)]
    mix_in = sem("mix_in")
    scale_in = sem("scale_in")
    gains_in = sem("gains_in")
    loaded = [[sem(f"loaded{s}_{q}") for q in range(2)] for s in range(3)]
    block_in = [[sem(f"block_in{s}_{q}") for q in range(3)] for s in range(3)]
    hi_done = [sem(f"hi_done{s}") for s in range(3)]
    lo_done = [sem(f"lo_done{s}") for s in range(3)]
    used = [sem(f"used{s}") for s in range(3)]
    y_cleared = sem("y_cleared")
    slot_free = sem("slot_free")
    pool_w_scaled = sem("pool_w_scaled")
    sq_done = sem("sq_done")
    inv_done = sem("inv_done")
    dve_step = sem("dve_step")
    pool_step = sem("pool_step")
    act_step = sem("act_step")
    barrier = sem("barrier")
    router_in = [sem(f"router_in{L}") for L in range(2)]
    ahead = [sem(f"ahead{L}") for L in range(2)]
    poolx_done = sem("poolx_done")
    dT_ps = sem("dT_ps")
    dT_hi_done = sem("dT_hi_done")
    dT_lo_done = sem("dT_lo_done")
    py_ps = sem("py_ps")
    h_done = sem("h_done")
    xn_done = sem("xn_done")
    xn_out = [sem("xn_out0"), sem("xn_out1")]
    rT_ps = sem("rT_ps")
    rT_done = sem("rT_done")
    lgT_ps = sem("lgT_ps")
    lgT_done = sem("lgT_done")
    lg_ps = sem("lg_ps")
    soft_in = sem("soft_in")
    soft_out = sem("soft_out")
    sel_done = sem("sel_done")
    rank_ps = sem("rank_ps")
    slots_done = sem("slots_done")
    tok_ps = sem("tok_ps")
    tok_done = sem("tok_done")
    eid_done = sem("eid_done")
    idx_done = sem("idx_done")
    idle_done = sem("idle_done")
    gathered = [[sem(f"gathered{L}_{q}") for q in range(2)] for L in range(2)]
    xT_ps = sem("xT_ps")
    xT_hi_done = sem("xT_hi_done")
    xT_lo_done = sem("xT_lo_done")
    silu_done = sem("silu_done")
    act_done = sem("act_done")
    aT_ps = sem("aT_ps")
    aT_hi_done = sem("aT_hi_done")
    aT_lo_done = sem("aT_lo_done")
    y_act = sem("y_act")
    y_out = [sem("y_out0"), sem("y_out1")]
    y_back = [sem(f"y_back{q}") for q in range(4)]
    y_added = sem("y_added")
    xhat_done = sem("xhat_done")
    h_spilled = [sem(f"h_spilled{t}") for t in range(T)]
    h_back = [sem(f"h_back{t}") for t in range(T)]
    hT_ps = sem("hT_ps")
    hT_hi_done = sem("hT_hi_done")
    hT_lo_done = sem("hT_lo_done")
    wf_done = sem("wf_done")
    z_ps = sem("z_ps")
    zf_dve = sem("zf_dve")
    zf_act = sem("zf_act")
    f_hi_done = sem("f_hi_done")
    f_lo_done = sem("f_lo_done")
    f_out = sem("f_out")
    ones_out = sem("ones_out")
    v_ps = sem("v_ps")
    v_done = sem("v_done")
    kq_ps = sem("kq_ps")
    kq_hi_done = sem("kq_hi_done")
    kq_lo_done = sem("kq_lo_done")
    kq_out = [sem("kq_out0"), sem("kq_out1")]
    head_in = [sem("head_in0"), sem("head_in1")]
    qk_ps = sem("qk_ps")
    max_done = sem("max_done")
    exp_done = sem("exp_done")
    pT_ps = sem("pT_ps")
    pT_dve = sem("pT_dve")
    pT_act = sem("pT_act")
    pv_ps = sem("pv_ps")
    rinv_done = sem("rinv_done")
    o_done = sem("o_done")
    oT_ps = sem("oT_ps")
    oT_hi_done = sem("oT_hi_done")
    oT_lo_done = sem("oT_lo_done")
    op_ps = sem("op_ps")
    op_done = sem("op_done")
    fin_done = sem("fin_done")
    out_done = [sem(f"out_done{q}") for q in range(4)]

    M_MOE0 = (1, 0, 0)
    PROJ = []
    nxt = [M_MOE0[0] + BLOCKS, BLOCKS, BLOCKS]
    LOADS = {(0, 0): 1}
    n_loads = {(0, 0): 1}
    for i in range(16):
        s = (i + 1) % 3
        PROJ.append((s, nxt[s]))
        n_loads[s, nxt[s] % 2] = n_loads.get((s, nxt[s] % 2), 0) + 1
        LOADS[s, nxt[s]] = n_loads[s, nxt[s] % 2]
        nxt[s] += 1
    M_MOE1 = tuple(nxt)
    M_MOE = (M_MOE0, M_MOE1)

    def raw_at(s, which, L=0):
        return raw_third[L][s][:, :] if which == 2 else raw[:, s + 3 * which, :]

    def load(sp, slot, done, parts, needed=None):
        if needed is not None:
            sp.sem_inc(slot_free, 1)
        for j, src in enumerate(parts):
            dst = slot[:, j * CH // 2:(j + 1) * CH // 2]
            if len(src.shape) == 3:
                dst = dst.rearrange("p (k n) -> p k n", k=src.shape[1])
            if needed is None:
                sp.dma_start(dst, src).then_inc(done, 16)
            else:
                sp.dma_start(dst, src, cond=needed).then_inc(done, 16)

    def wait_above_zero(eng, sm, value, plus):
        if not isinstance(value, int) or value + plus > 0:
            eng.wait_ge(sm, value + plus)

    def later(place, n):
        which, turn = place
        return (which + n) % 3, turn + (which + n) // 3

    def hi(act, s, m, gain=None):
        act.wait_ge(loaded[s][m % 2], 32 * LOADS[s, m])
        act.wait_ge(used[s], m)
        src = raw_at(s, m % 2)
        if gain is None:
            return act.activation(w_hi[:, s, :], src, ACT.Copy).then_inc(hi_done[s], 1)
        n = CH // K
        for k in range(K):
            ins = act.activation(w_hi[:, s, k * n:(k + 1) * n], src[:, k * n:(k + 1) * n], ACT.Copy,
                                 scale=gain[:, k:k + 1])
        ins.then_inc(hi_done[s], 1)

    def hi_block(act, L, s, b, place):
        which, turn = place
        act.wait_ge(block_in[s][which], 32 * ((11, 10, 10)[which] * L + turn + 1))
        wait_above_zero(act, used[s], M_MOE[L][s] + b, 0)
        act.activation(w_hi[:, s, :], raw_at(s, which, L), ACT.Copy).then_inc(hi_done[s], 1)

    def lo_of(dve, s, src):
        dve.tensor_tensor(w_lo[:, s, :], src, w_hi[:, s, :].bitcast(F32), ALU.subtract).then_inc(lo_done[s], 1)

    def lo(dve, s, m, gain=None):
        dve.wait_ge(hi_done[s], m + 1)
        src = raw_at(s, m % 2)
        if gain is None:
            return lo_of(dve, s, src)
        n = CH // K
        for k in range(K):
            ins = dve.scalar_tensor_tensor(out=w_lo[:, s, k * n:(k + 1) * n], in0=src[:, k * n:(k + 1) * n],
                                           scalar=gain[:, k:k + 1],
                                           in1=w_hi[:, s, k * n:(k + 1) * n].bitcast(F32),
                                           op0=ALU.mult, op1=ALU.subtract)
        ins.then_inc(lo_done[s], 1)

    def lo_block(dve, L, s, b, place):
        dve.wait_ge(hi_done[s], M_MOE[L][s] + b + 1)
        lo_of(dve, s, raw_at(s, place[0], L))

    def three(pe, o, a_hi, a_lo, b_hi, b_lo, first, last):
        pe.matmul(o, a_hi, b_hi, start=first, stop=False)
        pe.matmul(o, a_hi, b_lo, start=False, stop=False)
        return pe.matmul(o, a_lo, b_hi, start=False, stop=last)

    n_barrier = {}

    def meet(eng, key):
        n_barrier[key] = n_barrier.get(key, 0) + 1
        eng.drain().then_inc(barrier, 1)
        eng.wait_ge(barrier, 4 * n_barrier[key])

    chain = {"dve": 0, "pool": 0, "act": 0}
    steps = {"dve": dve_step, "pool": pool_step, "act": act_step}

    def link(eng, who, ins):
        chain[who] += 1
        ins.then_inc(steps[who], 1)
        eng.wait_ge(steps[who], chain[who])

    def blocks(eng, L, body, flush, skip, skip_two, finish):
        eng.wait_ge(eid_done, L + 1)
        live = eng.value_load(moe_mem[L]["tab_i"][0:1, 2, 0:1], min_val=LEAST, max_val=BLOCKS)

        def step(b, par, place, last=False):
            with eng.If(b < live):
                body(b, par, place, False, last)
                if last:
                    finish()
            with eng.Else():
                with eng.If(b - 1 < live):
                    flush(b, par, place, last)
                with eng.Else():
                    skip(b, par, place, last)

        def pair(b, place):
            with eng.If(b - 1 < live):
                step(b, 1, place)
                step(b + 1, 0, later(place, 1))
            with eng.Else():
                skip_two(b, place)

        for b in range(3):
            body(b, b % 2, (b % 3, b // 3), b == 0, False)
        sixes = (BLOCKS - 5) // 6
        with eng.Fori(0, sixes) as i:
            for j in range(3):
                pair(6 * i + 3 + 2 * j, later((0, 2 * i + 1), 2 * j))
        for b in range(3 + 6 * sixes, BLOCKS - 2, 2):
            pair(b, (b % 3, b // 3))
        step(BLOCKS - 2, 1, ((BLOCKS - 2) % 3, (BLOCKS - 2) // 3))
        step(BLOCKS - 1, 0, ((BLOCKS - 1) % 3, (BLOCKS - 1) // 3), True)

    def count(eng, *counts):
        eng.drain()
        for sems, n in counts:
            for sm in sems:
                eng.sem_inc(sm, n)

    def fresh_mask(eng, L):
        eng.wait_ge(eid_done, L + 1)
        row = moe_mem[L]["tab_i"]
        low = eng.value_load(row[0:1, 2, 1:2], min_val=0, max_val=2 ** 16 - 1)
        high = eng.value_load(row[0:1, 2, 2:3], min_val=0, max_val=2 ** 15 - 1)
        return low + high * 2 ** 16

    def is_fresh(mask, b):
        return (mask >> b) & 1

    def bc(ap, shape):
        return ap.to_broadcast(shape)

    block = nc.Block()
    block.__enter__()

    def load_head(sp, hd, par):
        q1, q2, k1, k2 = heads_mem[par]
        for dst, src in ((q1[0:HD, :], q2_d[bass.ds(hd, 1), 0:HD, :]),
                         (q1[HD:P, :], ql_d[bass.ds(hd, 1), :, :]),
                         (k1[0:HD, :], kh_d[bass.ds(hd, 1), :, :]),
                         (k1[HD:P, :], kh_d[bass.ds(hd, 1), :, :]),
                         (q2[0:HK, :], q2_d[bass.ds(hd, 1), :, :]),
                         (k2[0:HK, :], k2_d[bass.ds(hd, 1), :, :])):
            sp.dma_start(dst.bitcast(F32), src.rearrange("h d n -> (h d) n")).then_inc(head_in[par], 16)

    def load_expert(sp, L, e, b, place, needed=None, done=None):
        base = M_MOE[L]
        which, turn = place
        for s in range(3):
            if s < 2:
                ws = [w[L][bass.ds(e, 1)].rearrange("e (p k) f -> p (e k) f", k=K)[:, 4 * s:4 * s + 4, :]
                      for w in (w_gate, w_up)]
            else:
                wd = w_down[L][bass.ds(e, 1)].rearrange("e (p k) n -> p (e k) n", k=KF)
                ws = [wd[:, 0, :], wd[:, 1, :]]
            if isinstance(b, int) and b < 3:
                wait_above_zero(sp, lo_done[s], base[s], 0)
            else:
                sp.wait_ge(lo_done[s], base[s] + b - 2)
            load(sp, raw_at(s, which, L), done or block_in[s][which], ws, needed)

    def sp_moe(sp, L):
        m = moe_mem[L]
        base = M_MOE[L]
        for t in range(T):
            sp.wait_ge(xn_done, T * L + t + 1)
            sp.dma_start(xn_d[t * P:(t + 1) * P, :], m["xn"][:, t % 2, :]).then_inc(xn_out[t % 2], 16)
        sp.wait_ge(ahead[L], 96)
        for q in range(2):
            sp.wait_ge(xn_out[q], 64 * (L + 1))
        sp.wait_ge(eid_done, L + 1)

        def table(row, b):
            return sp.value_load(m["tab_i"][0:1, row, bass.ds(b, 1)], min_val=0, max_val=NE - 1)

        def load_block(b, place):
            load_expert(sp, L, table(0, b), b, place, table(1, b))

        def store_y(b, par):
            sp.wait_ge(y_act, L * BLOCKS + b + 1)
            sp.dma_start(y_d[bass.ds(b * P, P), :], m["y"][:, par, :]).then_inc(y_out[par], 16)

        def body(b, par, place, first, last):
            if not isinstance(b, int) or b + 3 < BLOCKS:
                load_block(b + 3, later(place, 3))
            if not first:
                store_y(b - 1, 1 - par)

        def no_load(b, par, place, last):
            if not isinstance(b, int) or b + 3 < BLOCKS:
                for s in range(3):
                    sp.sem_inc(block_in[s][place[0]], 32)
            if last:
                sp.sem_inc(y_out[par], 16)

        def flush(b, par, place, last):
            store_y(b - 1, 1 - par)
            no_load(b, par, place, last)

        def skip(b, par, place, last):
            sp.sem_inc(y_out[1 - par], 16)
            no_load(b, par, place, last)

        for b in range(3):
            load_block(b, (b, 0))
        sp.wait_ge(y_cleared, 16)

        def skip_two(b, place):
            for q in range(2):
                sp.sem_inc(y_out[q], 16)
                if not isinstance(b, int) or b + q + 3 < BLOCKS:
                    for s in range(3):
                        sp.sem_inc(block_in[s][(place[0] + q) % 3], 32)

        blocks(sp, L, body, flush, skip, skip_two, lambda: store_y(BLOCKS - 1, 0))

    def proj_load(sp, i):
        w = (w_v, w_k, w_q[0], w_o[0])[i // 4]
        s, m = PROJ[i]
        c = i % 4
        src = w.rearrange("(p k) n -> p k n", k=K)[:, :, c * 256:(c + 1) * 256]
        sp.wait_ge(lo_done[s], m if i < 3 else m - 1)
        load(sp, raw_at(s, m % 2), loaded[s][m % 2], [src[:, 0:4, :], src[:, 4:8, :]])

    @block.sync
    def _(sp):
        for t in range(T):
            sp.dma_start(h0[:, t, :], x[0, t * P:(t + 1) * P, :]).then_inc(x_in[t], 16)
            if t == 0:
                sp.dma_start(gain_bc0[:, :], mix_norm[0:1, :].partition_broadcast(P)).then_inc(mix_in, 16)
            if t == 2:
                pw = pool_w[0].rearrange("g (c p) d -> p g c d", p=P)
                for j in range(2):
                    dst = raw[:, 0, j * CH // 2:(j + 1) * CH // 2].rearrange("p (g c d) -> p g c d", g=2, c=2)
                    sp.dma_start(dst, pw[:, 2 * j:2 * j + 2, :, :]).then_inc(loaded[0][0], 16)
        sp.dma_start(gain_kv[:, :], kv_norm.rearrange("(p k) -> p k", k=K)).then_inc(gains_in, 16)
        sp.dma_start(gain_q[:, :], mix_norm[1].rearrange("(p k) -> p k", k=K)).then_inc(gains_in, 16)
        sp.dma_start(wf_raw[:, :, :], w_f.rearrange("(p k) n -> p k n", k=K)).then_inc(gains_in, 16)
        sp.dma_start(bf_col[0:HEADS, :], b_f.unsqueeze(1)).then_inc(gains_in, 16)
        for L in range(2):
            m = moe_mem[L]
            for dst, src in ((m["gain"][:, :], ffn_norm[L:L + 1, :].partition_broadcast(P)),
                             (m["wr"][:, :, 0:G], router_g[L].rearrange("(p k) n -> p k n", k=K)),
                             (m["wr"][:, :, G:G + NE], router_e[L].rearrange("(p k) n -> p k n", k=K)),
                             (m["br"][:, 0:G], router_g_b[L:L + 1, :].partition_broadcast(P)),
                             (m["br"][:, G:G + NE], router_e_b[L:L + 1, :].partition_broadcast(P))):
                sp.dma_start(dst, src).then_inc(router_in[L], 16)
            load_expert(sp, L, 0, 0, (0, 0), done=ahead[L])
            if L == 0:
                sp.wait_ge(consts, 1)
                sp.dma_start(y_d[LEAST * P:, :].rearrange("(p b) (c n) -> p (b c) n", p=P, n=P),
                             bc(ones[:, :].unsqueeze(1), [P, (BLOCKS - LEAST) * D // P, P])).then_inc(y_cleared, 16)
            sp_moe(sp, L)
            if L == 1:
                break
            proj_load(sp, 0)
            for t in range(T):
                sp.wait_ge(y_added, t + 1)
                sp.dma_start(h_d[t * P:(t + 1) * P, :], h0[:, t, :]).then_inc(h_spilled[t], 16)
                if t in (3, 5, 7):
                    proj_load(sp, (t - 1) // 2)
            for d, row in ((q2_d, HD), (q2_d, HD + 1), (k2_d, HD + 2), (k2_d, HD + 3)):
                sp.dma_start(d[:, row, :].rearrange("h (c n) -> h c n", n=P),
                             ones[0:HEADS, :].unsqueeze(1).to_broadcast([HEADS, S // P, P]))\
                  .then_inc(ones_out, 16)
            sp.wait_ge(hT_ps, T)
            proj_load(sp, 4)
            for half in range(2):
                cols = slice(512 * half, 512 * half + 512)
                sp.wait_ge(f_lo_done, half + 1)
                for row, j, d in ((66, 0, q2_d), (67, 1, q2_d), (64, 2, k2_d), (65, 3, k2_d)):
                    sp.dma_start(d[:, row, cols], stage[0:HEADS, j, :].bitcast(F32)).then_inc(f_out, 16)
            for i in range(5, 7):
                proj_load(sp, i)
            for c in range(8):
                proj_load(sp, 7 + c)
                for u in range(4):
                    n = 4 * c + u
                    i, par = n // 2 % 8, n % 2
                    half = n % 2
                    cols = slice(512 * half, 512 * half + 512)
                    sp.wait_ge(kq_lo_done, n + 1)
                    full, aug = (kh_d, k2_d) if n < 16 else (ql_d, q2_d)
                    jf, ja = (0, 1) if n < 16 else (1, 0)
                    sp.dma_start(full[2 * i:2 * i + 2, :, cols].rearrange("h d n -> (h d) n"),
                                 stage[:, 2 * par + jf, :].bitcast(F32)).then_inc(kq_out[par], 16)
                    for z in range(2):
                        sp.dma_start(aug[2 * i + z, 0:HD, cols],
                                     stage[HD * z:HD * z + HD, 2 * par + ja, :].bitcast(F32)).then_inc(kq_out[par], 16)
                if c == 6:
                    for q in range(2):
                        sp.wait_ge(kq_out[q], 48 * 14)
                    sp.wait_ge(f_out, 128)
                    sp.wait_ge(ones_out, 64)
                    sp.wait_ge(lo_done[PROJ[13][0]], PROJ[13][1] + 1)
                    load_head(sp, 0, 0)
            proj_load(sp, 15)
            for q in range(2):
                sp.wait_ge(kq_out[q], 48 * 16)
            sp.wait_ge(barrier, 4 * 1)
            load_head(sp, 1, 1)
            with sp.Fori(0, HEADS // 2 - 1) as p:
                hd = 2 * p
                sp.wait_ge(qk_ps, hd * T + T)
                load_head(sp, hd + 2, 0)
                sp.wait_ge(qk_ps, hd * T + 2 * T)
                load_head(sp, hd + 3, 1)
            for t in range(T):
                sp.wait_ge(oT_ps, t + 1)
                sp.dma_start(h1[:, t, :], h_d[t * P:(t + 1) * P, :]).then_inc(h_back[t], 16)
        sp.wait_ge(used[1], M_MOE1[1] + BLOCKS)
        sp.dma_start(fin_gain[:, :], final_norm.unsqueeze(0).partition_broadcast(P)).then_inc(gains_in, 16)
        for t in range(T):
            sp.wait_ge(fin_done, t + 1)
            sp.dma_start(out[0, t * P:(t + 1) * P, :], fin_out[:, t % 4, :]).then_inc(out_done[t % 4], 16)
        for q in range(4):
            sp.wait_ge(out_done[q], 16 * T // 4)
        for s in range(3):
            for q in range(2):
                sp.wait_ge(loaded[s][q], 32 * n_loads[s, q])
            for q in range(3):
                sp.wait_ge(block_in[s][q], 2 * 32 * (11, 10, 10)[q])

    n_inv = [0]

    def rsqrt_tile(pool, t):
        n_inv[0] += 1
        pool.wait_ge(sq_done, n_inv[0])
        link(pool, "pool", pool.tensor_scalar(sumsq[:, t:t + 1], sumsq[:, t:t + 1], 1.0 / D, EPS, ALU.mult, ALU.add))
        pool.tensor_tensor(inv[:, t:t + 1], sumsq[:, t:t + 1], halfneg[:, t:t + 1], ALU.pow).then_inc(inv_done, 1)

    def pool_moe(pool, L):
        m = moe_mem[L]
        pool.wait_ge(tok_done, L + 1)
        for q in range(2):
            pool.wait_ge(xn_out[q], 64 * (L + 1))

        def gather(b, par):
            if not isinstance(b, int) or b >= 2:
                pool.wait_ge(xT_ps, L * BLOCKS + b - 1)
            wait_above_zero(pool, idle_done, L * BLOCKS + b, 0)
            pool.tensor_copy(idx_now[:, par:par + 1], m["tok_i"][:, bass.ds(b, 1)]).then_inc(idx_done, 1)
            pool.wait_ge(idx_done, L * BLOCKS + b + 1)
            pool.tensor_tensor(idle[:, :], halfneg[:, 0:1], halfneg[:, 0:1], ALU.add).then_inc(idle_done, 1)
            pool.indirect_dma_start(
                out=m["xg"][:, par, :], out_offset=None, in_=xn_d[:, :],
                in_offset=bass.IndirectOffsetOnAxis(ap=idx_now[:, par:par + 1].bitcast(U32), axis=0),
            ).then_inc(gathered[L][par], 16)

        def body(b, par, place, first, last):
            if not last:
                gather(b + 1, 1 - par)

        def skip(b, par, place, last):
            if not last:
                count(pool, ((idx_done, idle_done), 1))

        gather(0, 0)
        blocks(pool, L, body, skip, skip, lambda b, place: count(pool, ((idx_done, idle_done), 2)), lambda: None)
        pool.wait_ge(y_out[0], 16 * 16 * (L + 1))
        pool.wait_ge(y_out[1], 16 * 15 * (L + 1))

        def gather_y(t):
            if t >= 4:
                pool.wait_ge(y_added, T * L + t - 3)
            for j in range(2):
                pool.indirect_dma_start(
                    out=yg[t % 4][:, j, :], out_offset=None, in_=y_d[:, :],
                    in_offset=bass.IndirectOffsetOnAxis(ap=pos_i[:, j, t:t + 1].bitcast(U32), axis=0),
                ).then_inc(y_back[t % 4], 16)

        for t in range(4):
            gather_y(t)
        for t in range(T):
            if t + 4 < T:
                gather_y(t + 4)
            rsqrt_tile(pool, t)

    @block.gpsimd
    def _(pool):
        pool.memset(halfneg[:, :], -0.5)
        pool.memset(ones[:, :], 1.0)
        pool.memset(ident[:, :], 0.0)
        pool.memset(before[:, :], 1.0)
        pool.memset(upto[:, :], 1.0)
        pool.memset(future_bf[:, :], 0.0)
        for g, w in enumerate(WINDOWS):
            pool.memset(band[:, g, :], 1.0)
            pool.memset(band_prev[:, g, :], 1.0 / w)
        pool.iota(iota_p[:, :], [[1, P]], base=0, channel_multiplier=0, allow_small_or_imprecise_dtypes=True)
        pool.iota(idx_row[:, :], [[1, P]], base=1, channel_multiplier=0, allow_small_or_imprecise_dtypes=True)
        pool.iota(io4[:, :], [[1, 4]], base=-8, channel_multiplier=0, allow_small_or_imprecise_dtypes=True)
        pool.iota(thr[:, :], [[P, T]], base=0, channel_multiplier=0, allow_small_or_imprecise_dtypes=True)
        pool.iota(tok_part[:, :, 0], [[P, T]], base=0, channel_multiplier=0, allow_small_or_imprecise_dtypes=True)
        link(pool, "pool", pool.iota(tok_part[:, :, 1], [[0, T]], base=0, channel_multiplier=1,
                                     allow_small_or_imprecise_dtypes=True))
        row = [[1, P]]
        pool.affine_select(out=ident[:, :], in_=ident[:, :], compare_op=ALU.not_equal, fill=1.0, base=0,
                           pattern=[[-1, P]], channel_multiplier=1)
        pool.affine_select(out=before[:, :], in_=before[:, :], compare_op=ALU.is_gt, fill=0.0, base=0,
                           pattern=row, channel_multiplier=-1)
        pool.affine_select(out=upto[:, :], in_=upto[:, :], compare_op=ALU.is_ge, fill=0.0, base=0,
                           pattern=row, channel_multiplier=-1)
        pool.affine_select(out=future_bf[:, :], in_=future_bf[:, :], compare_op=ALU.is_ge, fill=NEG, base=0,
                           pattern=[[-1, P]], channel_multiplier=1)
        for g, w in enumerate(WINDOWS):
            pool.affine_select(out=band_prev[:, g, :], in_=band_prev[:, g, :], compare_op=ALU.is_ge, fill=0.0,
                               base=w - 1 - P, pattern=[[-1, P]], channel_multiplier=1)
            link(pool, "pool", pool.affine_select(out=band[:, g, :], in_=band[:, g, :], compare_op=ALU.is_ge,
                                                  fill=0.0, base=0, pattern=row, channel_multiplier=-1))
            last = pool.affine_select(out=band[:, g, :], in_=band[:, g, :], compare_op=ALU.is_ge, fill=0.0,
                                      base=w - 1, pattern=[[-1, P]], channel_multiplier=1)
        last.then_inc(consts, 1)
        for t in range(2 * T):
            rsqrt_tile(pool, t % T)
        pool_moe(pool, 0)
        meet(pool, "pool")
        meet(pool, "pool")
        for t in range(T):
            rsqrt_tile(pool, t)
        pool_moe(pool, 1)

    def act_moe(act, L):
        m = moe_mem[L]
        base = M_MOE[L]
        N = L * BLOCKS
        act.wait_ge(lgT_ps, T * (L + 1))
        act.activation(m["lgT"][0:G + NE, :], banks(6, 2)[0:G + NE, :], ACT.Copy).then_inc(lgT_done, 1)
        for j in range(2):
            act.wait_ge(soft_in, 2 * L + j + 1)
            if j == 0:
                act.activation(m["t4"][:, :, :], m["t4"][:, :, :], ACT.Exp).then_inc(soft_out, 1)
            else:
                act.activation(m["e2"][:, :], m["e2"][:, :], ACT.Exp).then_inc(soft_out, 1)

        def xT_hi_(b, par):
            act.wait_ge(xT_ps, N + b + 1)
            if not isinstance(b, int) or b >= 2:
                act.wait_ge(used[1], base[1] + b - 1)
            act.activation(m["xT_hi"][:, par, :], banks(2, 2), ACT.Copy).then_inc(xT_hi_done, 1)

        def aT_hi_(b):
            act.wait_ge(aT_ps, N + b + 1)
            wait_above_zero(act, used[2], base[2] + b, 0)
            act.activation(m["aT_hi"][:, :], ps[:, 4, 0:FE], ACT.Copy).then_inc(aT_hi_done, 1)

        def y_copy(b, par):
            act.wait_ge(used[2], base[2] + b + 1)
            if not isinstance(b, int) or b >= 2:
                act.wait_ge(y_out[par], y_count(L, b, par))
            act.activation(m["y"][:, par, :], banks(5, 2), ACT.Copy).then_inc(y_act, 1)

        mask = fresh_mask(act, L)

        def body(b, par, place, first, last):
            def middle():
                act.wait_ge(used[1], base[1] + b + 1)
                if not first:
                    act.wait_ge(act_done, N + b)
                act.activation(m["silu"][:, :], ps[:, par, 0:FE], ACT.Silu).then_inc(silu_done, 1)

            if not first:
                aT_hi_(b - 1)
            if last:
                middle()
            else:
                xT_hi_(b + 1, 1 - par)
                with act.If(is_fresh(mask, b + 1)):
                    hi_block(act, L, 0, b + 1, later(place, 1))
                    middle()
                    hi_block(act, L, 1, b + 1, later(place, 1))
                with act.Else():
                    count(act, (hi_done[0:1], 1))
                    middle()
                    count(act, (hi_done[1:2], 1))
            with act.If(is_fresh(mask, b)):
                hi_block(act, L, 2, b, place)
            with act.Else():
                count(act, (hi_done[2:3], 1))
            if not first:
                y_copy(b - 1, 1 - par)

        def finish():
            aT_hi_(BLOCKS - 1)
            y_copy(BLOCKS - 1, 0)

        def not_done(last):
            count(act, ((hi_done[2], silu_done), 1))
            if last:
                count(act, ((aT_hi_done, y_act), 1))
            else:
                count(act, ((xT_hi_done, *hi_done[0:2]), 1))

        def flush(b, par, place, last):
            aT_hi_(b - 1)
            y_copy(b - 1, 1 - par)
            not_done(last)

        def skip(b, par, place, last):
            count(act, ((aT_hi_done, y_act), 1))
            not_done(last)

        hi_block(act, L, 0, 0, (0, 0))
        hi_block(act, L, 1, 0, (0, 0))
        xT_hi_(0, 0)
        blocks(act, L, body, flush, skip,
               lambda b, place: count(act, ((aT_hi_done, y_act, silu_done, xT_hi_done, *hi_done), 2)), finish)

    def y_count(L, b, par):
        per = (16, 15)[par] * 16 * L
        return per + 8 * (b - par)

    def router_square(act, L, t):
        if L == 0:
            act.wait_ge(h_done, t + 1)
        else:
            act.wait_ge(op_done, 3 * T + t + 1)
        act.wait_ge(sq_done, T * (1 + 2 * L) + t)
        act.activation(moe_mem[L]["junk"][:, :], (h0, h1)[L][:, t, :], ACT.Square, accum_out=sumsq[:, t:t + 1])\
           .then_inc(sq_done, 1)

    def router_T(act, L, t):
        act.wait_ge(rT_ps, T * L + t + 1)
        wait_above_zero(act, lgT_ps, T * L + t, 0)
        act.activation(moe_mem[L]["rT"][:, :], banks(2, 2), ACT.Copy).then_inc(rT_done, 1)

    @block.scalar
    def _(act):
        act.dma_start(scale_bc[:, :], pool_scale[0:1, :].partition_broadcast(P)).then_inc(scale_in, 16)
        for t in range(T):
            act.wait_ge(x_in[t], 16)
            act.activation(pool_x[:, t, :], h0[:, t, :], ACT.Square, accum_out=sumsq[:, t:t + 1]).then_inc(sq_done, 1)
        act.wait_ge(pool_w_scaled, 1)
        act.activation(w_hi[:, 0, :], raw[:, 0, :], ACT.Copy).then_inc(hi_done[0], 1)
        for t in range(T):
            act.wait_ge(dT_ps, t + 1)
            if t >= 1:
                act.wait_ge(py_ps, t)
            act.activation(dT_hi[:, :, :].rearrange("p k n -> p (k n)"), banks(0, 2), ACT.Copy)\
               .then_inc(dT_hi_done, 1)
            if t >= 1:
                router_square(act, 0, t - 1)
            if t >= 2:
                router_T(act, 0, t - 2)
        router_square(act, 0, T - 1)
        router_T(act, 0, T - 2)
        router_T(act, 0, T - 1)
        act_moe(act, 0)
        hi(act, *PROJ[0], gain_kv)
        for t in range(T + 2):
            if t < T:
                act.wait_ge(y_added, t + 1)
                if t:
                    act.wait_ge(sq_done, 2 * T + t)
                act.activation(square[:, :], h0[:, t, :], ACT.Square, accum_out=sumsq[:, t:t + 1])\
                   .then_inc(sq_done, 1)
            if 1 <= t <= T:
                if t >= 3:
                    act.wait_ge(hT_ps, t - 2)
                act.wait_ge(inv_done, 2 * T + t)
                act.activation(xhat[:, (t - 1) % 2, :], h0[:, t - 1, :], ACT.Copy, scale=inv[:, t - 1:t])\
                   .then_inc(xhat_done, 1)
            if t >= 2:
                act.wait_ge(hT_ps, t - 1)
                act.activation(hT_hi[:, :, (t - 2) * P:(t - 1) * P],
                               banks(2 * (t % 2), 2).rearrange("p (k n) -> p k n", k=K), ACT.Copy)\
                   .then_inc(hT_hi_done, 1)

        def v_copy(c, t):
            n = T * c + t
            act.wait_ge(v_ps, n + 1)
            if c == 0:
                act.wait_ge(h_spilled[t], 16)
                act.wait_ge(xhat_done, t + 1)
            act.activation(val[:, t, c * 256:(c + 1) * 256], ps[:, 4 + n % 4, 0:256], ACT.Copy).then_inc(v_done, 1)

        for t in range(4):
            v_copy(0, t)
        act.wait_ge(y_added, T)
        hi(act, *PROJ[1], gain_kv)
        for t in range(4, T):
            v_copy(0, t)
        act.wait_ge(gains_in, 16 * 4)
        for k in range(K):
            act.activation(wf_hi[:, k, :], wf_raw[:, k, :], ACT.Copy, scale=gain_kv[:, k:k + 1]).then_inc(wf_done, 1)
        hi(act, *PROJ[2], gain_kv)
        hi(act, *PROJ[3], gain_kv)
        act.wait_ge(zf_dve, 1)
        act.activation(zf[0:HEADS, 1, :], zf[0:HEADS, 1, :], ACT.Exp, scale=-1.0).then_inc(zf_act, 1)
        act.wait_ge(zf_act, 1)
        act.activation(zf[0:HEADS, 1, :], zf[0:HEADS, 1, :], ACT.Ln, bias=1.0).then_inc(zf_act, 1)
        for t in range(T):
            v_copy(1, t)
        hi(act, *PROJ[4], gain_kv)
        for half in range(2):
            act.wait_ge(zf_dve, 2)
            if half:
                act.wait_ge(f_out, 64)
                act.wait_ge(f_lo_done, 1)
            act.activation(stage[0:HEADS, 0, :], zf[0:HEADS, 0, 512 * half:512 * half + 512], ACT.Copy)\
               .then_inc(f_hi_done, 1)
        for c in range(2, 4):
            for t in range(T):
                v_copy(c, t)
            hi(act, *PROJ[c + 3], gain_kv)
        hi_next = 7
        for n in range(32):
            act.wait_ge(kq_ps, n + 1)
            if n >= 2:
                act.wait_ge(kq_out[n % 2], 48 * (n // 2))
            elif n == 0:
                act.wait_ge(f_out, 128)
            scale = 1.0 if n < 16 else HD ** -0.5
            act.activation(stage[:, 2 * (n % 2), :], ps[:, n % 4, :], ACT.Copy, scale=scale).then_inc(kq_hi_done, 1)
            if n % 4 == 3 and hi_next < 15:
                g = gain_kv if hi_next < 8 else gain_q if hi_next < 12 else None
                hi(act, *PROJ[hi_next], g)
                hi_next += 1
        meet(act, "act")

        def exp_(hd, i):
            u, q = i % 2, i % 4
            act.wait_ge(max_done, hd * T + i + 1)
            if not isinstance(hd, int) or hd * T + i >= 2:
                act.wait_ge(pT_ps, hd * T + i - 1)
            if not isinstance(hd, int) or hd * T + i >= 4:
                act.wait_ge(rinv_done, hd * T + i - 3)
            n = (ORDER[i] + 1) * P
            act.activation(probs[:, u, 0:n], banks(2 * u, 2)[:, 0:n], ACT.Exp, bias=neg_max[:, q:q + 1],
                           accum_out=row_sum[:, q:q + 1]).then_inc(exp_done, 1)

        def pT_late(hd, i):
            if ORDER[i] >= 4:
                act.wait_ge(pT_ps, hd * T + i + 1)
                wait_above_zero(act, pv_ps, hd * T + i, -1)
                n = (ORDER[i] - 3) * P
                act.activation(probsT[:, i % 2, 512:512 + n], ps[:, 5, 0:n], ACT.Copy).then_inc(pT_act, 1)

        def pair(hd, last):
            for j in range(2):
                for i in range(T):
                    if i < T - 1:
                        exp_(hd + j, i + 1)
                    elif not (last and j == 1):
                        exp_(hd + j + 1, 0)
                    pT_late(hd + j, i)

        for s, m in (PROJ[10], PROJ[11]):
            act.wait_ge(lo_done[s], m + 1)
        exp_(0, 0)
        pair(0, False)
        with act.Fori(1, HEADS // 2 - 1) as p:
            pair(2 * p, False)
        pair(HEADS - 2, True)
        meet(act, "act")
        for t in range(T):
            act.wait_ge(oT_ps, t + 1)
            act.activation(oT_hi[:, :, t * P:(t + 1) * P], banks(2 * (t % 2), 2).rearrange("p (k n) -> p k n", k=K),
                           ACT.Copy).then_inc(oT_hi_done, 1)
        hi(act, *PROJ[15])
        for t in range(T):
            router_square(act, 1, t)
            if t >= 1:
                router_T(act, 1, t - 1)
        router_T(act, 1, T - 1)
        act_moe(act, 1)
        for t in range(T):
            act.wait_ge(y_added, T + t + 1)
            if t:
                act.wait_ge(sq_done, 4 * T + t)
            act.activation(fin_junk[:, :], h1[:, t, :], ACT.Square, accum_out=sumsq[:, t:t + 1]).then_inc(sq_done, 1)

    def router_norm(dve, L, t):
        m = moe_mem[L]
        if t == 0:
            dve.wait_ge(router_in[L], 16 * 5)
        dve.wait_ge(inv_done, T * (1 + 2 * L) + t + 1)
        if t >= 2:
            dve.wait_ge(xn_out[t % 2], 64 * L + 16 * (t // 2))
            dve.wait_ge(rT_ps, T * L + t - 1)
        dve.scalar_tensor_tensor(out=m["xn"][:, t % 2, :], in0=(h0, h1)[L][:, t, :], scalar=inv[:, t:t + 1],
                                 in1=m["gain"][:, :], op0=ALU.mult, op1=ALU.mult).then_inc(xn_done, 1)

    def dve_moe(dve, L, follow):
        m = moe_mem[L]
        base = M_MOE[L]
        N = L * BLOCKS
        h = (h0, h1)[L]

        def do(ins):
            link(dve, "dve", ins)

        dve.wait_ge(lg_ps, L + 1)
        do(dve.memset(m["zero"][:, :], 0.0))
        for n in range(NB // 2):
            ins = dve.memset(m["bit"][:, n:NB:NB // 2], 2.0 ** n)
        do(ins)
        do(dve.memset(m["cum"][:, 0, :], 0.0))
        lg, gl = m["lg"], m["lg"][:, :, 0:G]
        el = m["lg"][:, :, G:G + NE].rearrange("p t (g e) -> p t g e", g=G)
        do(dve.tensor_tensor(lg[:, :, :], ps[:, 5, 0:T * (G + NE)].rearrange("p (t n) -> p t n", t=T),
                             bc(m["br"][:, :].unsqueeze(1), [P, T, G + NE]), ALU.add))

        def first_max(values, top, index, one_hot):
            do(dve.tensor_reduce(top[:, :], values, AX.X, ALU.max))
            do(dve.tensor_tensor(one_hot, values, bc(top[:, :].unsqueeze(2), [P, T, 4]), ALU.is_ge))
            do(dve.tensor_tensor(one_hot, one_hot, bc(io4[:, :].unsqueeze(1), [P, T, 4]), ALU.mult))
            do(dve.tensor_reduce(index[:, :], one_hot, AX.X, ALU.min))
            do(dve.tensor_tensor(one_hot, bc(io4[:, :].unsqueeze(1), [P, T, 4]),
                                 bc(index[:, :].unsqueeze(2), [P, T, 4]), ALU.is_equal))

        first_max(gl, m["gm"], m["gi"], m["og"][:, :, :])
        do(dve.tensor_tensor(m["t4"][:, :, :], gl, bc(m["gm"][:, :].unsqueeze(2), [P, T, G]), ALU.subtract))
        dve.sem_inc(soft_in, 1)
        t16 = m["t16"][:, :, :].rearrange("p t (g e) -> p t g e", g=G)
        do(dve.tensor_tensor(t16, el, bc(m["og"][:, :, :].unsqueeze(3), [P, T, G, E]), ALU.mult))
        do(dve.tensor_reduce(m["es"][:, :, :], m["t16"][:, :, :].rearrange("p t (g e) -> p t e g", g=G), AX.X, ALU.add))
        first_max(m["es"][:, :, :], m["m1"], m["gi"], m["o1"][:, :, :])
        do(dve.scalar_tensor_tensor(out=m["es"][:, :, :], in0=m["o1"][:, :, :], scalar=3 * NEG, in1=m["es"][:, :, :],
                                    op0=ALU.mult, op1=ALU.add))
        first_max(m["es"][:, :, :], m["m2"], m["gi"], m["o2"][:, :, :])
        do(dve.tensor_tensor(m["e2"][:, :], m["m2"][:, :], m["m1"][:, :], ALU.subtract))
        dve.sem_inc(soft_in, 1)
        for s_, o_ in (("s1", "o1"), ("s2", "o2")):
            do(dve.tensor_tensor(m[s_][:, :, :].rearrange("p t (g e) -> p t g e", g=G),
                                 bc(m["og"][:, :, :].unsqueeze(3), [P, T, G, E]),
                                 bc(m[o_][:, :, :].unsqueeze(2), [P, T, G, E]), ALU.mult))
        do(dve.tensor_tensor(m["sel"][:, :, :], m["s1"][:, :, :], m["s2"][:, :, :], ALU.add))
        for t in range(T):
            do(dve.tensor_tensor(m["cum"][:, t + 1, :], m["cum"][:, t, :], m["sel"][:, t, :], ALU.add))
        dve.sem_inc(sel_done, 1)
        dve.wait_ge(rank_ps, L + 1)
        cmp_ = m["cmp"][:, 0:NE * T].rearrange("p (e t) -> p e t", e=NE)
        do(dve.tensor_tensor(cmp_, bc(ps[:, 6, P:P + NE].unsqueeze(2), [P, NE, T]),
                             bc(thr[:, :].unsqueeze(1), [P, NE, T]), ALU.is_gt))
        do(dve.tensor_reduce(m["nb"][:, :], cmp_, AX.X, ALU.add))
        do(dve.tensor_tensor_scan(m["end"][:, :], m["nb"][:, :], m["zero"][:, :], 0.0, ALU.add, ALU.add))
        do(dve.tensor_tensor(m["base"][:, :], m["end"][:, :], m["nb"][:, :], ALU.subtract))
        do(dve.scalar_tensor_tensor(out=m["pf"][:, :, :], in0=bc(m["base"][:, :].unsqueeze(1), [P, T, NE]),
                                    scalar=float(P), in1=ps[:, 6, 0:P].rearrange("p (t e) -> p t e", t=T),
                                    op0=ALU.mult, op1=ALU.add))
        for j, s_ in enumerate(("s1", "s2")):
            do(dve.tensor_tensor(m["t16"][:, :, :], m["pf"][:, :, :], m[s_][:, :, :], ALU.mult))
            do(dve.tensor_reduce(m["pos"][:, j, :], m["t16"][:, :, :], AX.X, ALU.add))
        do(dve.tensor_copy(pos_i[:, :, :], m["pos"][:, :, :]))
        flat_i = pos_i[:, :, :].rearrange("p j t -> p (j t)")
        do(dve.tensor_scalar(m["part_i"][:, 0, :], flat_i, P - 1, None, ALU.bitwise_and))
        do(dve.tensor_scalar(m["part_i"][:, 1, :], flat_i, 7, None, ALU.arith_shift_right))
        do(dve.tensor_copy(m["part"][:, :, :], m["part_i"][:, :, :]))
        do(dve.tensor_tensor(m["slot_of"][:, :, :], bc(iota_p[:, :].unsqueeze(1), [P, 2 * T, P]),
                             bc(m["part"][:, 0, :].unsqueeze(2), [P, 2 * T, P]), ALU.is_equal))
        do(dve.tensor_tensor(m["blk_of"][:, :, :], bc(iota_p[:, 0:NB].unsqueeze(1), [P, 2 * T, NB]),
                             bc(m["part"][:, 1, :].unsqueeze(2), [P, 2 * T, NB]), ALU.is_equal))
        for j in range(2):
            ins = dve.tensor_tensor(m["tok_of"][:, j * T:(j + 1) * T, :, :],
                                    bc(m["blk_of"][:, j * T:(j + 1) * T, :].unsqueeze(2), [P, T, 2, NB]),
                                    bc(tok_part[:, :, :].unsqueeze(3), [P, T, 2, NB]), ALU.mult)
            ins.then_inc(slots_done, 1)
        cmp2 = m["cmp"][:, :].rearrange("p (b e) -> p b e", e=NE)
        do(dve.tensor_tensor(cmp2, bc(iota_p[:, 0:NB].unsqueeze(2), [P, NB, NE]),
                             bc(m["end"][:, :].unsqueeze(1), [P, NB, NE]), ALU.is_ge))
        do(dve.tensor_reduce(m["tab"][:, 1, :], cmp2, AX.X, ALU.add))
        dve.wait_ge(tok_ps, L + 1)
        do(dve.tensor_copy(m["tok"][:, :], ps[:, 6, 256:256 + NB]))
        dve.tensor_tensor(m["tok_i"][:, :], m["tok"][:, :], ps[:, 6, 256 + NB:256 + 2 * NB], ALU.add)\
           .then_inc(tok_done, 1)
        do(dve.tensor_scalar(m["tab"][:, 0, :], m["tab"][:, 1, :], float(NE - 1), None, ALU.min))
        do(dve.tensor_tensor(m["tab"][:, 1, 1:NB], m["tab"][:, 0, 1:NB], m["tab"][:, 0, 0:NB - 1], ALU.not_equal))
        do(dve.memset(m["tab"][:, 1, 0:1], 1.0))
        do(dve.scalar_tensor_tensor(out=m["tab"][:, 1, :], in0=iota_p[:, 0:NB], scalar=m["end"][:, NE - 1:NE],
                                    in1=m["tab"][:, 1, :], op0=ALU.is_lt, op1=ALU.mult))
        do(dve.tensor_copy(m["tab"][:, 2, :], bc(m["end"][:, NE - 1:NE], [P, NB])))
        do(dve.tensor_tensor(m["bit"][:, :], m["bit"][:, :], m["tab"][:, 1, :], ALU.mult))
        do(dve.tensor_reduce(m["tab"][:, 2, 1:3], m["bit"][:, :].rearrange("p (h n) -> p h n", h=2), AX.X, ALU.add))
        do(dve.tensor_scalar(m["tab"][:, 1, 0:1], m["tab"][:, 0, 0:1], 0.0, None, ALU.not_equal))
        dve.tensor_copy(m["tab_i"][:, :, :], m["tab"][:, :, :]).then_inc(eid_done, 1)

        def combine_weights():
            dve.wait_ge(soft_out, 2 * L + 1)
            do(dve.tensor_reduce(m["gw"][:, :], m["t4"][:, :, :], AX.X, ALU.add))
            do(dve.reciprocal(m["gw"][:, :], m["gw"][:, :]))
            dve.wait_ge(soft_out, 2 * L + 2)
            do(dve.tensor_scalar(m["m1"][:, :], m["e2"][:, :], 1.0, None, ALU.add))
            do(dve.reciprocal(m["m1"][:, :], m["m1"][:, :]))
            do(dve.tensor_tensor(wt[:, 0, :], m["m1"][:, :], m["gw"][:, :], ALU.mult))
            do(dve.tensor_tensor(wt[:, 1, :], wt[:, 0, :], m["e2"][:, :], ALU.mult))

        def xT_lo_(b, par):
            dve.wait_ge(xT_hi_done, N + b + 1)
            dve.tensor_tensor(m["xT_lo"][:, par, :], banks(2, 2), m["xT_hi"][:, par, :].bitcast(F32), ALU.subtract)\
               .then_inc(xT_lo_done, 1)

        def aT_lo_(b):
            dve.wait_ge(aT_hi_done, N + b + 1)
            dve.tensor_tensor(m["aT_lo"][:, :], ps[:, 4, 0:FE], m["aT_hi"][:, :].bitcast(F32), ALU.subtract)\
               .then_inc(aT_lo_done, 1)

        mask = fresh_mask(dve, L)

        def body(b, par, place, first, last):
            def middle():
                dve.wait_ge(silu_done, N + b + 1)
                if not first:
                    dve.wait_ge(aT_ps, N + b)
                dve.tensor_tensor(m["act"][:, :], m["silu"][:, :], ps[:, par, FE:2 * FE], ALU.mult)\
                   .then_inc(act_done, 1)

            if not first:
                aT_lo_(b - 1)
            if last:
                middle()
            else:
                xT_lo_(b + 1, 1 - par)
                with dve.If(is_fresh(mask, b + 1)):
                    lo_block(dve, L, 0, b + 1, later(place, 1))
                    middle()
                    lo_block(dve, L, 1, b + 1, later(place, 1))
                with dve.Else():
                    count(dve, (lo_done[0:1], 1))
                    middle()
                    count(dve, (lo_done[1:2], 1))
            with dve.If(is_fresh(mask, b)):
                lo_block(dve, L, 2, b, place)
            with dve.Else():
                count(dve, (lo_done[2:3], 1))

        def not_done(last):
            count(dve, ((lo_done[2], act_done), 1))
            count(dve, ((aT_lo_done,) if last else (xT_lo_done, *lo_done[0:2]), 1))

        def flush(b, par, place, last):
            aT_lo_(b - 1)
            not_done(last)

        def skip(b, par, place, last):
            count(dve, ((aT_lo_done,), 1))
            not_done(last)

        combine_weights()
        lo_block(dve, L, 0, 0, (0, 0))
        lo_block(dve, L, 1, 0, (0, 0))
        xT_lo_(0, 0)
        blocks(dve, L, body, flush, skip,
               lambda b, place: count(dve, ((aT_lo_done, act_done, xT_lo_done, *lo_done), 2)),
               lambda: aT_lo_(BLOCKS - 1))
        for t in range(T):
            dve.wait_ge(y_back[t % 4], 64 * L + 32 * (t // 4 + 1))
            for j in range(2):
                ins = dve.scalar_tensor_tensor(out=h[:, t, :], in0=yg[t % 4][:, j, :],
                                               scalar=wt[:, j, t:t + 1], in1=h[:, t, :],
                                               op0=ALU.mult, op1=ALU.add)
                if j == 0:
                    do(ins)
            ins.then_inc(y_added, 1)
            follow(t)

    @block.vector
    def _(dve):
        def do(ins):
            link(dve, "dve", ins)

        dve.wait_ge(consts, 1)
        do(dve.tensor_copy(ident_bf[:, :], ident[:, :]))
        head = WINDOWS[-1]
        for g, w in enumerate(WINDOWS):
            dve.scalar_tensor_tensor(out=band0[:, g, head:P], in0=band[:, g, head:P], scalar=1.0 / w,
                                     in1=ident[:, head:P], op0=ALU.mult, op1=ALU.subtract)
            do(dve.tensor_scalar(band0[:, g, 0:head], idx_row[:, 0:head], float(w), None, ALU.min))
            do(dve.reciprocal(band0[:, g, 0:head], band0[:, g, 0:head]))
            do(dve.tensor_tensor(band0[:, g, 0:head], band0[:, g, 0:head], band[:, g, 0:head], ALU.mult))
            do(dve.tensor_tensor(band0[:, g, 0:head], band0[:, g, 0:head], ident[:, 0:head], ALU.subtract))
            ins = dve.scalar_tensor_tensor(out=band[:, g, :], in0=band[:, g, :], scalar=1.0 / w, in1=ident[:, :],
                                           op0=ALU.mult, op1=ALU.subtract)
        ins.then_inc(consts, 1)

        def normed(t):
            dve.wait_ge(inv_done, t + 1)
            dve.scalar_tensor_tensor(out=pool_x[:, t, :], in0=h0[:, t, :], scalar=inv[:, t:t + 1],
                                     in1=gain_bc0[:, :], op0=ALU.mult, op1=ALU.mult).then_inc(poolx_done, 1)

        dve.wait_ge(mix_in, 16)
        normed(0)
        dve.wait_ge(scale_in, 16)
        dve.wait_ge(loaded[0][0], 32)
        for c in range(2):
            rw = raw[:, 0, :].rearrange("p (g c d) -> p g c d", g=4, c=2)[:, :, c, :]
            ins = dve.tensor_tensor(rw, rw, scale_bc[:, :].rearrange("p (g d) -> p g d", g=4), ALU.mult)
            do(ins) if c == 0 else ins.then_inc(pool_w_scaled, 1)
        normed(1)
        dve.wait_ge(hi_done[0], 1)
        dve.tensor_tensor(w_lo[:, 0, :], raw[:, 0, :], w_hi[:, 0, :].bitcast(F32), ALU.subtract).then_inc(lo_done[0], 1)
        for t in range(T):
            dve.wait_ge(dT_hi_done, t + 1)
            dve.tensor_tensor(dT_lo[:, :, :].rearrange("p k n -> p (k n)"), banks(0, 2),
                              dT_hi[:, :, :].rearrange("p k n -> p (k n)").bitcast(F32), ALU.subtract)\
               .then_inc(dT_lo_done, 1)
            if t >= 1:
                router_norm(dve, 0, t - 1)
            dve.wait_ge(py_ps, t + 1)
            dve.tensor_tensor(h0[:, t, :], h0[:, t, :], banks(4, 2), ALU.add).then_inc(h_done, 1)
            if t + 2 < T:
                normed(t + 2)
        router_norm(dve, 0, T - 1)

        def hT_lo_(t):
            dve.wait_ge(hT_hi_done, t + 1)
            dve.tensor_tensor(hT_lo[:, :, t * P:(t + 1) * P], banks(2 * (t % 2), 2).rearrange("p (k n) -> p k n", k=K),
                              hT_hi[:, :, t * P:(t + 1) * P].bitcast(F32), ALU.subtract).then_inc(hT_lo_done, 1)

        def after_sum(t):
            if t == 1:
                lo(dve, *PROJ[0], gain_kv)
            if t >= 3:
                hT_lo_(t - 3)

        dve_moe(dve, 0, after_sum)
        for t in range(T - 3, T):
            hT_lo_(t)
        lo(dve, *PROJ[1], gain_kv)
        for k in range(K):
            dve.wait_ge(wf_done, K)
            dve.scalar_tensor_tensor(out=wf_lo[:, k, :], in0=wf_raw[:, k, :], scalar=gain_kv[:, k:k + 1],
                                     in1=wf_hi[:, k, :].bitcast(F32), op0=ALU.mult, op1=ALU.subtract)\
               .then_inc(wf_done, 1)
        lo(dve, *PROJ[2], gain_kv)
        lo(dve, *PROJ[3], gain_kv)
        dve.wait_ge(z_ps, 1)
        z, lf, ln_ = banks(0, 2)[0:HEADS, :], zf[0:HEADS, 0, :], zf[0:HEADS, 1, :]
        do(dve.tensor_scalar(lf, z, bf_col[0:HEADS, :], None, ALU.add))
        do(dve.scalar_tensor_tensor(out=ln_, in0=lf, scalar=-1.0, in1=lf, op0=ALU.mult, op1=ALU.max))
        dve.sem_inc(zf_dve, 1)
        do(dve.tensor_scalar(lf, lf, 0.0, None, ALU.min))
        dve.wait_ge(zf_act, 2)
        dve.tensor_tensor_scan(lf, lf, ln_, 0.0, ALU.add, ALU.subtract).then_inc(zf_dve, 1)
        lo(dve, *PROJ[4], gain_kv)
        for half in range(2):
            dve.wait_ge(f_hi_done, half + 1)
            if half:
                dve.wait_ge(f_out, 64)
            do(dve.tensor_tensor(stage[0:HEADS, 1, :], lf[:, 512 * half:512 * half + 512],
                                 stage[0:HEADS, 0, :].bitcast(F32), ALU.subtract))
            do(dve.tensor_scalar(stage[0:HEADS, 2, :], stage[0:HEADS, 0, :].bitcast(F32), -1.0, None, ALU.mult))
            dve.tensor_scalar(stage[0:HEADS, 3, :], stage[0:HEADS, 1, :].bitcast(F32), -1.0, None, ALU.mult)\
               .then_inc(f_lo_done, 1)
        for i in range(5, 7):
            lo(dve, *PROJ[i], gain_kv)
        lo_next = 7
        for n in range(32):
            dve.wait_ge(kq_hi_done, n + 1)
            scale = 1.0 if n < 16 else HD ** -0.5
            dve.scalar_tensor_tensor(out=stage[:, 2 * (n % 2) + 1, :], in0=ps[:, n % 4, :], scalar=scale,
                                     in1=stage[:, 2 * (n % 2), :].bitcast(F32), op0=ALU.mult, op1=ALU.subtract)\
               .then_inc(kq_lo_done, 1)
            if n % 4 == 3 and lo_next < 15:
                g = gain_kv if lo_next < 8 else gain_q if lo_next < 12 else None
                lo(dve, *PROJ[lo_next], g)
                lo_next += 1
        meet(dve, "dve")

        def max_(hd, i):
            u, q = i % 2, i % 4
            dve.wait_ge(qk_ps, hd * T + i + 1)
            if not isinstance(hd, int) or hd * T + i >= 4:
                dve.wait_ge(exp_done, hd * T + i - 3)
            dve.tensor_reduce(neg_max[:, q:q + 1], banks(2 * u, 2)[:, 0:(ORDER[i] + 1) * P], AX.X, ALU.max,
                              negate=True).then_inc(max_done, 1)

        def pT_early(hd, i):
            dve.wait_ge(pT_ps, hd * T + i + 1)
            n = min(ORDER[i] + 1, 4) * P
            dve.tensor_copy(probsT[:, i % 2, 0:n], ps[:, 4, 0:n]).then_inc(pT_dve, 1)

        def o_(hd, i):
            u, q = i % 2, i % 4
            dve.reciprocal(row_inv[:, u:u + 1], row_sum[:, q:q + 1]).then_inc(rinv_done, 1)
            dve.wait_ge(pv_ps, hd * T + i + 1)
            dve.wait_ge(rinv_done, hd * T + i + 1)
            dve.tensor_scalar(o_tok[:, ORDER[i], bass.ds(hd * HD, HD)], ps[:, 6 + u, 0:HD], row_inv[:, u:u + 1], None,
                              ALU.mult).then_inc(o_done, 1)

        def pair(hd, first, last):
            for j in range(2):
                for i in range(T):
                    if i < T - 1:
                        max_(hd + j, i + 1)
                    elif not (last and j == 1):
                        max_(hd + j + 1, 0)
                    pT_early(hd + j, i)
                    if i:
                        o_(hd + j, i - 1)
                    elif not (first and j == 0):
                        o_(hd + j - 1, T - 1)

        max_(0, 0)
        pair(0, True, False)
        with dve.Fori(1, HEADS // 2 - 1) as p:
            pair(2 * p, False, False)
        pair(HEADS - 2, False, True)
        o_(HEADS - 1, T - 1)
        meet(dve, "dve")

        def oT_lo_(t):
            dve.wait_ge(oT_hi_done, t + 1)
            dve.tensor_tensor(oT_lo[:, :, t * P:(t + 1) * P], banks(2 * (t % 2), 2).rearrange("p (k n) -> p k n", k=K),
                              oT_hi[:, :, t * P:(t + 1) * P].bitcast(F32), ALU.subtract).then_inc(oT_lo_done, 1)

        oT_lo_(0)
        oT_lo_(1)
        for c in range(4):
            if c == 1:
                lo(dve, *PROJ[15])
            for t in range(T):
                n = T * c + t
                if c == 0:
                    if t + 2 < T:
                        oT_lo_(t + 2)
                    dve.wait_ge(h_back[t], 16)
                if c == 3 and t >= 1:
                    router_norm(dve, 1, t - 1)
                dve.wait_ge(op_ps, n + 1)
                hv = h1[:, t, c * 256:(c + 1) * 256]
                dve.tensor_tensor(hv, hv, ps[:, 4 + n % 2, 0:256], ALU.add).then_inc(op_done, 1)
        router_norm(dve, 1, T - 1)

        def final(t):
            dve.wait_ge(inv_done, 4 * T + t + 1)
            if t == 0:
                dve.wait_ge(gains_in, 16 * 5)
            if t >= 4:
                dve.wait_ge(out_done[t % 4], 16)
            dve.scalar_tensor_tensor(out=fin_out[:, t % 4, :], in0=h1[:, t, :], scalar=inv[:, t:t + 1],
                                     in1=fin_gain[:, :], op0=ALU.mult, op1=ALU.mult).then_inc(fin_done, 1)

        dve_moe(dve, 1, lambda t: final(t - 1) if t else None)
        final(T - 1)

    def transposes(pe, src, bank, n):
        dst = banks(bank, 2) if n * P > 512 else ps[:, bank, :]
        for k in range(n):
            ins = pe.transpose(dst[:, k * P:(k + 1) * P], src[:, k:n * P:n], ident[:, :])
        return ins

    def router_turn(pe, L, t):
        pe.wait_ge(xn_done, T * L + t + 1)
        wait_above_zero(pe, rT_done, T * L + t, 0)
        transposes(pe, moe_mem[L]["xn"][:, t % 2, :], 2, K).then_inc(rT_ps, 1)

    def router_logits(pe, L, t):
        if t == 0:
            pe.wait_ge(router_in[L], 16 * 5)
        pe.wait_ge(rT_done, T * L + t + 1)
        for k in range(K):
            ins = pe.matmul(banks(6, 2)[0:G + NE, t * P:(t + 1) * P], moe_mem[L]["wr"][:, k, :],
                            moe_mem[L]["rT"][:, k * P:(k + 1) * P], start=(k == 0), stop=(k == K - 1))
        ins.then_inc(lgT_ps, 1)

    def pe_moe(pe, L):
        m = moe_mem[L]
        base = M_MOE[L]
        N = L * BLOCKS
        pe.wait_ge(lgT_done, L + 1)
        for t in range(T):
            ins = pe.transpose(ps[:, 5, t * (G + NE):(t + 1) * (G + NE)], m["lgT"][0:G + NE, t * P:(t + 1) * P],
                               ident[0:G + NE, 0:G + NE])
        ins.then_inc(lg_ps, 1)
        pe.wait_ge(sel_done, L + 1)
        sel = m["sel"][:, :, :].rearrange("p t e -> p (t e)")
        cum = m["cum"][:, 0:T, :].rearrange("p t e -> p (t e)")
        pe.matmul(ps[:, 6, 0:P], before[:, :], sel, start=True, stop=False)
        pe.matmul(ps[:, 6, 0:P], ones[:, :], cum, start=False, stop=True)
        pe.matmul(ps[:, 6, P:P + NE], ones[:, :], m["cum"][:, T, :], start=True, stop=True).then_inc(rank_ps, 1)
        pe.wait_ge(slots_done, 2 * L + 2)
        for j in range(2 * T):
            ins = pe.matmul(ps[:, 6, 256:256 + 2 * NB], m["slot_of"][:, j, :],
                            m["tok_of"][:, j, :, :].rearrange("p h n -> p (h n)"),
                            start=(j == 0), stop=(j == 2 * T - 1))
        ins.then_inc(tok_ps, 1)

        def xT(b, par):
            pe.wait_ge(gathered[L][par], 8 * (b - par) + 16)
            wait_above_zero(pe, xT_lo_done, N + b, 0)
            transposes(pe, m["xg"][:, par, :], 2, K).then_inc(xT_ps, 1)

        def gate_up(b, par, s):
            pe.wait_ge(lo_done[s], base[s] + b + 1)
            if s == 0:
                pe.wait_ge(xT_lo_done, N + b + 1)
                if not isinstance(b, int) or b >= 2:
                    pe.wait_ge(act_done, N + b - 1)
            o = ps[:, par, :].rearrange("p (j f) -> p j f", j=2)
            for k in range(4):
                kk = 4 * s + k
                wh = w_hi[:, s, :].rearrange("p (j k f) -> p j k f", j=2, k=4)[:, :, k, :]
                wl = w_lo[:, s, :].rearrange("p (j k f) -> p j k f", j=2, k=4)[:, :, k, :]
                ins = three(pe, o, m["xT_hi"][:, par, kk * P:(kk + 1) * P], m["xT_lo"][:, par, kk * P:(kk + 1) * P],
                            wh, wl, kk == 0, kk == K - 1)
            ins.then_inc(used[s], 1)

        def aT(b):
            pe.wait_ge(act_done, N + b + 1)
            wait_above_zero(pe, aT_lo_done, N + b, 0)
            transposes(pe, m["act"][:, :], 4, KF).then_inc(aT_ps, 1)

        def down(b):
            pe.wait_ge(lo_done[2], base[2] + b + 1)
            pe.wait_ge(aT_lo_done, N + b + 1)
            if not isinstance(b, int) or b >= 1:
                pe.wait_ge(y_act, N + b)
            for k in range(KF):
                for half in range(2):
                    c = slice(1024 * k + 512 * half, 1024 * k + 512 * half + 512)
                    ins = three(pe, ps[:, 5 + half, :], m["aT_hi"][:, k * P:(k + 1) * P],
                                m["aT_lo"][:, k * P:(k + 1) * P], w_hi[:, 2, c], w_lo[:, 2, c], k == 0, k == KF - 1)
            ins.then_inc(used[2], 1)

        def body(b, par, place, first, last):
            gate_up(b, par, 0)
            if not first:
                aT(b - 1)
            if not last:
                xT(b + 1, 1 - par)
            gate_up(b, par, 1)
            if not first:
                down(b - 1)

        def finish():
            aT(BLOCKS - 1)
            down(BLOCKS - 1)

        def not_done(last):
            count(pe, (used[0:2], 1))
            count(pe, ((aT_ps, used[2]) if last else (xT_ps,), 1))

        def flush(b, par, place, last):
            aT(b - 1)
            down(b - 1)
            not_done(last)

        def skip(b, par, place, last):
            count(pe, ((aT_ps, used[2]), 1))
            not_done(last)

        xT(0, 0)
        blocks(pe, L, body, flush, skip, lambda b, place: count(pe, ((aT_ps, xT_ps, *used), 2)), finish)

    @block.tensor
    def _(pe):
        pe.wait_ge(consts, 2)

        def pooled(t):
            pe.wait_ge(poolx_done, t + 1)
            if t >= 1:
                pe.wait_ge(dT_lo_done, t)
            for c in range(K):
                g = c // 2
                o = banks(0, 2)[:, c * P:(c + 1) * P]
                ins = pe.matmul(o, pool_x[:, t, c * P:(c + 1) * P], (band if t else band0)[:, g, :],
                                start=True, stop=(t == 0))
                if t:
                    ins = pe.matmul(o[:, 0:REACH], pool_x[:, t - 1, c * P:(c + 1) * P],
                                    band_prev[:, g, 0:REACH], start=False, stop=True)
            ins.then_inc(dT_ps, 1)

        pooled(0)
        for t in range(T):
            pe.wait_ge(dT_lo_done, t + 1)
            if t == 0:
                pe.wait_ge(lo_done[0], 1)
            if t >= 1:
                pe.wait_ge(h_done, t)
            for g in range(4):
                o = banks(4, 2)[:, g * GW:(g + 1) * GW]
                for c in range(2):
                    w = slice((2 * g + c) * GW, (2 * g + c + 1) * GW)
                    ins = three(pe, o, dT_hi[:, 2 * g + c, :], dT_lo[:, 2 * g + c, :], w_hi[:, 0, w], w_lo[:, 0, w],
                                c == 0, c == 1)
            ins.then_inc(py_ps, 1)
            if t + 1 < T:
                pooled(t + 1)
            if t >= 1:
                router_turn(pe, 0, t - 1)
            if t >= 2:
                router_logits(pe, 0, t - 2)
        pe.drain().then_inc(used[0], 1)
        router_logits(pe, 0, T - 2)
        router_turn(pe, 0, T - 1)
        router_logits(pe, 0, T - 1)
        pe_moe(pe, 0)
        def v_tile(c, t):
            s, mm = PROJ[c]
            n = T * c + t
            if n >= 4:
                pe.wait_ge(v_done, n - 3)
            for k in range(K):
                w = slice(k * 256, (k + 1) * 256)
                ins = three(pe, ps[:, 4 + n % 4, 0:256], hT_hi[:, k, t * P:(t + 1) * P],
                            hT_lo[:, k, t * P:(t + 1) * P], w_hi[:, s, w], w_lo[:, s, w], k == 0, k == K - 1)
            ins.then_inc(v_ps, 1)

        for t in range(T + 3):
            if t < T:
                pe.wait_ge(xhat_done, t + 1)
                if t >= 2:
                    pe.wait_ge(hT_lo_done, t - 1)
                transposes(pe, xhat[:, t % 2, :], 2 * (t % 2), K).then_inc(hT_ps, 1)
            if t == 3:
                pe.wait_ge(lo_done[PROJ[0][0]], PROJ[0][1] + 1)
            if t >= 3:
                pe.wait_ge(hT_lo_done, t - 2)
                v_tile(0, t - 3)
        pe.drain().then_inc(used[PROJ[0][0]], 1)
        pe.wait_ge(wf_done, 2 * K)
        for half in range(2):
            tok = slice(512 * half, 512 * half + 512)
            for k in range(K):
                ins = three(pe, ps[0:HEADS, half, :], wf_hi[:, k, :], wf_lo[:, k, :], hT_hi[:, k, tok],
                            hT_lo[:, k, tok], k == 0, k == K - 1)
        ins.then_inc(z_ps, 1)
        for c in range(1, 4):
            s, mm = PROJ[c]
            pe.wait_ge(lo_done[s], mm + 1)
            for t in range(T):
                v_tile(c, t)
            pe.drain().then_inc(used[s], 1)
        for c in range(8):
            s, mm = PROJ[4 + c]
            pe.wait_ge(lo_done[s], mm + 1)
            for r in range(2):
                for half in range(2):
                    n = 4 * c + 2 * r + half
                    if n >= 4:
                        pe.wait_ge(kq_lo_done, n - 3)
                    elif n == 0:
                        pe.wait_ge(zf_dve, 1)
                    for k in range(K):
                        w = slice(k * 256 + r * P, k * 256 + (r + 1) * P)
                        tok = slice(512 * half, 512 * half + 512)
                        ins = three(pe, ps[:, n % 4, :], w_hi[:, s, w], w_lo[:, s, w], hT_hi[:, k, tok],
                                    hT_lo[:, k, tok], k == 0, k == K - 1)
                    ins.then_inc(kq_ps, 1)
            pe.drain().then_inc(used[s], 1)
        meet(pe, "pe")

        def scores(hd, hpar, u, i):
            if i == 0:
                pe.wait_ge(head_in[hpar], 48 * (hd - hpar) + 96)
            if not isinstance(hd, int) or hd * T + i >= 2:
                pe.wait_ge(exp_done, hd * T + i - 1)
            q1, q2, k1, k2 = heads_mem[hpar]
            q = ORDER[i]
            tt = slice(q * P, (q + 1) * P)
            n = (q + 1) * P
            for c in range(0, n, 512):
                w = min(512, n - c)
                o = banks(2 * u, 2)[:, c:c + w]
                last = c + w == n
                pe.matmul(o, q1[:, tt], k1[:, c:c + w], start=True, stop=False)
                pe.matmul(o, q2[0:HK, tt], k2[0:HK, c:c + w], start=False, stop=not last)
            pe.matmul(banks(2 * u, 2)[:, q * P:n], ident_bf[:, :], future_bf[:, :], start=False, stop=True)\
              .then_inc(qk_ps, 1)

        def turn(hd, i):
            pe.wait_ge(exp_done, hd * T + i + 1)
            if not isinstance(hd, int) or hd * T + i >= 1:
                pe.wait_ge(pT_dve, hd * T + i)
            if ORDER[i] >= 4:
                wait_above_zero(pe, pT_act, hd * (T // 2), i // 2)
            for j in range(ORDER[i] + 1):
                ins = pe.transpose(banks(4, 2)[:, j * P:(j + 1) * P], probs[:, i % 2, j * P:(j + 1) * P], ident[:, :])
            ins.then_inc(pT_ps, 1)

        def weigh(hd, i):
            pe.wait_ge(pT_dve, hd * T + i + 1)
            if ORDER[i] >= 4:
                pe.wait_ge(pT_act, hd * (T // 2) + i // 2 + 1)
            if not isinstance(hd, int) or hd * T + i >= 2:
                pe.wait_ge(o_done, hd * T + i - 1)
            for j in range(ORDER[i] + 1):
                ins = pe.matmul(ps[:, 6 + i % 2, 0:HD], probsT[:, i % 2, j * P:(j + 1) * P],
                                val[:, j, bass.ds(hd * HD, HD)], start=(j == 0), stop=(j == ORDER[i]))
            ins.then_inc(pv_ps, 1)

        def pair(hd, first, last):
            for j in range(2):
                for i in range(T):
                    if i < T - 1:
                        scores(hd + j, j, (i + 1) % 2, i + 1)
                    elif not (last and j == 1):
                        scores(hd + j + 1, 1 - j, 0, 0)
                    turn(hd + j, i)
                    if i:
                        weigh(hd + j, i - 1)
                    elif not (first and j == 0):
                        weigh(hd + j - 1, T - 1)

        scores(0, 0, 0, 0)
        pair(0, True, False)
        with pe.Fori(1, HEADS // 2 - 1) as p:
            pair(2 * p, False, False)
        pair(HEADS - 2, False, True)
        weigh(HEADS - 1, T - 1)
        meet(pe, "pe")

        def turn_values(t):
            if t >= 2:
                pe.wait_ge(oT_lo_done, t - 1)
            transposes(pe, o_tok[:, t, :], 2 * (t % 2), K).then_inc(oT_ps, 1)

        turn_values(0)
        turn_values(1)
        for c in range(4):
            s, mm = PROJ[12 + c]
            pe.wait_ge(lo_done[s], mm + 1)
            for t in range(T):
                n = T * c + t
                if c == 0:
                    pe.wait_ge(oT_lo_done, t + 1)
                if c == 0 and t + 2 < T:
                    turn_values(t + 2)
                if n >= 2:
                    pe.wait_ge(op_done, n - 1)
                for k in range(K):
                    w = slice(k * 256, (k + 1) * 256)
                    ins = three(pe, ps[:, 4 + n % 2, 0:256], oT_hi[:, k, t * P:(t + 1) * P],
                                oT_lo[:, k, t * P:(t + 1) * P], w_hi[:, s, w], w_lo[:, s, w], k == 0, k == K - 1)
                ins.then_inc(op_ps, 1)
                if c == 3 and t >= 1:
                    router_turn(pe, 1, t - 1)
                if c == 3 and t >= 2:
                    router_logits(pe, 1, t - 2)
            pe.drain().then_inc(used[s], 1)
        router_logits(pe, 1, T - 2)
        router_turn(pe, 1, T - 1)
        router_logits(pe, 1, T - 1)
        pe_moe(pe, 1)

    block.__exit__(None, None, None)


_INS = ['x', 'mix_norm', 'ffn_norm', 'pool_w', 'pool_scale', 'kv_norm', 'w_k', 'w_v', 'w_f', 'b_f', 'w_q', 'w_o',
        'router_g', 'router_g_b', 'router_e', 'router_e_b', 'w_gate', 'w_up', 'w_down', 'final_norm']


def kernel(**inputs):
    import numpy as np
    import concourse.bacc as bacc
    from concourse.bass_utils import run_bass_kernel_spmd

    nc = bacc.Bacc("TRN2", target_bir_lowering=False, num_devices=1)
    arrays, aps = {}, []
    for name in _INS:
        a = np.ascontiguousarray(inputs[name])
        arrays[f"in_{name}"] = a
        aps.append(nc.dram_tensor(f"in_{name}", a.shape, mybir.dt.from_np(a.dtype), kind="ExternalInput").ap())
    aps.append(nc.dram_tensor("out_0", (1, S, D), F32, kind="ExternalOutput").ap())
    trunk(nc, *aps)
    r = run_bass_kernel_spmd(nc, [arrays], core_ids=[0])
    return np.asarray(r.results[0]["out_0"])
```
